# Optimizing a Trainium2 kernel written in Bass

```python
import math
import jax, jax.numpy as jnp
from jax import lax
import numpy as np

D_MODEL = 1024
BATCH = 1
SEQ = 128
DEPTH = 2
DEC_BATCH = 1
DEC_SEQ = 1024
PAST_LEN = 128

GRID_W = 64
N_MIXERS = 2
N_MLA = (DEPTH + 1) // 2
N_SSM = DEPTH // 2
N_MOD = 6
EPS = 1e-6

MLA_HEADS = 8
QK_NOPE = 128
QK_ROPE = 64
V_HEAD = 128
Q_LORA = 384
KV_LORA = 256
ROPE_THETA = 10000.0
ROPE_PAIRS_PER_AXIS = QK_ROPE // 4
Q_BLOCK = 128
ATTN_SCALE = (QK_NOPE + QK_ROPE) ** -0.5

D_INNER = 2 * D_MODEL
SSM_HEAD_DIM = 64
SSM_HEADS = D_INNER // SSM_HEAD_DIM
SSM_GROUPS = 4
D_STATE = 128
D_CONV = 3
CHUNK = 128
CONV_DIM = D_INNER + 2 * SSM_GROUPS * D_STATE
IN_PROJ_DIM = D_INNER + CONV_DIM + 2 * SSM_HEADS

N_EXPERTS = 16
D_FF_EXPERT = 1024
CAPACITY_FACTOR = 2

kernel_name = 'hybrid_mla_ssd_ecmoe_diffusion_step'

def rms_norm(x, g):
    xf = x.astype(jnp.float32)
    y = xf * lax.rsqrt(jnp.mean(xf * xf, axis=-1, keepdims=True) + EPS)
    return (y * g.astype(jnp.float32)).astype(x.dtype)

def modulation(cond, w_mod, b_mod):
    m = jax.nn.silu(cond) @ w_mod + b_mod
    return jnp.split(m, N_MOD, axis=-1)

def axial_rope_tables(grid_rows, dtype):
    row = jnp.repeat(jnp.arange(grid_rows), GRID_W).astype(jnp.float32)
    col = jnp.tile(jnp.arange(GRID_W), grid_rows).astype(jnp.float32)
    inv = ROPE_THETA ** (-jnp.arange(ROPE_PAIRS_PER_AXIS, dtype=jnp.float32) / ROPE_PAIRS_PER_AXIS)
    ang = jnp.concatenate([row[:, None] * inv, col[:, None] * inv], axis=-1)
    return jnp.cos(ang).astype(dtype), jnp.sin(ang).astype(dtype)

def apply_rope(x, cos, sin):
    half = QK_ROPE // 2
    x1, x2 = x[..., :half], x[..., half:]
    return jnp.concatenate([x1 * cos - x2 * sin, x2 * cos + x1 * sin], axis=-1)

def mla_project(h, w_dq, q_norm_g, w_uq, w_dkv, kv_norm_g):
    b, l, _ = h.shape
    q = (rms_norm(h @ w_dq, q_norm_g) @ w_uq).reshape(b, l, MLA_HEADS, QK_NOPE + QK_ROPE)
    kv = h @ w_dkv
    ckv = rms_norm(kv[..., :KV_LORA], kv_norm_g)
    return q[..., :QK_NOPE], q[..., QK_NOPE:], ckv, kv[..., KV_LORA:]

def mla_expand(ckv, w_ukv):
    b, s, _ = ckv.shape
    kv = (ckv @ w_ukv).reshape(b, s, MLA_HEADS, QK_NOPE + V_HEAD)
    return kv[..., :QK_NOPE], kv[..., QK_NOPE:]

def mla_attention(q_nope, q_rope, k_nope, k_rope, v):
    b, l, h, _ = q_nope.shape
    nb = l // Q_BLOCK
    qn = jnp.moveaxis(q_nope.reshape(b, nb, Q_BLOCK, h, QK_NOPE), 1, 0)
    qr = jnp.moveaxis(q_rope.reshape(b, nb, Q_BLOCK, h, QK_ROPE), 1, 0)

    def block(args):
        qn_b, qr_b = args
        s = (jnp.einsum('bqhd,bkhd->bhqk', qn_b, k_nope).astype(jnp.float32)
             + jnp.einsum('bqhd,bkd->bhqk', qr_b, k_rope).astype(jnp.float32)) * ATTN_SCALE
        p = jax.nn.softmax(s, axis=-1).astype(v.dtype)
        return jnp.einsum('bhqk,bkhd->bqhd', p, v)

    o = lax.map(block, (qn, qr))
    return jnp.moveaxis(o, 0, 1).reshape(b, l, h * V_HEAD)

def mla_context(h, w_dq, q_norm_g, w_uq, w_dkv, kv_norm_g, w_ukv, w_o):
    q_nope, q_rope, ckv, k_rope = mla_project(h, w_dq, q_norm_g, w_uq, w_dkv, kv_norm_g)
    k_nope, v = mla_expand(ckv, w_ukv)
    o = mla_attention(q_nope, q_rope, k_nope, k_rope, v)
    return o @ w_o, ckv, k_rope

def mla_latent(h, ckv_ctx, krope_ctx, cos, sin, w_dq, q_norm_g, w_uq, w_dkv, kv_norm_g, w_ukv, w_o):
    q_nope, q_rope, ckv, k_rope = mla_project(h, w_dq, q_norm_g, w_uq, w_dkv, kv_norm_g)
    q_rope = apply_rope(q_rope, cos[:, None, :], sin[:, None, :])
    k_rope = apply_rope(k_rope, cos, sin)
    ckv_all = jnp.concatenate([ckv_ctx.astype(ckv.dtype), ckv], axis=1)
    krope_all = jnp.concatenate([krope_ctx.astype(k_rope.dtype), k_rope], axis=1)
    k_nope, v = mla_expand(ckv_all, w_ukv)
    o = mla_attention(q_nope, q_rope, k_nope, krope_all, v)
    return o @ w_o

def centred_depthwise_conv(x, conv_w, conv_b):
    pad = D_CONV // 2
    w = conv_w.T[:, None, :].astype(x.dtype)
    y = lax.conv_general_dilated(x, w, window_strides=(1,), padding=[(pad, pad)],
                                 dimension_numbers=('NWC', 'WIO', 'NWC'),
                                 feature_group_count=x.shape[-1])
    return y + conv_b.astype(x.dtype)

def ssd_chunked_scan(x, dt, a, b_in, c_in, h0):
    bsz, l, h, p = x.shape
    g, n = SSM_GROUPS, D_STATE
    r = h // g
    nc = l // CHUNK
    f32 = jnp.float32
    xc = x.astype(f32).reshape(bsz, nc, CHUNK, g, r, p)
    dtc = dt.astype(f32).reshape(bsz, nc, CHUNK, g, r)
    bc = b_in.astype(f32).reshape(bsz, nc, CHUNK, g, n)
    cc = c_in.astype(f32).reshape(bsz, nc, CHUNK, g, n)
    a_cs = jnp.cumsum(dtc * a.reshape(g, r), axis=2)
    lower = jnp.tril(jnp.ones((CHUNK, CHUNK), dtype=bool))
    seg = a_cs[:, :, :, None] - a_cs[:, :, None, :]
    decay = jnp.exp(jnp.where(lower[:, :, None, None], seg, -jnp.inf))
    cb = jnp.einsum('bcign,bcjgn->bcijg', cc, bc)
    w = cb[..., None] * decay * dtc[:, :, None]
    y_diag = jnp.einsum('bcijgr,bcjgrp->bcigrp', w, xc)
    to_end = jnp.exp(a_cs[:, :, -1:] - a_cs) * dtc
    states = jnp.einsum('bcqgn,bcqgr,bcqgrp->bcgrpn', bc, to_end, xc)
    chunk_decay = jnp.exp(a_cs[:, :, -1])

    def step(state, inp):
        dec, st = inp
        return dec[..., None, None] * state + st, state

    h_last, h_in = lax.scan(step, h0.astype(f32).reshape(bsz, g, r, p, n),
                            (jnp.moveaxis(chunk_decay, 1, 0), jnp.moveaxis(states, 1, 0)))
    h_in = jnp.moveaxis(h_in, 0, 1)
    y_off = jnp.einsum('bcqgn,bcgrpn->bcqgrp', cc, h_in) * jnp.exp(a_cs)[..., None]
    y = (y_diag + y_off).reshape(bsz, l, h, p)
    return y, h_last.reshape(bsz, h, p, n)

def bidir_mamba2(h, h0_fwd, h0_bwd, w_in, conv_w, conv_b, dt_bias, a_log, d_skip, norm_g, w_out):
    bsz, l, _ = h.shape
    gn = SSM_GROUPS * D_STATE
    zxbcdt = h @ w_in
    z = zxbcdt[..., :D_INNER]
    xbc = jax.nn.silu(centred_depthwise_conv(zxbcdt[..., D_INNER:D_INNER + CONV_DIM], conv_w, conv_b))
    dt_raw = zxbcdt[..., D_INNER + CONV_DIM:]
    x = xbc[..., :D_INNER].reshape(bsz, l, SSM_HEADS, SSM_HEAD_DIM)
    b_in = xbc[..., D_INNER:D_INNER + gn].reshape(bsz, l, SSM_GROUPS, D_STATE)
    c_in = xbc[..., D_INNER + gn:].reshape(bsz, l, SSM_GROUPS, D_STATE)
    dt = jax.nn.softplus(dt_raw.astype(jnp.float32) + dt_bias.reshape(-1).astype(jnp.float32))
    dt = dt.reshape(bsz, l, 2, SSM_HEADS)
    a = -jnp.exp(a_log.astype(jnp.float32))
    flip = lambda t: jnp.flip(t, axis=1)
    y_f, h_f = ssd_chunked_scan(x, dt[:, :, 0], a[0], b_in, c_in, h0_fwd)
    y_b, h_b = ssd_chunked_scan(flip(x), flip(dt[:, :, 1]), a[1], flip(b_in), flip(c_in), h0_bwd)
    y = y_f + flip(y_b) + d_skip.astype(jnp.float32)[:, None] * x.astype(jnp.float32)
    y = y.reshape(bsz, l, D_INNER) * jax.nn.silu(z.astype(jnp.float32))
    y = rms_norm(y, norm_g).astype(h.dtype)
    return y @ w_out, h_f, h_b

def expert_choice_moe(h, w_router, w_gate, w_up, w_down):
    bsz, l, d = h.shape
    t = h.reshape(bsz * l, d)
    cap = CAPACITY_FACTOR * (bsz * l) // N_EXPERTS
    aff = jax.nn.softmax((t @ w_router).astype(jnp.float32), axis=-1)
    gates, idx = lax.top_k(aff.T, cap)
    xe = t[idx]
    hid = jax.nn.silu(jnp.einsum('ecd,edf->ecf', xe, w_gate)) * jnp.einsum('ecd,edf->ecf', xe, w_up)
    ye = jnp.einsum('ecf,efd->ecd', hid, w_down) * gates[..., None].astype(h.dtype)
    out = jnp.zeros_like(t).at[idx.reshape(-1)].add(ye.reshape(-1, d))
    return out.reshape(bsz, l, d)

def setup_inputs(seed: int = 0) -> dict:
    key = jax.random.key(seed)
    keys = iter(jax.random.split(key, 40))
    f32 = jnp.float32

    def nrm(shape, scale=1.0):
        return jax.random.normal(next(keys), shape, f32) * scale

    def gain(shape):
        return 1.0 + nrm(shape, 0.02)

    D = D_MODEL
    H = SSM_HEADS
    dt0 = jnp.exp(jax.random.uniform(next(keys), (N_SSM, 2, H), f32, math.log(1e-3), math.log(1e-1)))
    dt_bias = dt0 + jnp.log(-jnp.expm1(-dt0))
    a_log = jnp.log(jax.random.uniform(next(keys), (N_SSM, 2, H), f32, 1.0, 16.0))
    return {
        'x_prompt': nrm((BATCH, SEQ, D)),
        'x_sample': nrm((DEC_BATCH, DEC_SEQ, D)),
        'cache_ckv': nrm((DEC_BATCH, N_MLA, PAST_LEN, KV_LORA)),
        'cache_krope': nrm((DEC_BATCH, N_MLA, PAST_LEN, QK_ROPE)),
        'state_ssm': nrm((DEC_BATCH, N_SSM, 2, H, SSM_HEAD_DIM, D_STATE), 0.5),
        'c': nrm((DEC_BATCH, D)),
        'c_ctx': nrm((D,)),
        'w_mod': nrm((DEPTH, D, N_MOD * D), D ** -0.5),
        'b_mod': nrm((DEPTH, N_MOD * D), 0.01),
        'norm1_g': gain((DEPTH, D)),
        'norm2_g': gain((DEPTH, D)),
        'final_norm_g': gain((D,)),
        'mla_w_dq': nrm((N_MLA, D, Q_LORA), D ** -0.5),
        'mla_q_norm_g': gain((N_MLA, Q_LORA)),
        'mla_w_uq': nrm((N_MLA, Q_LORA, MLA_HEADS * (QK_NOPE + QK_ROPE)), Q_LORA ** -0.5),
        'mla_w_dkv': nrm((N_MLA, D, KV_LORA + QK_ROPE), D ** -0.5),
        'mla_kv_norm_g': gain((N_MLA, KV_LORA)),
        'mla_w_ukv': nrm((N_MLA, KV_LORA, MLA_HEADS * (QK_NOPE + V_HEAD)), KV_LORA ** -0.5),
        'mla_w_o': nrm((N_MLA, MLA_HEADS * V_HEAD, D), (MLA_HEADS * V_HEAD) ** -0.5),
        'ssm_w_in': nrm((N_SSM, D, IN_PROJ_DIM), D ** -0.5),
        'ssm_conv_w': nrm((N_SSM, CONV_DIM, D_CONV), D_CONV ** -0.5),
        'ssm_conv_b': nrm((N_SSM, CONV_DIM), 0.01),
        'ssm_dt_bias': dt_bias,
        'ssm_a_log': a_log,
        'ssm_d_skip': 1.0 + nrm((N_SSM, H), 0.1),
        'ssm_norm_g': gain((N_SSM, D_INNER)),
        'ssm_w_out': nrm((N_SSM, D_INNER, D), D_INNER ** -0.5),
        'moe_w_router': nrm((DEPTH, D, N_EXPERTS), D ** -0.5),
        'moe_w_gate': nrm((DEPTH, N_EXPERTS, D, D_FF_EXPERT), D ** -0.5),
        'moe_w_up': nrm((DEPTH, N_EXPERTS, D, D_FF_EXPERT), D ** -0.5),
        'moe_w_down': nrm((DEPTH, N_EXPERTS, D_FF_EXPERT, D), D_FF_EXPERT ** -0.5),
    }

def reference(x_prompt, x_sample, cache_ckv, cache_krope, state_ssm, c, c_ctx,
              w_mod, b_mod, norm1_g, norm2_g, final_norm_g,
              mla_w_dq, mla_q_norm_g, mla_w_uq, mla_w_dkv, mla_kv_norm_g, mla_w_ukv, mla_w_o,
              ssm_w_in, ssm_conv_w, ssm_conv_b, ssm_dt_bias, ssm_a_log, ssm_d_skip, ssm_norm_g, ssm_w_out,
              moe_w_router, moe_w_gate, moe_w_up, moe_w_down):
    grid_rows = x_sample.shape[1] // GRID_W
    cos, sin = axial_rope_tables(grid_rows, x_sample.dtype)
    xp, xs = x_prompt, x_sample
    new_ckv, new_krope, new_ssm = [], [], []
    for l in range(DEPTH):
        sh1p, sc1p, g1p, sh2p, sc2p, g2p = modulation(c_ctx, w_mod[l], b_mod[l])
        sh1s, sc1s, g1s, sh2s, sc2s, g2s = modulation(c[:, None, :], w_mod[l], b_mod[l])
        hp = rms_norm(xp, norm1_g[l]) * (1.0 + sc1p) + sh1p
        hs = rms_norm(xs, norm1_g[l]) * (1.0 + sc1s) + sh1s
        j = l // N_MIXERS
        if l % N_MIXERS == 0:
            mla = (mla_w_dq[j], mla_q_norm_g[j], mla_w_uq[j], mla_w_dkv[j], mla_kv_norm_g[j], mla_w_ukv[j], mla_w_o[j])
            op, ckv, krope = mla_context(hp, *mla)
            os_ = mla_latent(hs, cache_ckv[:, j], cache_krope[:, j], cos, sin, *mla)
            new_ckv.append(ckv)
            new_krope.append(krope)
        else:
            ssm = (ssm_w_in[j], ssm_conv_w[j], ssm_conv_b[j], ssm_dt_bias[j], ssm_a_log[j], ssm_d_skip[j], ssm_norm_g[j], ssm_w_out[j])
            zero = jnp.zeros((xp.shape[0], SSM_HEADS, SSM_HEAD_DIM, D_STATE), jnp.float32)
            op, h_f, h_b = bidir_mamba2(hp, zero, zero, *ssm)
            os_, _, _ = bidir_mamba2(hs, state_ssm[:, j, 0], state_ssm[:, j, 1], *ssm)
            new_ssm.append(jnp.stack([h_f, h_b], axis=1))
        xp = xp + g1p * op
        xs = xs + g1s * os_
        moe = (moe_w_router[l], moe_w_gate[l], moe_w_up[l], moe_w_down[l])
        xp = xp + g2p * expert_choice_moe(rms_norm(xp, norm2_g[l]) * (1.0 + sc2p) + sh2p, *moe)
        xs = xs + g2s * expert_choice_moe(rms_norm(xs, norm2_g[l]) * (1.0 + sc2s) + sh2s, *moe)
    y_prompt = rms_norm(xp, final_norm_g)
    y_sample = rms_norm(xs, final_norm_g)
    new_ckv_arr = jnp.stack(new_ckv, axis=1)
    new_krope_arr = jnp.stack(new_krope, axis=1)
    new_ssm_arr = jnp.stack(new_ssm, axis=1)
    return (y_prompt, y_sample, new_ckv_arr, new_krope_arr, new_ssm_arr)


_drawn_inputs = setup_inputs


def setup_inputs(seed=0):
    import zlib

    import numpy as np

    out = dict(_drawn_inputs(seed))
    spreads = {}
    factors = {'cache_ckv': 2.87,
     'cache_krope': 4.422,
     'final_norm_g': 7.244,
     'mla_q_norm_g': 3.593,
     'mla_kv_norm_g': 2.824,
     'ssm_conv_b': 4.26,
     'ssm_d_skip': 2.802,
     'ssm_norm_g': 15.28,
     'norm2_g': 3.965}
    for name, (base, spread) in spreads.items():
        noise = np.random.default_rng([zlib.crc32(name.encode()), seed]).standard_normal(out[name].shape)
        drawn = base * np.exp(spread * noise) if base else spread * noise
        out[name] = __import__('jax').numpy.asarray(drawn.astype(out[name].dtype))
    for name, factor in factors.items():
        out[name] = (out[name] * factor).astype(out[name].dtype)
    return out
```

```python
from contextlib import ExitStack

import numpy as np

import concourse.bass as bass
from concourse import mybir

F32 = mybir.dt.float32
U32 = mybir.dt.uint32
ACT = mybir.ActivationFunctionType
ALU = mybir.AluOpType
X = mybir.AxisListType.X

P = 128
D = 1024
KD = D // P
SEQ, DEC = 128, 1024
T = SEQ + DEC
NB = T // P
TILE = 384
NT = T // TILE
DEPTH = 2
EPS = 1e-6
HEADS, NOPE, ROPE, VD = 8, 128, 64, 128
QR, KVR = 384, 256
KQ, KKV = QR // P, KVR // P
PAST = 128
KEYS = T + PAST
SAMPLE_KEYS = PAST + DEC
SCALE = (NOPE + ROPE) ** -0.5
GRID_W = 64
THETA = 10000.0
DI = 2048
HD = 64
SH = DI // HD
SG = 4
NS = 128
HPG = SH // SG
GN = SG * NS
CONV = DI + 2 * GN
MC = CONV // P
IN_DIM = DI + CONV + 2 * SH
NE = 16
FF = 1024
CAP_S = 2 * DEC // NE
CAP_P = 2 * SEQ // NE
CAP = CAP_S + CAP_P
V_N1, V_N2, V_CTX, V_C, V_QG, V_KVG, V_SG, V_CB = 0, 16, 32, 40, 48, 51, 53, 69
V_ALL = V_CB + MC


class Steps:

    def __init__(self, eng, sem, turn=0, per_turn=0, before=0):
        self.eng, self.sem, self.base, self.n = eng, sem, turn * per_turn + before, 0

    def did(self, ins):
        ins.then_inc(self.sem, 1)
        self.n += 1

    def settle(self):
        self.eng.wait_ge(self.sem, self.base + self.n)

    def alone(self, ins):
        self.did(ins)
        self.settle()


def wait_alone(eng, sem, value):
    eng.wait_ge(sem, value)
    eng.nop(nofuse=True)


class Stage:

    def __init__(self, nc, name):
        self.nc, self.name = nc, name
        self.ctx = ExitStack()
        self.sems = []

    def __enter__(self):
        return self

    def sb(self, name, shape, dt=F32):
        return self.ctx.enter_context(self.nc.sbuf_tensor(f"{self.name}_{name}", shape, dt))

    def sem(self, name):
        s = self.nc.alloc_semaphore(f"{self.name}_{name}")
        self.sems.append(s)
        return s

    def __exit__(self, *e):
        if e[0] is None:
            self.nc.clear_and_free_semaphores(self.sems)
            self.nc.all_engine_barrier()
        self.ctx.__exit__(*e)


def bcast_rows(ap, n):
    return ap.partition_broadcast(n)


class Modulation:

    CH = 6 * D // 512

    def __init__(self, st, g, io, l):
        self.g, self.io, self.l = g, io, l
        self.w = st.sb("m_w", [P, 4, KD, 512])
        self.row = st.sb("m_row", [2, 4, 512])
        self.rows = st.sb("m_rows", [2, 6 * D])
        self.sel = st.sb("m_sel", [2, 2, P])
        self.w_in = [st.sem(f"m_w_in{i}") for i in range(4)]
        self.row_mm, self.row_ok = st.sem("m_row_mm"), st.sem("m_row_ok")
        self.col_mm, self.col_ok = st.sem("m_col_mm"), st.sem("m_col_ok")
        self.sel_ok, self.gate_mm, self.done = st.sem("m_sel_ok"), st.sem("m_gate_mm"), st.sem("m_done")

    def sync(self, sp):
        def load(u, c0):
            sp.dma_start(self.w[:, u], self.io["w_mod"][self.l].rearrange("(k p) n -> p k n", p=P)[
                :, :, bass.ds(c0 + u * 512, 512)]).then_inc(self.w_in[u], 16)

        for u in range(4):
            load(u, 0)
        with sp.Fori(1, self.CH // 4) as i:
            for u in range(4):
                sp.wait_ge(self.row_mm, 4 * i + u - 3)
                load(u, 2048 * i)

    def tensor(self, pe):
        PS, g = self.g.PS, self.g

        def columns(i, u):
            pe.wait_ge(self.row_ok, 4 * i + u + 1)
            wait_alone(pe, self.col_ok, 4 * i + max(0, u - 1))
            for m in range(4):
                last = pe.transpose(PS[:, 3 + u % 2, 2 * m:2 * m + 2], self.row[:, u, P * m:P * m + P], g.ident[0:2, 0:2])
            last.then_inc(self.col_mm, 1)

        with pe.Fori(0, self.CH // 4) as i:
            for u in range(4):
                pe.wait_ge(self.w_in[u], 16 * i + 16)
                pe.wait_ge(self.row_ok, 4 * i + max(0, u - 1))
                for k in range(KD):
                    last = pe.matmul(PS[0:2, 1 + u % 2, :], g.cond[:, k, :], self.w[:, u, k, :], start=(k == 0), stop=(k == KD - 1))
                last.then_inc(self.row_mm, 1)
                if u:
                    columns(i, u - 1)
            columns(i, 3)
        pe.wait_ge(self.sel_ok, 1)
        pe.wait_ge(self.row_ok, self.CH)
        pe.wait_ge(self.col_ok, self.CH)
        for j in range(2):
            for half in range(2):
                c0 = 2 * D + 512 * half
                pe.matmul(PS[:, 1 + 2 * j + half, :], self.sel[:, j], self.rows[:, c0:c0 + 512], start=True,
                          stop=True).then_inc(self.gate_mm, 1)

    def scalar(self, act):
        PS, g, l = self.g.PS, self.g, self.l

        def rows(i, u):
            act.wait_ge(self.row_mm, 4 * i + u + 1)
            act.wait_ge(self.col_mm, 4 * i)
            act.copy(self.rows[:, bass.ds(2048 * i + 512 * u, 512)], PS[0:2, 1 + u % 2, :])
            act.copy(self.row[:, u], PS[0:2, 1 + u % 2, :]).then_inc(self.row_ok, 1)

        def columns(i, u):
            act.wait_ge(self.col_mm, 4 * i + u + 1)
            for m in range(4):
                n = 16 * i + 4 * u + m
                last = act.activation(g.modc[:, l, bass.ds(n, 1), :].squeeze(1), PS[:, 3 + u % 2, 2 * m:2 * m + 2], ACT.Identity,
                                      bias=g.bcol[:, bass.ds(n + 48 * l, 1)])
            last.then_inc(self.col_ok, 1)

        with act.Fori(0, self.CH // 4) as i:
            for u in range(4):
                rows(i, u)
                if u:
                    columns(i, u - 1)
            columns(i, 3)

    def vector(self, dve):
        PS, g, l = self.g.PS, self.g, self.l
        dve.tensor_copy(self.sel[:], g.ident[0:2, 0:2].unsqueeze(2).to_broadcast([2, 2, P])).then_inc(self.sel_ok, 1)
        dve.wait_ge(self.col_ok, self.CH)
        for w, at in ((0, V_N1), (1, V_N2)):
            for b0, b1, j in ((0, 1, 0), (1, NB, 1)):
                m0, nb = 24 * w, b1 - b0
                dve.scalar_tensor_tensor(
                    out=g.gain[:, l, w, :, b0:b1],
                    in0=g.modc[:, l, m0 + 8:m0 + 16, j:j + 1].to_broadcast([P, KD, nb]), scalar=1.0,
                    in1=g.vcol[:, at + 8 * l:at + 8 * l + 8].unsqueeze(2).to_broadcast([P, KD, nb]),
                    op0=ALU.add, op1=ALU.mult).then_inc(self.done, 1)
                dve.tensor_copy(g.shift[:, l, w, :, b0:b1],
                                g.modc[:, l, m0:m0 + 8, j:j + 1].to_broadcast([P, KD, nb])).then_inc(self.done, 1)
        for n in range(4):
            dve.wait_ge(self.gate_mm, n + 1)
            c0 = 512 * (n % 2)
            dve.tensor_tensor(g.gate_row[:, n // 2, c0:c0 + 512], PS[:, 1 + n, :], g.gate_bias[:, l, c0:c0 + 512],
                              ALU.add).then_inc(self.done, 1)


def start(nc, g, io):
    with Stage(nc, "start") as st:
        rows_a = st.sb("rows_a", [2 * 48, P])
        rows_b = st.sb("rows_b", [V_ALL, P])
        rows_c = st.sb("rows_c", [MC, 3 * P])
        small, copied, made = st.sem("small"), st.sem("copied"), st.sem("made")
        turned, cols, cond_ok = st.sem("turned"), st.sem("cols"), st.sem("cond_ok")
        mod = Modulation(st, g, io, 0)
        PS = g.PS

        with nc.Block(no_gpsimd_drain=True) as block:
            @block.sync
            def _(sp):
                mod.sync(sp)

            @block.scalar
            def _(act):
                act.dma_start(rows_a[:], io["b_mod"].rearrange("l (m p) -> (l m) p", p=P)).then_inc(small, 16)
                for at, name in ((V_N1, "norm1_g"), (V_N2, "norm2_g"), (V_C, "c"), (V_QG, "mla_q_norm_g"),
                                 (V_KVG, "mla_kv_norm_g"), (V_SG, "ssm_norm_g"), (V_CB, "ssm_conv_b")):
                    rows = io[name].rearrange("l (m p) -> (l m) p", p=P)
                    act.dma_start(rows_b[at:at + rows.shape[0], :], rows).then_inc(small, 16)
                act.dma_start(rows_b[V_CTX:V_CTX + KD, :], io["c_ctx"].rearrange("(m p) -> m p", p=P)).then_inc(small, 16)
                act.dma_start(rows_c[:], io["ssm_conv_w"][0].rearrange("(m p) j -> m (p j)", p=P)).then_inc(small, 16)
                for l in range(DEPTH):
                    act.dma_start(g.gate_bias[:, l], io["b_mod"][l, 2 * D:3 * D].partition_broadcast(P)).then_inc(copied, 16)
                act.dma_start(g.res[0:SEQ, :], io["x_prompt"][0]).then_inc(copied, 16)
                act.dma_start(g.res[SEQ:T, :], io["x_sample"][0]).then_inc(copied, 16)
                act.wait_ge(cols, 5)
                act.activation(g.cond[:, :, 0], g.vcol[:, V_CTX:V_CTX + KD], ACT.Silu).then_inc(cond_ok, 1)
                act.activation(g.cond[:, :, 1], g.vcol[:, V_C:V_C + KD], ACT.Silu).then_inc(cond_ok, 1)
                mod.scalar(act)
                act.wait_ge(copied, 64)

            @block.gpsimd
            def _(pool):
                pool.memset(g.ident[:], 0.0).then_inc(made, 1)
                pool.memset(g.ones[:], 1.0).then_inc(made, 1)
                pool.wait_ge(made, 2)
                pool.affine_select(out=g.ident[:], in_=g.ident[:], compare_op=ALU.not_equal, fill=1.0, base=0,
                                   pattern=[[-1, P]], channel_multiplier=1).then_inc(made, 1)
                pool.memset(g.fold[:], 0.0).then_inc(made, 1)
                for n, base in enumerate((0, 64, -64)):
                    pool.wait_ge(made, 4 + n)
                    pool.affine_select(out=g.fold[:], in_=g.fold[:], compare_op=ALU.not_equal, fill=1.0, base=base,
                                       pattern=[[-1, P]], channel_multiplier=1).then_inc(made, 1)
                pool.affine_select(out=g.upper[:], in_=g.ones[:], compare_op=ALU.is_ge, fill=0.0, base=0,
                                   pattern=[[1, P]], channel_multiplier=-1).then_inc(made, 1)
                pool.affine_select(out=g.lower[:], in_=g.ones[:], compare_op=ALU.is_ge, fill=0.0, base=0,
                                   pattern=[[-1, P]], channel_multiplier=1).then_inc(made, 1)

            @block.tensor
            def _(pe):
                pe.wait_ge(small, 16 * 10)
                pe.wait_ge(made, 3)
                pe.transpose(PS[:, 0, 0:96], rows_a[:], g.ident[0:96, 0:96]).then_inc(turned, 1)
                pe.transpose(PS[:, 1, 0:V_ALL], rows_b[:], g.ident[0:V_ALL, 0:V_ALL]).then_inc(turned, 1)
                for j in range(3):
                    pe.transpose(PS[:, 2 + j, 0:MC], rows_c[:, j:3 * P:3], g.ident[0:MC, 0:MC]).then_inc(turned, 1)
                pe.wait_ge(cols, 5)
                pe.wait_ge(cond_ok, 2)
                mod.tensor(pe)

            @block.vector
            def _(dve):
                dve.wait_ge(turned, 5)
                dve.tensor_copy(g.bcol[:], PS[:, 0, 0:96]).then_inc(cols, 1)
                dve.tensor_copy(g.vcol[:], PS[:, 1, 0:V_ALL]).then_inc(cols, 1)
                for j in range(3):
                    dve.tensor_copy(g.convw[:, j, :], PS[:, 2 + j, 0:MC]).then_inc(cols, 1)
                dve.wait_ge(made, 3)
                dve.wait_ge(copied, 64)
                mod.vector(dve)


def norm(nc, g, io, layer, which, hT=None):
    with Stage(nc, f"norm{layer}{which}") as st:
        x = st.sb("x", [P, NB, D])
        junk = st.sb("junk", [P, D])
        ssq = st.sb("ssq", [P, NB])
        root = st.sb("root", [P, NB])
        rstd = st.sb("rstd", [P, NB])
        xn = st.sb("xn", [P, 3, D])
        x_in = st.sem("x_in")
        sq = st.sem("sq")
        ms = st.sem("ms")
        rt = st.sem("rt")
        rs = st.sem("rs")
        xn_ok = st.sem("xn_ok")
        turned = st.sem("turned")
        ev_a = st.sem("ev_a")
        ev_d = st.sem("ev_d")
        PS = g.PS
        router = which == 1
        if router:
            hs = st.sb("hs", [P, 3, KD, P])
            wr = st.sb("wr", [P, KD, NE])
            mx = st.sb("mx", [P, 3])
            ex = st.sb("ex", [P, 3, NE])
            tot = st.sb("tot", [P, 3])
            inv = st.sb("inv", [P, 3])
            pr = st.sb("pr", [P, 3, NE])
            wr_in = st.sem("wr_in")
            saved = [st.sem(f"saved{u}") for u in range(3)]
            lg = st.sem("lg")
            less = st.sb("less", [P, 3, NE])
            less_ok = st.sem("less_ok")
            ex_ok = st.sem("ex_ok")
            chain = st.sem("chain")
            pr_ok = st.sem("pr_ok")
            pt = st.sem("pt")
            af = st.sem("af")

        def h_out(u, i, k0, k1):
            if router:
                return hs[:, u, k0:k1, :]
            return hT[:, k0:k1, bass.ds(i * 3 * P + u * P, P)]

        with nc.Block(no_gpsimd_drain=True) as block:
            @block.sync
            def _(sp):
                sp.dma_start(x[:], g.res.rearrange("(b p) d -> p b d", p=P)).then_inc(x_in, 16)
                if router:
                    sp.dma_start(wr[:], io["moe_w_router"][layer].rearrange("(k p) e -> p k e", p=P)).then_inc(wr_in, 16)
                    with sp.Fori(0, 3) as i:
                        for u in range(3):
                            sp.wait_ge(xn_ok, 3 * i + u + 1)
                            sp.dma_start(g.normed[bass.ds(i * 3 * P + u * P, P), :], xn[:, u]).then_inc(saved[u], 16)
                    for u in range(3):
                        sp.wait_ge(saved[u], 48)

            @block.scalar
            def _(act):
                act.wait_ge(x_in, 16)
                for b in range(NB):
                    if b:
                        act.wait_ge(sq, b)
                    act.activation(junk[:], x[:, b], ACT.Square, accum_out=ssq[:, b:b + 1]).then_inc(sq, 1)
                act.wait_ge(ms, 1)
                act.activation(root[:], ssq[:], ACT.Sqrt).then_inc(rt, 1)
                act.wait_ge(rs, 1)
                with act.Fori(0, 3) as i:
                    for u in range(3):
                        act.wait_ge(turned, 3 * i)
                        if router:
                            act.wait_ge(saved[u], 16 * i)
                        act.activation(xn[:, u], x[:, bass.ds(3 * i + u, 1), :].squeeze(1), ACT.Copy,
                                       scale=rstd[:, bass.ds(3 * i + u, 1)]).then_inc(xn_ok, 1)
                    for u in range(3):
                        act.wait_ge(turned, 3 * i + u + 1)
                        if router:
                            act.wait_ge(lg, i)
                        for k in range(4, KD):
                            act.activation(h_out(u, i, k, k + 1).squeeze(1), PS[:, 2 * u + 1, P * (k - 4):P * (k - 3)],
                                           ACT.Identity,
                                           scale=g.gain[:, layer, which, k, bass.ds(3 * i + u, 1)],
                                           bias=g.shift[:, layer, which, k, bass.ds(3 * i + u, 1)]).then_inc(ev_a, 1)
                    if router:
                        act.wait_ge(less_ok, i + 1)
                        act.activation(ex[:], less[:], ACT.Exp).then_inc(ex_ok, 1)

            @block.vector
            def _(dve):
                dve.wait_ge(sq, NB)
                dve.tensor_scalar(ssq[:], ssq[:], 1.0 / D, EPS, ALU.mult, ALU.add).then_inc(ms, 1)
                dve.wait_ge(rt, 1)
                dve.reciprocal(rstd[:], root[:]).then_inc(rs, 1)
                with dve.Fori(0, 3) as i:
                    for u in range(3):
                        dve.wait_ge(turned, 3 * i + u + 1)
                        if router:
                            dve.wait_ge(lg, i)
                        for k in range(4):
                            dve.tensor_scalar(h_out(u, i, k, k + 1).squeeze(1), PS[:, 2 * u, P * k:P * k + P],
                                              g.gain[:, layer, which, k, bass.ds(3 * i + u, 1)],
                                              g.shift[:, layer, which, k, bass.ds(3 * i + u, 1)],
                                              ALU.mult, ALU.add).then_inc(ev_d, 1)
                    if router:
                        steps = Steps(dve, chain, i, 3)
                        logits = PS[:, 6, 0:3 * NE].rearrange("p (u e) -> p u e", e=NE)
                        dve.wait_ge(lg, i + 1)
                        steps.alone(dve.tensor_reduce(mx[:], logits, X, ALU.max))
                        dve.tensor_tensor(less[:], logits, mx[:].unsqueeze(2).to_broadcast([P, 3, NE]),
                                          ALU.subtract).then_inc(less_ok, 1)
                        dve.wait_ge(ex_ok, i + 1)
                        steps.alone(dve.tensor_reduce(tot[:], ex[:], X, ALU.add))
                        steps.alone(dve.reciprocal(inv[:], tot[:]))
                        dve.tensor_tensor(pr[:], ex[:], inv[:].unsqueeze(2).to_broadcast([P, 3, NE]),
                                          ALU.mult).then_inc(pr_ok, 1)
                        dve.wait_ge(pt, i + 1)
                        dve.tensor_copy(g.aff[:, bass.ds(i * 3 * P, 3 * P)], PS[0:NE, 7, 0:3 * P]).then_inc(af, 1)

            @block.tensor
            def _(pe):
                if router:
                    pe.wait_ge(wr_in, 16)
                with pe.Fori(0, 3) as i:
                    for u in range(3):
                        pe.wait_ge(xn_ok, 3 * i + u + 1)
                        pe.wait_ge(ev_a, 12 * i)
                        pe.wait_ge(ev_d, 12 * i)
                        for k in range(KD):
                            last = pe.transpose(PS[:, 2 * u + k // 4, P * (k % 4):P * (k % 4) + P],
                                                xn[:, u, P * k:P * k + P], g.ident[:])
                        last.then_inc(turned, 1)
                    if router:
                        for u in range(3):
                            pe.wait_ge(ev_a, 12 * i + 4 * u + 4)
                            pe.wait_ge(ev_d, 12 * i + 4 * u + 4)
                            pe.wait_ge(less_ok, i)
                            for k in range(KD):
                                last = pe.matmul(PS[:, 6, NE * u:NE * u + NE], hs[:, u, k], wr[:, k],
                                                 start=(k == 0), stop=(k == KD - 1))
                        last.then_inc(lg, 1)
                        pe.wait_ge(pr_ok, i + 1)
                        pe.wait_ge(af, i)
                        for u in range(3):
                            last = pe.transpose(PS[0:NE, 7, P * u:P * u + P], pr[:, u], g.ident[:])
                        last.then_inc(pt, 1)


def mla_project(nc, g, io, hT, m):
    with Stage(nc, "proj") as st:
        w = st.sb("w", [P, KD, QR + KVR + 2 * ROPE])
        sqr = st.sb("sqr", [P, KQ + KKV, TILE])
        root = st.sb("root", [P, 2, TILE])
        rinv = st.sb("rinv", [P, 2, TILE])
        kc = st.sb("kc", [P, TILE])
        cc = st.sb("cc", [P, KVR])
        ckr = st.sb("ckr", [P, 2 * ROPE])
        outs = st.sb("outs", [P, KVR + ROPE])
        epsc = st.sb("epsc", [P, 1])
        w_in, cache_in, eps_ok = st.sem("w_in"), st.sem("cache_in"), st.sem("eps_ok")
        prod, sq, sums, rt, rc = st.sem("prod"), st.sem("sq"), st.sem("sums"), st.sem("rt"), st.sem("rc")
        kc_ok, fold, k2_ok, lat_ok = st.sem("kc_ok"), st.sem("fold"), st.sem("k2_ok"), st.sem("lat_ok")
        tp, cache_ok, out_ok, stored = st.sem("tp"), st.sem("cache_ok"), st.sem("out_ok"), st.sem("stored")
        PS = g.PS
        NM = KQ + KKV

        def cols(i):
            return bass.ds(i * TILE, TILE)

        with nc.Block(no_gpsimd_drain=True) as block:
            @block.sync
            def _(sp):
                dkv = io["mla_w_dkv"][0].rearrange("(k p) n -> p k n", p=P)
                sp.dma_start(w[:, :, 0:QR], io["mla_w_dq"][0].rearrange("(k p) n -> p k n", p=P)).then_inc(w_in, 16)
                sp.dma_start(w[:, :, QR:QR + KVR + ROPE], dkv).then_inc(w_in, 16)
                at, h = QR + KVR + ROPE, ROPE // 2
                sp.dma_start(w[:, :, at:at + h], dkv[:, :, KVR + h:KVR + ROPE]).then_inc(w_in, 16)
                sp.dma_start(w[:, :, at + h:at + ROPE], dkv[:, :, KVR:KVR + h]).then_inc(w_in, 16)
                sp.dma_start(m.rope[:], io["rope"]).then_inc(w_in, 16)
                sp.dma_start(cc[:], io["cache_ckv"][0, 0]).then_inc(cache_in, 16)
                sp.dma_start(ckr[:, 0:ROPE], io["cache_krope"][0, 0]).then_inc(cache_in, 16)
                sp.dma_start(ckr[:, ROPE:2 * ROPE], io["cache_krope"][0, 0]).then_inc(cache_in, 16)
                sp.wait_ge(out_ok, 1)
                sp.dma_start(io["new_ckv"][0, 0], outs[:, 0:KVR]).then_inc(stored, 16)
                sp.dma_start(io["new_krope"][0, 0], outs[:, KVR:KVR + ROPE]).then_inc(stored, 16)
                sp.wait_ge(stored, 32)

            @block.tensor
            def _(pe):
                pe.wait_ge(cache_in, 48)
                for r in range(KKV):
                    pe.transpose(PS[:, 0, P * r:P * r + P], cc[:, P * r:P * r + P], g.ident[:])
                pe.transpose(PS[:, 0, P * KKV:P * KKV + P], ckr[:], g.ident[:]).then_inc(tp, 1)
                pe.wait_ge(w_in, 80)
                pe.wait_ge(cache_ok, 2)
                with pe.Fori(0, NT) as i:
                    pe.wait_ge(lat_ok, NM * i)
                    pe.wait_ge(k2_ok, i)
                    for n in range(NM + 1):
                        for k in range(KD):
                            last = pe.matmul(PS[:, n, 0:TILE], w[:, k, P * n:P * n + P], hT[:, k, cols(i)],
                                             start=(k == 0), stop=(k == KD - 1))
                        last.then_inc(prod, 1)
                    pe.wait_ge(sq, NM * i + NM)
                    for n in range(NM):
                        last = pe.matmul(PS[:, 6 + (n >= KQ), 0:TILE], g.ones[:], sqr[:, n, :],
                                         start=n in (0, KQ), stop=n in (KQ - 1, NM - 1))
                    last.then_inc(sums, 1)
                    pe.wait_ge(kc_ok, i + 1)
                    pe.matmul(PS[:, NM, 0:TILE], g.fold[:], kc[:], start=True, stop=True).then_inc(fold, 1)
                pe.wait_ge(lat_ok, NM * NT)
                pe.wait_ge(k2_ok, NT)
                for r in range(KKV):
                    pe.transpose(PS[:, 0, P * r:P * r + P], m.ckv[:, r, 0:P], g.ident[:])
                pe.transpose(PS[:, 0, P * KKV:P * KKV + ROPE], m.k2[0:ROPE, 0:P], g.ident[0:ROPE, 0:ROPE]).then_inc(tp, 1)

            @block.scalar
            def _(act):
                act.wait_ge(eps_ok, 1)
                with act.Fori(0, NT) as i:
                    act.wait_ge(sums, i)
                    for n in range(NM):
                        act.wait_ge(prod, (NM + 1) * i + n + 1)
                        act.activation(sqr[:, n, :], PS[:, n, 0:TILE], ACT.Square).then_inc(sq, 1)
                    act.wait_ge(sums, i + 1)
                    for j, width in ((0, QR), (1, KVR)):
                        act.activation(root[:, j, :], PS[:, 6 + j, 0:TILE], ACT.Sqrt, scale=1.0 / width,
                                       bias=epsc[:]).then_inc(rt, 1)

            @block.vector
            def _(dve):
                dve.memset(epsc[:], EPS).then_inc(eps_ok, 1)
                dve.wait_ge(tp, 1)
                dve.tensor_copy(m.ckv[:, :, T:KEYS], PS[:, 0, 0:KVR].rearrange("p (r t) -> p r t", r=KKV)).then_inc(cache_ok, 1)
                dve.tensor_copy(m.k2[:, T:KEYS], PS[:, 0, KVR:KVR + P]).then_inc(cache_ok, 1)
                with dve.Fori(0, NT) as i:
                    dve.wait_ge(prod, (NM + 1) * (i + 1))
                    dve.wait_ge(fold, i)
                    dve.tensor_tensor(kc[:], PS[:, NM, 0:TILE], m.rope[:, cols(i)], ALU.mult).then_inc(kc_ok, 1)
                    dve.wait_ge(fold, i + 1)
                    dve.tensor_copy(m.k2[:, cols(i)], PS[:, NM, 0:TILE]).then_inc(k2_ok, 1)
                    for j in range(2):
                        dve.wait_ge(rt, 2 * i + j + 1)
                        dve.reciprocal(rinv[:, j, :], root[:, j, :]).then_inc(rc, 1)
                        dve.wait_ge(rc, 2 * i + j + 1)
                        for n in (range(KQ) if j == 0 else range(KQ, NM)):
                            to = m.qlat[:, n, cols(i)] if j == 0 else m.ckv[:, n - KQ, cols(i)]
                            dve.scalar_tensor_tensor(out=to, in0=PS[:, n, 0:TILE], scalar=g.vcol[:, V_QG + n:V_QG + n + 1],
                                                     in1=rinv[:, j, :], op0=ALU.mult, op1=ALU.mult).then_inc(lat_ok, 1)
                dve.wait_ge(tp, 2)
                dve.tensor_copy(outs[:], PS[:, 0, 0:KVR + ROPE]).then_inc(out_ok, 1)


def mla_heads(nc, g, io, m):
    with Stage(nc, "attn") as st:
        wq = st.sb("wq", [P, KQ, 2 * P])
        wkv = st.sb("wkv", [P, KKV, 2 * P])
        qT = st.sb("qT", [P, T])
        q2 = st.sb("q2", [P, T])
        kT = st.sb("kT", [P, KEYS])
        v = st.sb("v", [P, KEYS // P, P])
        mx = st.sb("mx", [P, NB])
        nm = st.sb("nm", [P, NB])
        rsum = st.sb("rsum", [P, NB])
        rin = st.sb("rin", [P, NB])
        prob = st.sb("prob", [P, 2, SAMPLE_KEYS])
        pT = st.sb("pT", [P, NB, P])
        on = st.sb("on", [P, 2, P])
        w_in, w_used = st.sem("w_in"), st.sem("w_used")
        q_mm, q2_mm, k_mm, v_mm = st.sem("q_mm"), st.sem("q2_mm"), st.sem("k_mm"), st.sem("v_mm")
        q_ok, q2_ok, k_ok, v_ok = st.sem("q_ok"), st.sem("q2_ok"), st.sem("k_ok"), st.sem("v_ok")
        s_mm, mx_ok, nm_ok, p_ok = st.sem("s_mm"), st.sem("mx_ok"), st.sem("nm_ok"), st.sem("p_ok")
        t_mm, pt_a, pt_d = st.sem("t_mm"), st.sem("pt_a"), st.sem("pt_d")
        pv_mm, rin_ok, on_ok, ot_mm, ot_ok = st.sem("pv_mm"), st.sem("rin_ok"), st.sem("on_ok"), st.sem("ot_mm"), st.sem("ot_ok")
        PS = g.PS
        VB = KEYS // P
        blocks = list(range(1, NB)) + [0]

        def key_blocks(j):
            return list(range(1, VB)) if blocks[j] else [0]

        def groups(j):
            kb = key_blocks(j)
            return [(6 + n % 2, kb[3 * n:3 * n + 3]) for n in range((len(kb) + 2) // 3)]

        NG = [len(groups(j)) for j in range(NB)]
        GA = [(n + 1) // 2 for n in NG]
        GD = [n // 2 for n in NG]

        with nc.Block(no_gpsimd_drain=True) as block:
            @block.sync
            def _(sp):
                wuq = io["mla_w_uq"][0].rearrange("(k p) n -> p k n", p=P)
                wukv = io["mla_w_ukv"][0].rearrange("(k p) n -> p k n", p=P)
                hw = NOPE + ROPE
                with sp.Fori(0, HEADS) as h:
                    sp.wait_ge(w_used, h)
                    sp.dma_start(wq[:, :, 0:hw], wuq[:, :, bass.ds(h * hw, hw)]).then_inc(w_in, 16)
                    sp.dma_start(wq[:, :, hw:hw + 32], wuq[:, :, bass.ds(h * hw + NOPE + 32, 32)]).then_inc(w_in, 16)
                    sp.dma_start(wq[:, :, hw + 32:hw + 64], wuq[:, :, bass.ds(h * hw + NOPE, 32)]).then_inc(w_in, 16)
                    sp.dma_start(wkv[:], wukv[:, :, bass.ds(h * 2 * P, 2 * P)]).then_inc(w_in, 16)

            @block.tensor
            def _(pe):
                def scores(h, j, qb):
                    if j == 0:
                        pe.wait_ge(k_ok, h + 1)
                        pe.wait_ge(q2_ok, h + 1)
                    elif j == 1:
                        pe.wait_ge(v_ok, h + 1)
                    else:
                        pe.wait_ge(p_ok, NB * h + j - 1)
                    kb = key_blocks(j)
                    width = min(TILE, P * len(kb))
                    for t in range(P * len(kb) // width):
                        out = PS[:, 3 * (j % 2) + t, 0:width]
                        c0 = P * kb[0] + t * width
                        pe.matmul(out, qT[:, P * qb:P * qb + P], kT[:, c0:c0 + width], start=True, stop=False)
                        last = pe.matmul(out, q2[:, P * qb:P * qb + P], m.k2[:, c0:c0 + width], start=False, stop=True)
                    last.then_inc(s_mm, 1)

                def turn_out(h, j):
                    pe.wait_ge(on_ok, NB * h + j + 1)
                    pe.transpose(PS[:, 6, TILE:TILE + P], on[:, j % 2], g.ident[:]).then_inc(ot_mm, 1)

                def transposes(h, j, n):
                    bank, kbs = groups(j)[n]
                    for a in range(len(kbs)):
                        c0 = P * (3 * n + a)
                        last = pe.transpose(PS[:, bank, P * a:P * a + P], prob[:, j % 2, c0:c0 + P], g.ident[:])
                    last.then_inc(t_mm, 1)

                def first_transposes(h, j):
                    na = sum(GA[:j])
                    pe.wait_ge(p_ok, NB * h + j + 1)
                    pe.wait_ge(pt_a, sum(GA) * h + na)
                    pe.wait_ge(on_ok, NB * h + j)
                    if j:
                        turn_out(h, j - 1)
                    else:
                        pe.wait_ge(ot_ok, NB * h)
                    for n in range(min(2, NG[j])):
                        transposes(h, j, n)

                def values(h, j):
                    na, nd = sum(GA[:j]), sum(GD[:j])
                    if NG[j] == 3:
                        pe.wait_ge(pt_a, sum(GA) * h + na + 1)
                        pe.wait_ge(ot_ok, NB * h + j)
                        transposes(h, j, 2)
                        pe.wait_ge(pt_d, sum(GD) * h + nd + 1)
                    else:
                        pe.wait_ge(pt_a, sum(GA) * h + na + GA[j])
                    kbs = key_blocks(j)
                    for a, kb in enumerate(kbs):
                        if a == 6:
                            pe.wait_ge(pt_a, sum(GA) * h + na + GA[j])
                        last = pe.matmul(PS[:, 7, TILE:TILE + P], pT[:, a], v[:, kb], start=(a == 0),
                                         stop=(a == len(kbs) - 1))
                    last.then_inc(pv_mm, 1)

                with pe.Fori(0, HEADS) as h:
                    pe.wait_ge(w_in, 64 * h + 64)
                    pe.wait_ge(p_ok, NB * h)
                    for t in range(NT):
                        for k in range(KQ):
                            last = pe.matmul(PS[:, t, 0:TILE], wq[:, k, 0:P], m.qlat[:, k, TILE * t:TILE * t + TILE],
                                             start=(k == 0), stop=(k == KQ - 1))
                    last.then_inc(q_mm, 1)
                    for t in range(NT):
                        for k in range(KQ):
                            last = pe.matmul(PS[:, 3 + t, 0:TILE], wq[:, k, P:2 * P],
                                             m.qlat[:, k, TILE * t:TILE * t + TILE], start=(k == 0), stop=(k == KQ - 1))
                    last.then_inc(q2_mm, 1)
                    pe.wait_ge(q_ok, h + 1)
                    for t in range(3):
                        c0, c1 = TILE * t, (TILE * t + TILE if t < 2 else KEYS)
                        for r in range(KKV):
                            last = pe.matmul(PS[:, t, 0:c1 - c0], wkv[:, r, 0:P], m.ckv[:, r, c0:c1],
                                             start=(r == 0), stop=(r == KKV - 1))
                    last.then_inc(k_mm, 1)
                    pe.wait_ge(q2_ok, h + 1)
                    for kb in range(VB):
                        for r in range(KKV):
                            last = pe.matmul(PS[:, 3 + kb // 4, P * (kb % 4):P * (kb % 4) + P],
                                             m.ckv[:, r, P * kb:P * kb + P], wkv[:, r, P:2 * P],
                                             start=(r == 0), stop=(r == KKV - 1))
                    last.then_inc(v_mm, 1)
                    scores(h, 0, blocks[0])
                    scores(h, 1, blocks[1])
                    for j in range(NB):
                        first_transposes(h, j)
                        if j + 2 < NB:
                            scores(h, j + 2, blocks[j + 2])
                        values(h, j)
                    pe.wait_ge(pt_a, sum(GA) * h + sum(GA))
                    turn_out(h, NB - 1)

            @block.scalar
            def _(act):
                def exps(h, j):
                    pe_done = sum(NG[:j - 1]) if j > 1 else 0
                    act.wait_ge(t_mm, sum(NG) * h + pe_done)
                    act.wait_ge(nm_ok, NB * h + j + 1)
                    kb = key_blocks(j)
                    nt, width = max(1, len(kb) // 3), min(TILE, P * len(kb))
                    act.activation(prob[:, j % 2, 0:nt * width].rearrange("p (t k) -> p t k", t=nt),
                                   PS[:, 3 * (j % 2):3 * (j % 2) + nt, 0:width], ACT.Exp, bias=nm[:, j:j + 1],
                                   scale=SCALE, accum_out=rsum[:, j:j + 1]).then_inc(p_ok, 1)

                def out_cols(h, j):
                    act.wait_ge(ot_mm, NB * h + j + 1)
                    act.copy(m.oT[:, bass.ds(h, 1), P * blocks[j]:P * blocks[j] + P].squeeze(1),
                             PS[:, 6, TILE:TILE + P]).then_inc(ot_ok, 1)

                def evacuate(h, j, n):
                    bank, kbs = groups(j)[n]
                    act.wait_ge(t_mm, sum(NG) * h + sum(NG[:j]) + n + 1)
                    if n == 0 and j:
                        out_cols(h, j - 1)
                    act.copy(pT[:, 3 * n:3 * n + len(kbs)], PS[:, bank, 0:P * len(kbs)].rearrange(
                        "p (a k) -> p a k", k=P)).then_inc(pt_a, 1)

                with act.Fori(0, HEADS) as h:
                    act.wait_ge(q_mm, h + 1)
                    act.copy(qT[:].rearrange("p (t n) -> p t n", t=NT), PS[:, 0:NT, 0:TILE]).then_inc(q_ok, 1)
                    act.wait_ge(k_mm, h + 1)
                    act.copy(kT[:, 0:2 * TILE].rearrange("p (t n) -> p t n", t=2), PS[:, 0:2, 0:TILE])
                    act.copy(kT[:, 2 * TILE:KEYS], PS[:, 2, 0:KEYS - 2 * TILE]).then_inc(k_ok, 1)
                    exps(h, 0)
                    exps(h, 1)
                    for j in range(NB):
                        evacuate(h, j, 0)
                        if NG[j] == 3:
                            evacuate(h, j, 2)
                        if j + 2 < NB:
                            exps(h, j + 2)
                    out_cols(h, NB - 1)

            @block.vector
            def _(dve):
                def maxima(h, j):
                    dve.wait_ge(s_mm, NB * h + j + 1)
                    kb = key_blocks(j)
                    nt, width = max(1, len(kb) // 3), min(TILE, P * len(kb))
                    src = PS[:, 3 * (j % 2):3 * (j % 2) + nt, 0:width]
                    dve.tensor_reduce(mx[:, j:j + 1], src, mybir.AxisListType.XY, ALU.max).then_inc(mx_ok, 1)
                    dve.wait_ge(mx_ok, NB * h + j + 1)
                    dve.tensor_scalar(nm[:, j:j + 1], mx[:, j:j + 1], -SCALE, None, ALU.mult).then_inc(nm_ok, 1)

                def copy_group(h, j):
                    for n, (bank, kbs) in enumerate(groups(j)):
                        if n % 2:
                            dve.wait_ge(t_mm, sum(NG) * h + sum(NG[:j]) + n + 1)
                            dve.tensor_copy(pT[:, 3 * n:3 * n + len(kbs)], PS[:, bank, 0:P * len(kbs)].rearrange(
                                "p (a k) -> p a k", k=P)).then_inc(pt_d, 1)

                def finish(h, j):
                    dve.wait_ge(p_ok, NB * h + j + 1)
                    dve.reciprocal(rin[:, j:j + 1], rsum[:, j:j + 1]).then_inc(rin_ok, 1)
                    dve.wait_ge(pv_mm, NB * h + j + 1)
                    dve.wait_ge(rin_ok, NB * h + j + 1)
                    dve.tensor_scalar(on[:, j % 2], PS[:, 7, TILE:TILE + P], rin[:, j:j + 1], None,
                                      ALU.mult).then_inc(on_ok, 1)

                with dve.Fori(0, HEADS) as h:
                    dve.wait_ge(q2_mm, h + 1)
                    dve.tensor_tensor(q2[:].rearrange("p (t n) -> p t n", t=NT), PS[:, 3:6, 0:TILE],
                                      m.rope[:].rearrange("p (t n) -> p t n", t=NT), ALU.mult).then_inc(q2_ok, 1)
                    dve.wait_ge(v_mm, h + 1)
                    vf = v[:].rearrange("p a b -> p (a b)")
                    dve.tensor_copy(vf[:, 0:1024].rearrange("p (t n) -> p t n", t=2), PS[:, 3:5, :])
                    dve.tensor_copy(vf[:, 1024:1280], PS[:, 5, 0:256]).then_inc(v_ok, 1)
                    maxima(h, 0)
                    maxima(h, 1)
                    for j in range(NB):
                        copy_group(h, j)
                        if j + 2 < NB:
                            maxima(h, j + 2)
                        finish(h, j)

            @block.gpsimd
            def _(pool):
                with pool.Fori(0, HEADS) as h:
                    pool.wait_ge(v_mm, h + 1)
                    pool.sem_inc(w_used, 1)


def block_loop(eng, body):
    with eng.Fori(0, DEC // P // 2) as i:
        for u in range(2):
            body(2 * i + u, u, 2 * i + u + 1, 1)
    body(DEC // P, 0, 0, 0)


def project_out(nc, g, name, layer, kd, w_dram, take):
    with Stage(nc, name) as st:
        w = st.sb("w", [P, kd, D])
        x = st.sb("x", [P, 2, D])
        t = st.sb("t", [P, 2, D])
        w_in = st.sem("w_in")
        x_in = [st.sem("x_in0"), st.sem("x_in1")]
        saved = [st.sem("saved0"), st.sem("saved1")]
        mm, gated, added = st.sem("mm"), st.sem("gated"), st.sem("added")
        src, src_ok, engines = take(st, mm)
        PS = g.PS

        with nc.Block(no_gpsimd_drain=True) as block:
            @block.sync
            def _(sp):
                sp.dma_start(w[:], w_dram.rearrange("(k p) n -> p k n", p=P)).then_inc(w_in, 16)

                def body(n, u, b, grp):
                    if u == 0:
                        sp.wait_ge(saved[0], 8 * n)
                    else:
                        sp.wait_ge(saved[1], 8 * n - 8)
                    rows = bass.ds(b * P, P) if grp else slice(0, P)
                    sp.dma_start(x[:, u], g.res[rows, :]).then_inc(x_in[u], 16)
                    if engines.get("sync"):
                        engines["sync"](sp, n, u, b, grp)
                block_loop(sp, body)
                sp.wait_ge(saved[0], 16 * (DEC // P // 2 + 1))
                sp.wait_ge(saved[1], 16 * (DEC // P // 2))

            @block.tensor
            def _(pe):
                pe.wait_ge(w_in, 16)

                def body(n, u, b, grp):
                    if engines.get("tensor"):
                        engines["tensor"](pe, n, u, b, grp)
                    pe.wait_ge(src_ok, n + 1)
                    if u == 0:
                        pe.wait_ge(gated, n)
                    else:
                        pe.wait_ge(gated, n - 1)
                    for half in range(2):
                        for k in range(kd):
                            last = pe.matmul(PS[:, 2 * u + half, :], src[:, u, k, :], w[:, k, 512 * half:512 * half + 512],
                                             start=(k == 0), stop=(k == kd - 1))
                    last.then_inc(mm, 1)
                block_loop(pe, body)

            @block.scalar
            def _(act):
                if engines.get("before_scalar"):
                    engines["before_scalar"](act)

                def body(n, u, b, grp):
                    engines["scalar"](act, n, u, b, grp)
                block_loop(act, body)

            @block.vector
            def _(dve):
                if engines.get("before_vector"):
                    engines["before_vector"](dve)

                def body(n, u, b, grp):
                    if engines.get("vector"):
                        engines["vector"](dve, n, u, b, grp)
                    dve.wait_ge(mm, n + 1)
                    dve.wait_ge(x_in[u], 8 * n + 16 - 8 * u)
                    dve.tensor_tensor(t[:, u].rearrange("p (h n) -> p h n", h=2), PS[:, 2 * u:2 * u + 2, :],
                                      g.gate_row[:, grp].rearrange("p (h n) -> p h n", h=2),
                                      ALU.mult).then_inc(gated, 1)
                    dve.wait_ge(gated, n + 1)
                    dve.tensor_tensor(x[:, u], x[:, u], t[:, u], ALU.add).then_inc(added, 1)
                block_loop(dve, body)

            @block.gpsimd
            def _(pool):
                def body(n, u, b, grp):
                    pool.wait_ge(added, n + 1)
                    rows = bass.ds(b * P, P) if grp else slice(0, P)
                    pool.dma_start(g.res[rows, :], x[:, u]).then_inc(saved[u], 16)
                block_loop(pool, body)


def mla_out(nc, g, io, m):
    def take(st, mm):
        oc = st.sb("oc", [P, 2, HEADS, P])
        oc_ok = st.sem("oc_ok")

        def scalar(act, n, u, b, grp):
            if u == 0:
                act.wait_ge(mm, n)
            else:
                act.wait_ge(mm, n - 1)
            cols = bass.ds(b * P, P) if grp else slice(0, P)
            act.copy(oc[:, u], m.oT[:, :, cols]).then_inc(oc_ok, 1)
        return oc, oc_ok, {"scalar": scalar}
    project_out(nc, g, "wo", 0, HEADS, io["mla_w_o"][0], take)

def choose(nc, g, io, layer):
    with Stage(nc, f"topk{layer}") as st:
        best = st.sb("best", [NE, 8])
        at = st.sb("at", [NE, 8], U32)
        vals = st.sb("vals", [NE, CAP])
        rows = st.sb("rows", [NE, CAP])
        chain, picked, tp, out = st.sem("chain"), st.sem("picked"), st.sem("tp"), st.sem("out")
        PS = g.PS
        mod = Modulation(st, g, io, layer + 1) if layer + 1 < DEPTH else None
        with nc.Block(no_gpsimd_drain=True) as block:
            if mod:
                @block.sync
                def _(sp):
                    mod.sync(sp)

                @block.scalar
                def _(act):
                    mod.scalar(act)

            @block.vector
            def _(dve):
                def rounds(values, first, count, before):
                    with dve.Fori(0, count) as i:
                        steps = Steps(dve, chain, i, 5, before)
                        steps.did(dve.max(best[:], values))
                        wait_alone(dve, chain, steps.base + 1)
                        steps.did(dve.max_index(at[:], best[:], values))
                        steps.did(dve.tensor_copy(vals[:, bass.ds(first + i * 8, 8)], best[:]))
                        wait_alone(dve, chain, steps.base + 2)
                        steps.did(dve.match_replace(values, best[:], values, -1.0))
                        steps.did(dve.tensor_copy(rows[:, bass.ds(first + i * 8, 8)], at[:]))
                        steps.settle()
                rounds(g.aff[:, SEQ:T], 0, CAP_S // 8, 0)
                rounds(g.aff[:, 0:SEQ], CAP_S, CAP_P // 8, 5 * CAP_S // 8)
                dve.tensor_scalar(rows[:, 0:CAP_S], rows[:, 0:CAP_S], float(SEQ), None, ALU.add).then_inc(picked, 1)
                if mod:
                    mod.vector(dve)
                dve.wait_ge(tp, 1)
                dve.tensor_copy(g.row_s[:], PS[:, 0, 0:NE]).then_inc(out, 1)
                dve.tensor_copy(g.gate_s[:], PS[:, 0, NE:2 * NE]).then_inc(out, 1)
                dve.tensor_copy(g.row_p[:], PS[0:CAP_P, 0, 2 * NE:3 * NE]).then_inc(out, 1)
                dve.tensor_copy(g.gate_p[:], PS[0:CAP_P, 0, 3 * NE:4 * NE]).then_inc(out, 1)

            @block.tensor
            def _(pe):
                if mod:
                    mod.tensor(pe)
                pe.wait_ge(picked, 1)
                ident = g.ident[0:NE, 0:NE]
                pe.transpose(PS[:, 0, 0:NE], rows[:, 0:CAP_S], ident)
                pe.transpose(PS[:, 0, NE:2 * NE], vals[:, 0:CAP_S], ident)
                pe.transpose(PS[0:CAP_P, 0, 2 * NE:3 * NE], rows[:, CAP_S:CAP], ident)
                pe.transpose(PS[0:CAP_P, 0, 3 * NE:4 * NE], vals[:, CAP_S:CAP], ident).then_inc(tp, 1)


def experts(nc, g, io, layer):
    with Stage(nc, f"moe{layer}") as st:
        HB = 512
        wg = st.sb("wg", [P, 2, KD, HB])
        wu = st.sb("wu", [P, 2, KD, HB])
        wd = st.sb("wd", [P, 2, KD, HB])
        x_s = st.sb("x_s", [P, D])
        x_p = st.sb("x_p", [CAP_P, D])
        id_s = st.sb("id_s", [P, 2], U32)
        id_p = st.sb("id_p", [CAP_P, 2], U32)
        xT = st.sb("xT", [P, KD, CAP])
        sg = st.sb("sg", [P, KD, CAP])
        hid = st.sb("hid", [P, KD, CAP])
        ye = st.sb("ye", [P, KD, CAP])
        y_s = st.sb("y_s", [P, D])
        y_p = st.sb("y_p", [CAP_P, D])
        wg_in = [st.sem("wg_in0"), st.sem("wg_in1")]
        wu_in = [st.sem("wu_in0"), st.sem("wu_in1")]
        wd_in = [st.sem("wd_in0"), st.sem("wd_in1")]
        xs_in, xp_in = st.sem("xs_in"), st.sem("xp_in")
        id_ok, ys_out, yp_out = st.sem("id_ok"), st.sem("ys_out"), st.sem("yp_out")
        x_mm, xa_ok, xd_ok = st.sem("x_mm"), st.sem("xa_ok"), st.sem("xd_ok")
        half_gu, gu_mm, sg_ok, hid_ok = st.sem("half_gu"), st.sem("gu_mm"), st.sem("sg_ok"), st.sem("hid_ok")
        half_d, d_mm, ye_ok = st.sem("half_d"), st.sem("d_mm"), st.sem("ye_ok")
        back, ys_ok, yp_ok = st.sem("back"), st.sem("ys_ok"), st.sem("yp_ok")
        PS = g.PS
        TRIOS = [(0, 3), (3, 6), (6, 8)]

        def turns(eng, body):
            with eng.Fori(0, NE - 1) as e:
                body(e, True)
            body(NE - 1, False)

        def trio(bank, a, b):
            return PS[:, bank, 0:(b - a) * CAP].rearrange("p (m c) -> p m c", c=CAP)

        with nc.Block(no_gpsimd_drain=True) as block:
            @block.sync
            def _(sp):
                def view(w):
                    return w[layer].rearrange("e (k p) n -> p e k n", p=P)

                with sp.Fori(0, NE) as e:
                    for half in range(2):
                        sp.wait_ge(half_gu if half == 0 else gu_mm, e if half == 0 else 3 * e)
                        for buf, w, s in ((wg, io["moe_w_gate"], wg_in), (wu, io["moe_w_up"], wu_in)):
                            sp.dma_start(buf[:, half], view(w)[:, bass.ds(e, 1), :, HB * half:HB * half + HB].squeeze(1)
                                         ).then_inc(s[half], 16)
                    for half in range(2):
                        sp.wait_ge(half_d if half == 0 else d_mm, e if half == 0 else 3 * e)
                        sp.dma_start(wd[:, half], view(io["moe_w_down"])[:, bass.ds(e, 1), :, HB * half:HB * half + HB].squeeze(1)
                                     ).then_inc(wd_in[half], 16)

            @block.gpsimd
            def _(pool):
                def gather(e, n_ids):
                    pool.tensor_copy(id_s[:, 0:1], g.row_s[:, bass.ds(e, 1)]).then_inc(id_ok, 1)
                    pool.tensor_copy(id_p[:, 0:1], g.row_p[:, bass.ds(e, 1)]).then_inc(id_ok, 1)
                    wait_alone(pool, id_ok, n_ids + 2)
                    pool.indirect_dma_start(x_s[:], None, g.normed, bass.IndirectOffsetOnAxis(ap=id_s[:, 0:1], axis=0),
                                            bounds_check=T - 1, oob_is_err=False).then_inc(xs_in, 16)
                    pool.indirect_dma_start(x_p[:], None, g.normed, bass.IndirectOffsetOnAxis(ap=id_p[:, 0:1], axis=0),
                                            bounds_check=T - 1, oob_is_err=False).then_inc(xp_in, 16)

                def scatter(e, n_ids):
                    wait_alone(pool, ys_out, 16 * e)
                    pool.wait_ge(yp_out, 16 * e)
                    pool.tensor_copy(id_s[:, 1:2], g.row_s[:, bass.ds(e, 1)]).then_inc(id_ok, 1)
                    pool.tensor_copy(id_p[:, 1:2], g.row_p[:, bass.ds(e, 1)]).then_inc(id_ok, 1)
                    wait_alone(pool, id_ok, n_ids + 2)
                    wait_alone(pool, ys_ok, 2 * e + 2)
                    pool.indirect_dma_start(g.res, bass.IndirectOffsetOnAxis(ap=id_s[:, 1:2], axis=0), y_s[:], None,
                                            bounds_check=T - 1, compute_op=ALU.add).then_inc(ys_out, 16)
                    wait_alone(pool, yp_ok, e + 1)
                    pool.indirect_dma_start(g.res, bass.IndirectOffsetOnAxis(ap=id_p[:, 1:2], axis=0), y_p[:], None,
                                            bounds_check=T - 1, compute_op=ALU.add).then_inc(yp_out, 16)

                gather(0, 0)

                def body(e, more):
                    if more:
                        pool.wait_ge(x_mm, 3 * e + 3)
                        gather(e + 1, 4 * e + 2)
                        scatter(e, 4 * e + 4)
                    else:
                        scatter(e, 4 * e + 2)
                turns(pool, body)
                pool.wait_ge(ys_out, 16 * NE)
                pool.wait_ge(yp_out, 16 * NE)

            @block.tensor
            def _(pe):
                def tokens(e, rows_read, up_read):
                    pe.wait_ge(ys_ok, rows_read)
                    pe.wait_ge(xs_in, 16 * e + 16)
                    for k in range(KD):
                        last = pe.transpose(PS[:, 6 + k // 4, P * (k % 4):P * (k % 4) + P], x_s[:, P * k:P * k + P], g.ident[:])
                        if k % 4 == 3:
                            last.then_inc(x_mm, 1)
                    pe.wait_ge(hid_ok, up_read)
                    wait_alone(pe, xp_in, 16 * e + 16)
                    for k in range(KD):
                        last = pe.transpose(PS[:, 3, CAP_P * k:CAP_P * k + CAP_P], x_p[:, P * k:P * k + P],
                                            g.ident[0:CAP_P, 0:CAP_P])
                    last.then_inc(x_mm, 1)

                def rows_back(a, b):
                    for k in range(a, b):
                        pe.transpose(PS[:, 6 + k // 4, P * (k % 4):P * (k % 4) + P], ye[:, k, 0:CAP_S], g.ident[:])
                        last = pe.transpose(PS[0:CAP_P, 4 + k // 4, P * (k % 4):P * (k % 4) + P], ye[:, k, CAP_S:CAP], g.ident[:])
                    return last

                tokens(0, 0, 0)

                def body(e, more):
                    pe.wait_ge(xa_ok, 4 * e + 4)
                    pe.wait_ge(xd_ok, 6 * e + 6)
                    pe.wait_ge(ye_ok, 6 * e)
                    pe.wait_ge(yp_ok, e)
                    for q, (a, b) in enumerate(TRIOS):
                        for w, w_in, bank in ((wg, wg_in, q), (wu, wu_in, 3 + q)):
                            for f in range(a, b):
                                if f % 4 == 0:
                                    pe.wait_ge(w_in[f // 4], 16 * e + 16)
                                for k in range(KD):
                                    last = pe.matmul(PS[:, bank, CAP * (f - a):CAP * (f - a + 1)],
                                                     w[:, f // 4, k, P * (f % 4):P * (f % 4) + P], xT[:, k, :],
                                                     start=(k == 0), stop=(k == KD - 1))
                                if f == 3 and bank == 4:
                                    last.then_inc(half_gu, 1)
                        last.then_inc(gu_mm, 1)
                    if more:
                        tokens(e + 1, 2 * e, 3 * e + 1)
                    pe.wait_ge(hid_ok, 3 * e + 3)
                    for q, (a, b) in enumerate(TRIOS):
                        if q == 2:
                            if more:
                                pe.wait_ge(xa_ok, 4 * e + 8)
                                pe.wait_ge(xd_ok, 6 * e + 12)
                            else:
                                pe.wait_ge(ys_ok, 2 * e)
                            pe.wait_ge(ye_ok, 6 * e + 2)
                            rows_back(*TRIOS[0])
                        for f in range(a, b):
                            if f % 4 == 0:
                                pe.wait_ge(wd_in[f // 4], 16 * e + 16)
                            for k in range(KD):
                                last = pe.matmul(PS[:, q, CAP * (f - a):CAP * (f - a + 1)],
                                                 wd[:, f // 4, k, P * (f % 4):P * (f % 4) + P], hid[:, k, :],
                                                 start=(k == 0), stop=(k == KD - 1))
                            if f == 3:
                                last.then_inc(half_d, 1)
                        last.then_inc(d_mm, 1)
                    pe.wait_ge(ye_ok, 6 * e + 4)
                    rows_back(*TRIOS[1])
                    pe.wait_ge(ye_ok, 6 * e + 6)
                    rows_back(*TRIOS[2]).then_inc(back, 1)
                turns(pe, body)

            @block.scalar
            def _(act):
                def tokens(e):
                    act.wait_ge(x_mm, 3 * e + 2)
                    for k in range(4, KD):
                        act.activation(xT[:, k, 0:CAP_S], PS[:, 7, P * (k - 4):P * (k - 3)], ACT.Identity,
                                       scale=g.gain[:, layer, 1, k, 1:2], bias=g.shift[:, layer, 1, k, 1:2]).then_inc(xa_ok, 1)
                tokens(0)

                def body(e, more):
                    for q, (a, b) in enumerate(TRIOS):
                        act.wait_ge(gu_mm, 3 * e + q + 1)
                        act.activation(sg[:, a:b], trio(q, a, b), ACT.Silu).then_inc(sg_ok, 1)
                    if more:
                        tokens(e + 1)
                    act.wait_ge(back, e + 1)
                    act.wait_ge(ys_out, 16 * e)
                    for half in range(2):
                        act.activation(y_s[:, 512 * half:512 * half + 512], PS[:, 6 + half, :], ACT.Copy,
                                       scale=g.gate_s[:, bass.ds(e, 1)]).then_inc(ys_ok, 1)
                turns(act, body)

            @block.vector
            def _(dve):
                def tokens(e):
                    dve.wait_ge(x_mm, 3 * e + 1)
                    for k in range(4):
                        dve.tensor_scalar(xT[:, k, 0:CAP_S], PS[:, 6, P * k:P * k + P], g.gain[:, layer, 1, k, 1:2],
                                          g.shift[:, layer, 1, k, 1:2], ALU.mult, ALU.add).then_inc(xd_ok, 1)
                    dve.wait_ge(x_mm, 3 * e + 3)
                    dve.tensor_tensor(xT[:, :, CAP_S:CAP], PS[:, 3, 0:P].rearrange("p (k c) -> p k c", k=KD),
                                      g.gain[:, layer, 1, :, 0:1].to_broadcast([P, KD, CAP_P]), ALU.mult).then_inc(xd_ok, 1)
                    dve.wait_ge(xd_ok, 6 * e + 5)
                    dve.tensor_tensor(xT[:, :, CAP_S:CAP], xT[:, :, CAP_S:CAP],
                                      g.shift[:, layer, 1, :, 0:1].to_broadcast([P, KD, CAP_P]), ALU.add).then_inc(xd_ok, 1)
                tokens(0)

                def body(e, more):
                    for q, (a, b) in enumerate(TRIOS):
                        dve.wait_ge(sg_ok, 3 * e + q + 1)
                        dve.tensor_tensor(hid[:, a:b], sg[:, a:b], trio(3 + q, a, b), ALU.mult).then_inc(hid_ok, 1)
                    if more:
                        tokens(e + 1)
                    for q, (a, b) in enumerate(TRIOS):
                        dve.wait_ge(d_mm, 3 * e + q + 1)
                        for c0, c1, j in ((0, CAP_S, 1), (CAP_S, CAP, 0)):
                            dve.tensor_tensor(ye[:, a:b, c0:c1], trio(q, a, b)[:, :, c0:c1],
                                              g.modc[:, layer, 40 + a:40 + b, j:j + 1].to_broadcast([P, b - a, c1 - c0]),
                                              ALU.mult).then_inc(ye_ok, 1)
                    dve.wait_ge(back, e + 1)
                    dve.wait_ge(yp_out, 16 * e)
                    dve.tensor_scalar(y_p[:].rearrange("p (h n) -> p h n", h=2), PS[0:CAP_P, 4:6, :],
                                      g.gate_p[:, bass.ds(e, 1)], None, ALU.mult).then_inc(yp_ok, 1)
                turns(dve, body)

def ssm_gate_and_steps(nc, g, io, hT, q):
    with Stage(nc, "ssmz") as st:
        w = st.sb("w", [P, 2, KD, 512])
        zs = st.sb("zs", [P, 3, 512])
        wdt = st.sb("wdt", [P, KD, 2 * SH])
        bias = st.sb("bias", [P, 2 * SH])
        alog = st.sb("alog", [P, 2 * SH])
        a = st.sb("a", [P, 2 * SH])
        N2 = 2 * NB * SH
        v, e, s2, q2, pw = (st.sb(n, [P, N2]) for n in ("v", "e", "s2", "q2", "pw"))
        diff = st.sb("diff", [P, 2, NB, SH])
        w_in = [st.sem("w_in0"), st.sem("w_in1")]
        small, z_mm, z_ok = st.sem("small"), st.sem("z_mm"), st.sem("z_ok")
        z_out = [st.sem(f"z_out{i}") for i in range(3)]
        dt_mm, v_ok, e_ok, a_ok = st.sem("dt_mm"), st.sem("v_ok"), st.sem("e_ok"), st.sem("a_ok")
        chain, power, cum, exps = st.sem("chain"), st.sem("power"), st.sem("cum"), st.sem("exps")
        PS = g.PS
        w_dram = io["ssm_w_in"][0].rearrange("(k p) n -> p k n", p=P)
        NC_ = DI // 512

        with nc.Block(no_gpsimd_drain=True) as block:
            @block.sync
            def _(sp):
                sp.dma_start(wdt[:], w_dram[:, :, DI + CONV:IN_DIM]).then_inc(small, 16)
                sp.dma_start(bias[:], io["ssm_dt_bias"][0].rearrange("d h -> (d h)").partition_broadcast(P)).then_inc(small, 16)
                sp.dma_start(alog[:], io["ssm_a_log"][0].rearrange("d h -> (d h)").partition_broadcast(P)).then_inc(small, 16)
                sp.dma_start(q.skip[:], io["ssm_d_skip"][0].partition_broadcast(P)).then_inc(small, 16)
                with sp.Fori(0, NC_ // 2) as i:
                    for u in range(2):
                        sp.wait_ge(z_mm, 2 * NB * i)
                        sp.dma_start(w[:, u], w_dram[:, :, bass.ds(i * 1024 + 512 * u, 512)]).then_inc(w_in[u], 16)

            @block.gpsimd
            def _(pool):
                with pool.Fori(0, NC_ // 2) as i:
                    for u in range(2):
                        for b in range(NB):
                            pool.wait_ge(z_ok, 2 * NB * i + NB * u + b + 1)
                            pool.dma_start(g.z[P * b:P * b + P, bass.ds(i * 1024 + 512 * u, 512)], zs[:, b % 3]
                                           ).then_inc(z_out[b % 3], 16)
                for s in z_out:
                    pool.wait_ge(s, 16 * NC_ * NB // 3)

            @block.tensor
            def _(pe):
                pe.wait_ge(small, 64)
                for b in range(NB):
                    for k in range(KD):
                        last = pe.matmul(PS[:, 4 + b // 8, 64 * (b % 8):64 * (b % 8) + 64], hT[:, k, P * b:P * b + P],
                                         wdt[:, k], start=(k == 0), stop=(k == KD - 1))
                last.then_inc(dt_mm, 1)
                pe.wait_ge(chain, 12)
                f = q.da[:].rearrange("p d b h -> p d (b h)")
                for d in range(2):
                    pe.matmul(PS[:, 6, 0:NB * SH], (g.upper, g.lower)[d][:], f[:, d], start=True, stop=True).then_inc(cum, 1)
                    pe.matmul(PS[:, 7, 0:NB * SH], g.ones[:], f[:, d], start=True, stop=True).then_inc(cum, 1)
                    pe.wait_ge(exps, 2 * d + 2)
                    pe.wait_ge(chain, 13 + d)
                with pe.Fori(0, NC_ // 2) as i:
                    for u in range(2):
                        pe.wait_ge(w_in[u], 16 * i + 16)
                        for b in range(NB):
                            if b < 4:
                                pe.wait_ge(z_ok, 2 * NB * i)
                            else:
                                pe.wait_ge(z_ok, 2 * NB * i + NB * u + b - 3)
                            for k in range(KD):
                                last = pe.matmul(PS[:, 4 * u + b % 4, :], hT[:, k, P * b:P * b + P], w[:, u, k, :],
                                                 start=(k == 0), stop=(k == KD - 1))
                            last.then_inc(z_mm, 1)

            @block.scalar
            def _(act):
                act.wait_ge(small, 64)
                act.activation(a[:], alog[:], ACT.Exp).then_inc(a_ok, 1)
                act.wait_ge(v_ok, 4)
                act.activation(e[:], v[:], ACT.Abs).then_inc(e_ok, 1)
                act.wait_ge(e_ok, 1)
                act.activation(e[:], e[:], ACT.Exp, scale=-1.0).then_inc(e_ok, 1)
                for d in range(2):
                    act.wait_ge(cum, 2 * d + 2)
                    ps = PS[:, 6:8, 0:NB * SH]
                    act.activation(q.grow[:, d].rearrange("p b h -> p (b h)"), ps[:, 0], ACT.Exp).then_inc(exps, 1)
                    act.activation(q.dec[:, d].rearrange("p b h -> p (b h)"), ps[:, 1], ACT.Exp).then_inc(exps, 1)
                act.wait_ge(chain, 14)
                act.activation(diff[:], diff[:], ACT.Exp).then_inc(exps, 1)
                with act.Fori(0, NC_ // 2) as i:
                    for u in range(2):
                        for b in range(NB):
                            act.wait_ge(z_mm, 2 * NB * i + NB * u + b + 1)
                            act.wait_ge(z_out[b % 3], 16 * (6 * i + 3 * u + b // 3))
                            act.activation(zs[:, b % 3], PS[:, 4 * u + b % 4, :], ACT.Silu).then_inc(z_ok, 1)

            @block.vector
            def _(dve):
                dve.wait_ge(dt_mm, 1)
                vv = v[:].rearrange("p (d b h) -> p d b h", d=2, b=NB)
                for d in range(2):
                    for b0, b1, bank in ((0, 8, 4), (8, 9, 5)):
                        dve.tensor_tensor(vv[:, d, b0:b1],
                                          PS[:, bank, 0:64 * (b1 - b0)].rearrange("p (b d h) -> p b d h", d=2, h=SH)[:, :, d],
                                          bias[:, SH * d:SH * d + SH].unsqueeze(1).to_broadcast([P, b1 - b0, SH]),
                                          ALU.add).then_inc(v_ok, 1)
                steps, powers = Steps(dve, chain), Steps(dve, power)
                dve.wait_ge(e_ok, 2)
                steps.alone(dve.tensor_scalar(s2[:], e[:], 2.0, None, ALU.add))
                steps.alone(dve.reciprocal(s2[:], s2[:]))
                steps.alone(dve.tensor_tensor(s2[:], s2[:], e[:], ALU.mult))
                steps.alone(dve.tensor_tensor(q2[:], s2[:], s2[:], ALU.mult))
                steps.alone(dve.tensor_scalar(pw[:], q2[:], 1.0 / 15, 1.0 / 13, ALU.mult, ALU.add))
                for c in (11, 9, 7, 5, 3):
                    powers.alone(dve.tensor_tensor(pw[:], pw[:], q2[:], ALU.mult))
                    powers.alone(dve.tensor_scalar(pw[:], pw[:], 1.0 / c, None, ALU.add))
                steps.alone(dve.tensor_tensor(pw[:], pw[:], q2[:], ALU.mult))
                steps.alone(dve.scalar_tensor_tensor(out=pw[:], in0=pw[:], scalar=1.0, in1=s2[:], op0=ALU.add, op1=ALU.mult))
                steps.alone(dve.tensor_scalar(v[:], v[:], 0.0, None, ALU.max))
                dt = q.dt[:].rearrange("p d b h -> p (d b h)")
                steps.alone(dve.scalar_tensor_tensor(out=dt, in0=pw[:], scalar=2.0, in1=v[:], op0=ALU.mult, op1=ALU.add))
                dve.wait_ge(a_ok, 1)
                steps.alone(dve.tensor_scalar(a[:], a[:], -1.0, None, ALU.mult))
                for d in range(2):
                    steps.did(dve.tensor_tensor(q.da[:, d], q.dt[:, d],
                                                a[:, SH * d:SH * d + SH].unsqueeze(1).to_broadcast([P, NB, SH]), ALU.mult))
                steps.settle()
                assert steps.n == 12
                for d in range(2):
                    dve.wait_ge(exps, 2 * d + 2)
                    dd = diff[:, d].rearrange("p b h -> p (b h)")
                    powers.alone(dve.tensor_copy(dd, PS[:, 7, 0:NB * SH]))
                    steps.alone(dve.tensor_tensor(dd, dd, PS[:, 6, 0:NB * SH], ALU.subtract))
                dve.wait_ge(exps, 5)
                dve.tensor_tensor(q.toend[:], diff[:], q.dt[:], ALU.mult).then_inc(a_ok, 1)


def ssm_conv(nc, g, io, hT):
    with Stage(nc, "conv") as st:
        w = st.sb("w", [P, 2, KD, 2 * P])
        W = T + 4
        at_p, at_s = 1, SEQ + 3
        pre = st.sb("pre", [P, 2, W])
        acc = st.sb("acc", [P, 2, W])
        acc2 = st.sb("acc2", [P, W])
        act_ = st.sb("act", [P, 2, W])
        tok = st.sb("tok", [P, 2, NB, P])
        w_in = [st.sem("w_in0"), st.sem("w_in1")]
        zero, mm, pre_ok, chain = st.sem("zero"), st.sem("mm"), st.sem("pre_ok"), st.sem("chain")
        acc_ok, silu_ok, tp, ta_ok, td_ok = st.sem("acc_ok"), st.sem("silu_ok"), st.sem("tp"), st.sem("ta_ok"), st.sem("td_ok")
        saved_t = [st.sem("saved_t0"), st.sem("saved_t1")]
        saved_c = [st.sem("saved_c0"), st.sem("saved_c1")]
        PS = g.PS
        w_dram = io["ssm_w_in"][0].rearrange("(k p) n -> p k n", p=P)

        def turns(eng, body):
            with eng.Fori(0, DI // 512) as i:
                body(4 * i, "x", i)
            body(DI // P, "b", DI // 512)
            body(DI // P + 4, "c", DI // 512 + 1)

        def cols(b):
            return slice(at_p, at_p + P) if b == 0 else slice(at_s + P * (b - 1), at_s + P * b)

        with nc.Block(no_gpsimd_drain=True) as block:
            @block.sync
            def _(sp):
                def body(m0, kind, i):
                    for s in range(2):
                        sp.wait_ge(mm, 4 * i)
                        sp.dma_start(w[:, s], w_dram[:, :, bass.ds(m0 * P + DI + 2 * P * s, 2 * P)]).then_inc(w_in[s], 16)
                turns(sp, body)

            @block.gpsimd
            def _(pool):
                for s in range(2):
                    pool.memset(pre[:, s], 0.0).then_inc(zero, 1)

                def body(m0, kind, i):
                    for v in range(4):
                        if kind != "c":
                            pool.wait_ge(ta_ok, 4 * i + v + 1)
                            pool.wait_ge(td_ok, 8 * i + 2 * v + 2)
                            out = g.xs if kind == "x" else g.btok
                            c = bass.ds(m0 * P + P * v, P) if kind == "x" else slice(P * v, P * v + P)
                            pool.dma_start(out.rearrange("(b p) c -> p b c", p=P)[:, :, c], tok[:, v % 2]
                                           ).then_inc(saved_t[v % 2], 16)
                        if kind != "x":
                            pool.wait_ge(silu_ok, 4 * i + v + 1)
                            out = g.bT if kind == "b" else g.cT
                            s = saved_c[v % 2]
                            pool.dma_start(out[P * v:P * v + P, 0:SEQ], act_[:, v % 2, at_p:at_p + SEQ]).then_inc(s, 16)
                            pool.dma_start(out[P * v:P * v + P, SEQ:T], act_[:, v % 2, at_s:at_s + DEC]).then_inc(s, 16)
                turns(pool, body)
                for s in saved_t:
                    pool.wait_ge(s, 16 * 10)
                for s in saved_c:
                    pool.wait_ge(s, 16 * 8)

            @block.tensor
            def _(pe):
                def project(i, v):
                    if v % 2 == 0:
                        pe.wait_ge(w_in[v // 2], 16 * i + 16)
                    if v < 2:
                        pe.wait_ge(pre_ok, 4 * i)
                    else:
                        pe.wait_ge(pre_ok, 4 * i + v - 1)
                    for t in range(NT):
                        for k in range(KD):
                            last = pe.matmul(PS[:, 3 * (v % 2) + t, 0:TILE], w[:, v // 2, k, P * (v % 2):P * (v % 2) + P],
                                             hT[:, k, TILE * t:TILE * t + TILE], start=(k == 0), stop=(k == KD - 1))
                    last.then_inc(mm, 1)

                def turn(i, v):
                    pe.wait_ge(silu_ok, 4 * i + v + 1)
                    pe.wait_ge(td_ok, 8 * i + 2 * v)
                    pe.wait_ge(ta_ok, 4 * i + v)
                    for b in range(NB):
                        if b == 8:
                            pe.wait_ge(td_ok, 8 * i + 2 * v + 1)
                        last = pe.transpose(PS[:, 6 + b // 4 % 2, P * (b % 4):P * (b % 4) + P], act_[:, v % 2, cols(b)], g.ident[:])
                        if b in (3, 7, 8):
                            last.then_inc(tp, 1)

                def body(m0, kind, i):
                    for v in range(4):
                        project(i, v)
                        if v and kind != "c":
                            turn(i, v - 1)
                    if kind != "c":
                        turn(i, 3)
                turns(pe, body)

            @block.scalar
            def _(act):
                act.wait_ge(zero, 2)

                def take(i, v):
                    act.wait_ge(mm, 4 * i + v + 1)
                    if v < 2:
                        act.wait_ge(acc_ok, 4 * i)
                    else:
                        act.wait_ge(acc_ok, 4 * i + v - 1)
                    s, b0 = v % 2, 3 * (v % 2)
                    act.copy(pre[:, s, at_p:at_p + SEQ], PS[:, b0, 0:SEQ])
                    act.copy(pre[:, s, at_s:at_s + TILE - SEQ], PS[:, b0, SEQ:TILE])
                    act.copy(pre[:, s, at_s + TILE - SEQ:at_s + DEC].rearrange("p (t n) -> p t n", t=2),
                             PS[:, b0 + 1:b0 + 3, 0:TILE]).then_inc(pre_ok, 1)

                def silu(i, v, kind):
                    act.wait_ge(acc_ok, 4 * i + v + 1)
                    if kind != "c":
                        act.wait_ge(tp, 12 * i + max(0, 3 * (v - 1)))
                    if kind == "b" and v >= 2:
                        act.wait_ge(saved_c[v % 2], 32)
                    if kind == "c":
                        act.wait_ge(saved_c[v % 2], 64 + 32 * (v // 2))
                    act.activation(act_[:, v % 2, 1:W - 1], acc[:, v % 2, 1:W - 1], ACT.Silu).then_inc(silu_ok, 1)

                def turned(i, v):
                    act.wait_ge(tp, 12 * i + 3 * v + 2)
                    act.wait_ge(saved_t[v % 2], 32 * i + 16 * (v // 2))
                    act.copy(tok[:, v % 2, 4:8], PS[:, 7, :].rearrange("p (b c) -> p b c", c=P)).then_inc(ta_ok, 1)

                def body(m0, kind, i):
                    for v in range(4):
                        take(i, v)
                        if v and kind != "c":
                            turned(i, v - 1)
                        silu(i, v, kind)
                    if kind != "c":
                        turned(i, 3)
                turns(act, body)

            @block.vector
            def _(dve):
                def convolve(m0, i, v):
                    s = v % 2
                    m = m0 + v
                    n = slice(1, W - 1)
                    wj = [g.convw[:, j, bass.ds(m, 1)] for j in range(3)]
                    steps = Steps(dve, chain, i, 8, 2 * v)
                    dve.wait_ge(pre_ok, 4 * i + v + 1)
                    if v < 2:
                        dve.wait_ge(silu_ok, 4 * i)
                    else:
                        dve.wait_ge(silu_ok, 4 * i + v - 1)
                    steps.alone(dve.tensor_scalar(acc[:, s, n], pre[:, s, n], wj[1], g.vcol[:, bass.ds(m + V_CB, 1)],
                                                  ALU.mult, ALU.add))
                    steps.alone(dve.scalar_tensor_tensor(out=acc2[:, n], in0=pre[:, s, 0:W - 2], scalar=wj[0],
                                                         in1=acc[:, s, n], op0=ALU.mult, op1=ALU.add))
                    dve.scalar_tensor_tensor(out=acc[:, s, n], in0=pre[:, s, 2:W], scalar=wj[2],
                                             in1=acc2[:, n], op0=ALU.mult, op1=ALU.add).then_inc(acc_ok, 1)

                def turned(i, v):
                    dve.wait_ge(tp, 12 * i + 3 * v + 1)
                    dve.wait_ge(saved_t[v % 2], 32 * i + 16 * (v // 2))
                    dve.tensor_copy(tok[:, v % 2, 0:4], PS[:, 6, :].rearrange("p (b c) -> p b c", c=P)).then_inc(td_ok, 1)
                    dve.wait_ge(tp, 12 * i + 3 * v + 3)
                    dve.tensor_copy(tok[:, v % 2, 8], PS[:, 6, 0:P]).then_inc(td_ok, 1)

                def body(m0, kind, i):
                    for v in range(4):
                        convolve(m0, i, v)
                        if v and kind != "c":
                            turned(i, v - 1)
                    if kind != "c":
                        turned(i, 3)
                turns(dve, body)


def ssm_states(nc, g, io, q):
    NQ = DEC // P
    with Stage(nc, "states") as st:
        x = st.sb("x", [P, 2, 2, DI])
        b_ = st.sb("b", [P, 2, 2, GN])
        xw = st.sb("xw", [P, 2, DI])
        h = st.sb("h", [P, 2, 2, DI])
        raw = st.sb("raw", [P, 2, DI // P, NS])
        fin = st.sb("fin", [P, 2, DI // P, NS])
        x_in = [[st.sem(f"x_in{d}{u}") for u in range(2)] for d in range(2)]
        raw_in, init_mm, init_ok = st.sem("raw_in"), st.sem("init_mm"), st.sem("init_ok")
        xw_ok = [st.sem("xw_ok0"), st.sem("xw_ok1")]
        s_mm = [st.sem("s_mm0"), st.sem("s_mm1")]
        h_ok = [st.sem("h_ok0"), st.sem("h_ok1")]
        dec_ok = [st.sem("dec_ok0"), st.sem("dec_ok1")]
        h_out = [[st.sem(f"h_out{d}{u}") for u in range(2)] for d in range(2)]
        fin_mm, fin_ok, fin_out, zero = st.sem("fin_mm"), st.sem("fin_ok"), st.sem("fin_out"), st.sem("zero")
        PS = g.PS
        NBK = DI // P

        def loop(eng, body):
            with eng.Fori(0, NQ // 2) as i:
                for u in range(2):
                    body(2 * i + u, u, (2 * i + u + 1, i * -2 + NQ - u))
            body(NQ, 0, (0, 0))

        def rows(b, n):
            return bass.ds(b * P, P) if n is not NQ else slice(0, P)

        with nc.Block(no_gpsimd_drain=True) as block:
            @block.sync
            def _(sp):
                for d in range(2):
                    sp.dma_start(raw[:, d], io["state_ssm"][0, 0, d].rearrange("h p n -> (h p) n").rearrange(
                        "(m q) n -> q m n", q=P)).then_inc(raw_in, 16)

                def body(n, u, bs):
                    for d in range(2):
                        if u == 0:
                            sp.wait_ge(s_mm[d], n)
                        else:
                            sp.wait_ge(s_mm[d], n - 1)
                        sp.dma_start(x[:, d, u], g.xs[rows(bs[d], n), :]).then_inc(x_in[d][u], 16)
                        sp.dma_start(b_[:, d, u], g.btok[rows(bs[d], n), :]).then_inc(x_in[d][u], 16)
                loop(sp, body)

            @block.gpsimd
            def _(pool):
                def body(n, u, bs):
                    for d in range(2):
                        pool.wait_ge(x_in[d][u], 16 * n + 32 - 16 * u)
                        pool.wait_ge(s_mm[d], n)
                        te = q.toend[:, d, bass.ds(bs[d], 1)] if n is not NQ else q.toend[:, d, 0:1]
                        pool.tensor_tensor(xw[:, d].rearrange("p (h c) -> p h c", c=HD),
                                           x[:, d, u].rearrange("p (h c) -> p h c", c=HD),
                                           te.squeeze(1).unsqueeze(2).to_broadcast([P, SH, HD]), ALU.mult).then_inc(xw_ok[d], 1)
                loop(pool, body)

            @block.tensor
            def _(pe):
                pe.wait_ge(raw_in, 32)
                for d in range(2):
                    for m in range(NBK):
                        last = pe.transpose(PS[:, 4 * d + m // 4, P * (m % 4):P * (m % 4) + P], raw[:, d, m], g.ident[:])
                    last.then_inc(init_mm, 1)

                def body(n, u, bs):
                    for d in range(2):
                        pe.wait_ge(xw_ok[d], n + 1)
                        pe.wait_ge(h_ok[d], n + 1)
                        for k in range(SG):
                            last = pe.matmul(PS[:, 4 * d + k, :], b_[:, d, u, NS * k:NS * k + NS], xw[:, d, 512 * k:512 * k + 512],
                                             start=True, stop=True)
                        last.then_inc(s_mm[d], 1)
                loop(pe, body)
                for d in range(2):
                    pe.wait_ge(h_ok[d], NQ + 3)
                    for m in range(NBK):
                        last = pe.transpose(PS[:, 4 * d + m // 4, P * (m % 4):P * (m % 4) + P], h[:, d, 1, P * m:P * m + P], g.ident[:])
                    last.then_inc(fin_mm, 1)

            @block.vector
            def _(dve):
                for d in range(2):
                    dve.wait_ge(init_mm, d + 1)
                    dve.tensor_copy(h[:, d, 0].rearrange("p (b c) -> p b c", b=4), PS[:, 4 * d:4 * d + 4, :]).then_inc(h_ok[d], 1)

                def body(n, u, bs):
                    for d in range(2):
                        if n is NQ:
                            dve.wait_ge(h_out[d][1], 16 * (NQ // 2))
                            dve.memset(h[:, d, 0], 0.0).then_inc(h_ok[d], 1)
                            dve.wait_ge(h_ok[d], NQ + 2)
                            dec = q.dec[:, d, 0]
                            ready = n + 3
                        else:
                            dec = q.dec[:, d, bass.ds(bs[d], 1)].squeeze(1)
                            dve.wait_ge(h_ok[d], n + 1)
                            ready = n + 2
                            if u == 0:
                                dve.wait_ge(h_out[d][1], 8 * n)
                            else:
                                dve.wait_ge(h_out[d][0], 8 * n + 8)
                        new = h[:, d, 1 - u].rearrange("p (h c) -> p h c", c=HD)
                        dve.tensor_tensor(new, h[:, d, u].rearrange("p (h c) -> p h c", c=HD),
                                          dec.unsqueeze(2).to_broadcast([P, SH, HD]), ALU.mult).then_inc(dec_ok[d], 1)
                        dve.wait_ge(dec_ok[d], n + 1)
                        dve.wait_ge(s_mm[d], n + 1)
                        hb = h[:, d, 1 - u].rearrange("p (b c) -> p b c", b=4)
                        dve.tensor_tensor(hb, hb, PS[:, 4 * d:4 * d + 4, :], ALU.add).then_inc(h_ok[d], 1)
                loop(dve, body)
                for d in range(2):
                    dve.wait_ge(fin_mm, d + 1)
                    dve.tensor_copy(fin[:, d].rearrange("p (b m) n -> p b (m n)", b=4), PS[:, 4 * d:4 * d + 4, :]).then_inc(fin_ok, 1)

            @block.scalar
            def _(act):
                def body(n, u, bs):
                    for d in range(2):
                        if n is NQ:
                            act.wait_ge(h_ok[d], n + 2)
                            act.dma_start(g.hin[d, 0], h[:, d, u]).then_inc(h_out[d][u], 16)
                        else:
                            act.wait_ge(h_ok[d], n + 1)
                            act.dma_start(g.hin[d, bass.ds(bs[d], 1)].squeeze(0), h[:, d, u]).then_inc(h_out[d][u], 16)
                loop(act, body)
                for d in range(2):
                    act.wait_ge(fin_ok, d + 1)
                    act.dma_start(io["new_ssm"][0, 0, d].rearrange("h p n -> (h p) n").rearrange("(m q) n -> q m n", q=P),
                                  fin[:, d]).then_inc(fin_out, 16)
                for d in range(2):
                    act.wait_ge(h_out[d][0], 16 * (NQ // 2 + 1))
                    act.wait_ge(h_out[d][1], 16 * (NQ // 2))
                act.wait_ge(fin_out, 32)


def ssm_outputs(nc, g, io, q):
    with Stage(nc, "ssd") as st:
        x = st.sb("x", [P, 2, DI])
        z = st.sb("z", [P, 2, DI])
        hin = st.sb("hin", [P, 2, 2, DI])
        bT = st.sb("bT", [P, 2, SG, P])
        cT = st.sb("cT", [P, 2, SG, P])
        tri = st.sb("tri", [P, 2, P])
        cb = st.sb("cb", [P, 2, SG, P])
        seg = st.sb("seg", [P, 2, HPG, P])
        ex = st.sb("ex", [P, 2, HPG, P])
        wt = st.sb("wt", [P, 2, HPG, P])
        t1 = st.sb("t1", [P, 512])
        t2 = st.sb("t2", [P, 512])
        t3 = st.sb("t3", [P, 512])
        y = st.sb("y", [P, 2, DI])
        junk = st.sb("junk", [P, DI])
        ld = [st.sem("ld0"), st.sem("ld1")]
        tri_ok, cb_mm, cb_ok = st.sem("tri_ok"), st.sem("cb_mm"), st.sem("cb_ok")
        seg_ok, seg_mm, ex_ok, wt_ok = st.sem("seg_ok"), st.sem("seg_mm"), st.sem("ex_ok"), st.sem("wt_ok")
        yd_mm, off_mm, t_ok, u_ok = st.sem("yd_mm"), st.sem("off_mm"), st.sem("t_ok"), st.sem("u_ok")
        p_ok, y_ok, gt_ok, sq_ok = st.sem("p_ok"), st.sem("y_ok"), st.sem("gt_ok"), st.sem("sq_ok")
        y_out = [st.sem("y_out0"), st.sem("y_out1")]
        PS = g.PS

        def heads(ap):
            return ap.rearrange("p (h c) -> p h c", c=HD)

        def at(t, d, b, grp, h0=0, h1=SH):
            return (t[:, d, bass.ds(b, 1), h0:h1] if grp else t[:, d, 0:1, h0:h1]).squeeze(1)

        with nc.Block(no_gpsimd_drain=True) as block:
            @block.sync
            def _(sp):
                def body(n, u, b, grp):
                    rows = bass.ds(b * P, P) if grp else slice(0, P)
                    if u == 0:
                        sp.wait_ge(gt_ok, n)
                    else:
                        sp.wait_ge(gt_ok, n - 1)
                    sp.dma_start(bT[:, u], g.bT.rearrange("(k p) t -> p k t", p=P)[:, :, rows]).then_inc(ld[u], 16)
                    sp.dma_start(cT[:, u], g.cT.rearrange("(k p) t -> p k t", p=P)[:, :, rows]).then_inc(ld[u], 16)
                    sp.dma_start(x[:, u], g.xs[rows, :]).then_inc(ld[u], 16)
                    for d in range(2):
                        src = g.hin[d, bass.ds(b, 1)].squeeze(0) if grp else g.hin[d, 0]
                        sp.dma_start(hin[:, u, d], src).then_inc(ld[u], 16)
                    sp.dma_start(z[:, u], g.z[rows, :]).then_inc(ld[u], 16)
                block_loop(sp, body)

            def loaded(eng, n, u):
                wait_alone(eng, ld[u], 48 * n + 96 - 48 * u)

            @block.tensor
            def _(pe):
                pe.wait_ge(tri_ok, 2)

                def body(n, u, b, grp):
                    loaded(pe, n, u)
                    pe.wait_ge(cb_ok, 2 * n)
                    for k in range(SG):
                        last = pe.matmul(PS[:, 0, P * k:P * k + P], bT[:, u, k], cT[:, u, k], start=True, stop=True)
                    last.then_inc(cb_mm, 1)

                    def segments(k):
                        for d in range(2):
                            c = 8 * n + 2 * k + d
                            pe.wait_ge(seg_ok, c + 1)
                            if k or d:
                                pe.wait_ge(ex_ok, c - 1)
                            else:
                                pe.wait_ge(ex_ok, 8 * n)
                            for half in range(2):
                                last = pe.matmul(PS[:, 1 + 2 * d + half, :], tri[:, d],
                                                 seg[:, d, 4 * half:4 * half + 4].rearrange("p h i -> p (h i)"), start=True, stop=True)
                            last.then_inc(seg_mm, 1)

                    segments(0)
                    for k in range(SG):
                        if k + 1 < SG:
                            segments(k + 1)
                        pe.wait_ge(t_ok, 12 * n + 3 * k)
                        for d in range(2):
                            last = pe.matmul(PS[:, 6 + d, :], cT[:, u, k], hin[:, u, d, 512 * k:512 * k + 512], start=True, stop=True)
                        last.then_inc(off_mm, 1)
                        pe.wait_ge(wt_ok, 8 * n + 2 * k + 2)
                        for h in range(HPG):
                            for d in range(2):
                                c0 = 512 * k + HD * h
                                last = pe.matmul(PS[:, 5, HD * h:HD * h + HD], wt[:, d, h], x[:, u, c0:c0 + HD],
                                                 start=(d == 0), stop=(d == 1))
                        last.then_inc(yd_mm, 1)
                block_loop(pe, body)

            @block.gpsimd
            def _(pool):
                pool.affine_select(out=tri[:, 0], in_=g.ones[:], compare_op=ALU.is_gt, fill=0.0, base=0,
                                   pattern=[[-1, P]], channel_multiplier=1).then_inc(tri_ok, 1)
                pool.affine_select(out=tri[:, 1], in_=g.ones[:], compare_op=ALU.is_gt, fill=0.0, base=0,
                                   pattern=[[1, P]], channel_multiplier=-1).then_inc(tri_ok, 1)

                def body(n, u, b, grp):
                    def build(k):
                        for d in range(2):
                            c = 8 * n + 2 * k + d
                            if k:
                                pool.wait_ge(seg_mm, c - 1)
                            else:
                                pool.wait_ge(seg_mm, 8 * n)
                            pool.tensor_tensor(seg[:, d], (g.upper, g.lower)[d][:].unsqueeze(1).to_broadcast([P, HPG, P]),
                                               at(q.da, d, b, grp, HPG * k, HPG * k + HPG).unsqueeze(2).to_broadcast([P, HPG, P]),
                                               ALU.mult).then_inc(seg_ok, 1)

                    def finish(k):
                        c = 4 * n + k
                        if k == 0:
                            loaded(pool, n, u)
                            pool.wait_ge(y_out[u], 8 * n if u == 0 else 8 * n - 8)
                        cs = slice(512 * k, 512 * k + 512)
                        pool.wait_ge(y_ok, c)
                        pool.tensor_tensor(heads(t3[:]), heads(x[:, u, cs]),
                                           q.skip[:, HPG * k:HPG * k + HPG].unsqueeze(2).to_broadcast([P, HPG, HD]),
                                           ALU.mult).then_inc(p_ok, 1)
                        pool.wait_ge(p_ok, 2 * c + 1)
                        pool.wait_ge(t_ok, 3 * c + 3)
                        pool.tensor_tensor(t3[:], t3[:], t2[:], ALU.add).then_inc(p_ok, 1)
                        pool.wait_ge(p_ok, 2 * c + 2)
                        pool.tensor_tensor(y[:, u, cs], t3[:], t1[:], ALU.add).then_inc(y_ok, 1)

                    build(0)
                    for k in range(SG):
                        if k + 1 < SG:
                            build(k + 1)
                        finish(k)
                block_loop(pool, body)

            @block.scalar
            def _(act):
                def body(n, u, b, grp):
                    for k in range(SG):
                        for d in range(2):
                            c = 8 * n + 2 * k + d
                            act.wait_ge(seg_mm, c + 1)
                            if k:
                                act.wait_ge(wt_ok, c - 1)
                            else:
                                act.wait_ge(wt_ok, 8 * n)
                            act.activation(ex[:, d].rearrange("p (b h) i -> p b (h i)", b=2), PS[:, 1 + 2 * d:3 + 2 * d, :],
                                           ACT.Exp).then_inc(ex_ok, 1)
                    act.wait_ge(gt_ok, n + 1)
                    act.wait_ge(sq_ok, n)
                    act.activation(junk[:], y[:, u], ACT.Square,
                                   accum_out=q.ssq[:, bass.ds(b, 1)] if grp else q.ssq[:, 0:1]).then_inc(sq_ok, 1)
                    rows = bass.ds(b * P, P) if grp else slice(0, P)
                    act.dma_start(g.y[rows, :], y[:, u]).then_inc(y_out[u], 16)
                block_loop(act, body)
                act.wait_ge(y_out[0], 16 * 5)
                act.wait_ge(y_out[1], 16 * 4)

            @block.vector
            def _(dve):
                def body(n, u, b, grp):
                    dve.wait_ge(cb_mm, n + 1)
                    dve.wait_ge(yd_mm, 4 * n)
                    for d in range(2):
                        dve.tensor_tensor(cb[:, d], PS[:, 0, :].rearrange("p (k i) -> p k i", k=SG),
                                          (g.upper, g.lower)[d][:].unsqueeze(1).to_broadcast([P, SG, P]), ALU.mult).then_inc(cb_ok, 1)
                    dve.wait_ge(cb_ok, 2 * n + 2)

                    def weights(k):
                        for d in range(2):
                            c = 8 * n + 2 * k + d
                            dve.wait_ge(ex_ok, c + 1)
                            dve.wait_ge(yd_mm, 4 * n + k)
                            for h in range(HPG):
                                hh = HPG * k + h
                                last = dve.scalar_tensor_tensor(out=wt[:, d, h], in0=ex[:, d, h],
                                                                scalar=at(q.dt, d, b, grp, hh, hh + 1), in1=cb[:, d, k],
                                                                op0=ALU.mult, op1=ALU.mult)
                            last.then_inc(wt_ok, 1)

                    def parts(k):
                        c = 4 * n + k
                        dve.wait_ge(off_mm, c + 1)
                        dve.wait_ge(y_ok, c)
                        for d, t in ((0, t1), (1, t2)):
                            dve.tensor_tensor(heads(t[:]), heads(PS[:, 6 + d, :]),
                                              at(q.grow, d, b, grp, HPG * k, HPG * k + HPG).unsqueeze(2).to_broadcast([P, HPG, HD]),
                                              ALU.mult).then_inc(t_ok, 1)
                        dve.wait_ge(yd_mm, c + 1)
                        dve.wait_ge(t_ok, 3 * c + 2)
                        dve.tensor_tensor(t1[:], t1[:], PS[:, 5, :], ALU.add).then_inc(t_ok, 1)

                    for k in range(SG):
                        weights(k)
                        parts(k)
                    dve.wait_ge(y_ok, 4 * n + 4)
                    dve.tensor_tensor(y[:, u], y[:, u], z[:, u], ALU.mult).then_inc(gt_ok, 1)
                block_loop(dve, body)


def ssm_out(nc, g, io, q):
    def take(st, mm):
        KI = DI // P
        y = st.sb("y", [P, 2, DI])
        yT = st.sb("yT", [P, 2, KI, P])
        root = st.sb("root", [P, NB])
        rstd = st.sb("rstd", [P, NB])
        ms_ok, root_ok, rstd_ok = st.sem("ms_ok"), st.sem("root_ok"), st.sem("rstd_ok")
        y_in = [st.sem("y_in0"), st.sem("y_in1")]
        yn_ok, tp, ya_ok, yT_ok = st.sem("yn_ok"), st.sem("tp"), st.sem("ya_ok"), st.sem("yT_ok")
        PS = g.PS

        def sync(sp, n, u, b, grp):
            rows = bass.ds(b * P, P) if grp else slice(0, P)
            if u == 0:
                sp.wait_ge(tp, 2 * n)
            else:
                sp.wait_ge(tp, 2 * n - 2)
            sp.dma_start(y[:, u], g.y[rows, :]).then_inc(y_in[u], 16)

        def scalar(act, n, u, b, grp):
            act.wait_ge(rstd_ok, 1)
            act.wait_ge(y_in[u], 8 * n + 16 - 8 * u)
            sc = rstd[:, bass.ds(b, 1)] if grp else rstd[:, 0:1]
            act.activation(y[:, u], y[:, u], ACT.Copy, scale=sc).then_inc(yn_ok, 1)
            act.wait_ge(tp, 2 * n + 2)
            act.wait_ge(mm, n if u == 0 else n - 1)
            for k in range(KI // 2, KI):
                last = act.activation(yT[:, u, k], PS[:, 4 + k // 4, P * (k % 4):P * (k % 4) + P], ACT.Copy,
                                      scale=g.vcol[:, V_SG + k:V_SG + k + 1])
            last.then_inc(ya_ok, 1)

        def tensor(pe, n, u, b, grp):
            wait_alone(pe, yn_ok, n + 1)
            pe.wait_ge(yT_ok, n)
            for k in range(KI):
                last = pe.transpose(PS[:, 4 + k // 4, P * (k % 4):P * (k % 4) + P], y[:, u, P * k:P * k + P], g.ident[:])
                if k % 8 == 7:
                    last.then_inc(tp, 1)

        def vector(dve, n, u, b, grp):
            dve.wait_ge(tp, 2 * n + 1)
            dve.wait_ge(mm, n if u == 0 else n - 1)
            for k in range(KI // 2):
                last = dve.tensor_scalar(yT[:, u, k], PS[:, 4 + k // 4, P * (k % 4):P * (k % 4) + P],
                                         g.vcol[:, V_SG + k:V_SG + k + 1], None, ALU.mult)
            last.then_inc(ms_ok, 1)
            dve.wait_ge(ms_ok, n + 2)
            dve.wait_ge(ya_ok, n + 1)
            dve.sem_inc(yT_ok, 1)

        def before_vector(dve):
            dve.tensor_scalar(q.ssq[:], q.ssq[:], 1.0 / DI, EPS, ALU.mult, ALU.add).then_inc(ms_ok, 1)
            dve.wait_ge(root_ok, 1)
            dve.reciprocal(rstd[:], root[:]).then_inc(rstd_ok, 1)

        def before_scalar(act):
            act.wait_ge(ms_ok, 1)
            act.activation(root[:], q.ssq[:], ACT.Sqrt).then_inc(root_ok, 1)
        return yT, yT_ok, {"sync": sync, "scalar": scalar, "tensor": tensor, "vector": vector,
                           "before_vector": before_vector, "before_scalar": before_scalar}
    project_out(nc, g, "wout", 1, DI // P, io["ssm_w_out"][0], take)


def final_norm(nc, g, io):
    with Stage(nc, "final") as st:
        x = st.sb("x", [P, NB, D])
        junk = st.sb("junk", [P, D])
        gain = st.sb("gain", [P, D])
        ssq = st.sb("ssq", [P, NB])
        root = st.sb("root", [P, NB])
        x_in, sq, ms, rt, rs = st.sem("x_in"), st.sem("sq"), st.sem("ms"), st.sem("rt"), st.sem("rs")
        y_ok, y_out = st.sem("y_ok"), st.sem("y_out")
        with nc.Block(no_gpsimd_drain=True) as block:
            @block.sync
            def _(sp):
                sp.dma_start(x[:], g.res.rearrange("(b p) d -> p b d", p=P)).then_inc(x_in, 16)
                sp.dma_start(gain[:], io["final_norm_g"].partition_broadcast(P)).then_inc(x_in, 16)
                sp.wait_ge(y_ok, 1)
                sp.dma_start(io["y_prompt"][0], x[:, 0]).then_inc(y_out, 16)
                for b in range(1, NB):
                    sp.wait_ge(y_ok, b + 1)
                    sp.dma_start(io["y_sample"][0, P * (b - 1):P * b], x[:, b]).then_inc(y_out, 16)
                sp.wait_ge(y_out, 16 * NB)

            @block.scalar
            def _(act):
                act.wait_ge(x_in, 32)
                for b in range(NB):
                    if b:
                        act.wait_ge(sq, b)
                    act.activation(junk[:], x[:, b], ACT.Square, accum_out=ssq[:, b:b + 1]).then_inc(sq, 1)
                act.wait_ge(ms, 1)
                act.activation(root[:], ssq[:], ACT.Sqrt).then_inc(rt, 1)

            @block.vector
            def _(dve):
                dve.wait_ge(sq, NB)
                dve.tensor_scalar(ssq[:], ssq[:], 1.0 / D, EPS, ALU.mult, ALU.add).then_inc(ms, 1)
                dve.wait_ge(rt, 1)
                dve.reciprocal(root[:], root[:]).then_inc(rs, 1)
                dve.wait_ge(rs, 1)
                for b in range(NB):
                    dve.scalar_tensor_tensor(out=x[:, b], in0=x[:, b], scalar=root[:, b:b + 1], in1=gain[:],
                                             op0=ALU.mult, op1=ALU.mult).then_inc(y_ok, 1)


class Shared:
    pass


def build(nc, io):
    g = Shared()
    ctx = ExitStack()
    with ctx:
        def sb(name, shape, dt=F32):
            return ctx.enter_context(nc.sbuf_tensor(name, shape, dt))
        g.PS = ctx.enter_context(nc.psum_tensor("banks", [P, 8, 512], F32))
        g.ident = sb("ident", [P, P])
        g.ones = sb("ones", [P, P])
        g.fold = sb("fold", [P, P])
        g.upper = sb("upper", [P, P])
        g.lower = sb("lower", [P, P])
        g.vcol = sb("vcol", [P, V_ALL])
        g.convw = sb("convw", [P, 3, MC])
        g.modc = sb("modc", [P, DEPTH, 48, 2])
        g.gain = sb("gain", [P, DEPTH, 2, KD, NB])
        g.shift = sb("shift", [P, DEPTH, 2, KD, NB])
        g.gate_row = sb("gate_row", [P, 2, D])
        g.gate_bias = sb("gate_bias", [P, DEPTH, D])
        g.cond = sb("cond", [P, KD, 2])
        g.bcol = sb("bcol", [P, 96])
        g.aff = sb("aff", [NE, T])
        g.row_s = sb("row_s", [P, NE], U32)
        g.row_p = sb("row_p", [CAP_P, NE], U32)
        g.gate_s = sb("gate_s", [P, NE])
        g.gate_p = sb("gate_p", [CAP_P, NE])
        g.res = nc.dram_tensor("res", [T, D], F32, kind="Internal").ap()
        g.normed = nc.dram_tensor("normed", [T, D], F32, kind="Internal").ap()
        g.z, g.xs, g.y, g.btok, g.bT, g.cT, g.hin = (
            nc.dram_tensor("d_" + name, shape, F32, kind="Internal").ap()
            for name, shape in (("z", [T, DI]), ("xs", [T, DI]), ("y", [T, DI]), ("btok", [T, GN]),
                                ("bT", [GN, T]), ("cT", [GN, T]), ("hin", [2, NB, P, DI])))

        start(nc, g, io)
        m = Shared()
        with ExitStack() as c:
            def mb(name, shape):
                return c.enter_context(nc.sbuf_tensor(name, shape, F32))
            m.oT = mb("oT", [P, HEADS, T])
            m.qlat = mb("qlat", [P, KQ, T])
            m.ckv = mb("ckv", [P, KKV, KEYS])
            m.k2 = mb("k2", [P, KEYS])
            m.rope = mb("rope", [P, T])
            with nc.sbuf_tensor("hT0", [P, KD, T], F32) as hT:
                norm(nc, g, io, 0, 0, hT)
                mla_project(nc, g, io, hT, m)
            mla_heads(nc, g, io, m)
            mla_out(nc, g, io, m)
        norm(nc, g, io, 0, 1)
        choose(nc, g, io, 0)
        experts(nc, g, io, 0)
        q = Shared()
        with ExitStack() as c:
            def qb(name, shape):
                return c.enter_context(nc.sbuf_tensor(name, shape, F32))
            q.dt, q.da, q.grow, q.toend, q.dec = (qb("q" + n, [P, 2, NB, SH]) for n in ("dt", "da", "grow", "toend", "dec"))
            q.skip = qb("qskip", [P, SH])
            q.ssq = qb("qssq", [P, NB])
            with nc.sbuf_tensor("hT1", [P, KD, T], F32) as hT:
                norm(nc, g, io, 1, 0, hT)
                ssm_gate_and_steps(nc, g, io, hT, q)
                ssm_conv(nc, g, io, hT)
            ssm_states(nc, g, io, q)
            ssm_outputs(nc, g, io, q)
            ssm_out(nc, g, io, q)
        norm(nc, g, io, 1, 1)
        choose(nc, g, io, 1)
        experts(nc, g, io, 1)
        final_norm(nc, g, io)


_INS = ["x_prompt", "x_sample", "cache_ckv", "cache_krope", "state_ssm", "c", "c_ctx", "w_mod", "b_mod", "norm1_g",
        "norm2_g", "final_norm_g", "mla_w_dq", "mla_q_norm_g", "mla_w_uq", "mla_w_dkv", "mla_kv_norm_g", "mla_w_ukv",
        "mla_w_o", "ssm_w_in", "ssm_conv_w", "ssm_conv_b", "ssm_dt_bias", "ssm_a_log", "ssm_d_skip", "ssm_norm_g",
        "ssm_w_out", "moe_w_router", "moe_w_gate", "moe_w_up", "moe_w_down"]
_OUTS = [("y_prompt", (1, SEQ, D)), ("y_sample", (1, DEC, D)), ("new_ckv", (1, 1, SEQ, KVR)),
         ("new_krope", (1, 1, SEQ, ROPE)), ("new_ssm", (1, 1, 2, SH, HD, NS))]


def rope_table():
    rows = DEC // GRID_W
    row = np.repeat(np.arange(rows), GRID_W).astype(np.float32)
    col = np.tile(np.arange(GRID_W), rows).astype(np.float32)
    pairs = ROPE // 4
    inv = np.float32(THETA) ** (-np.arange(pairs, dtype=np.float32) / np.float32(pairs))
    ang = np.concatenate([row[:, None] * inv, col[:, None] * inv], axis=-1).astype(np.float32)
    tab = np.zeros((P, T), np.float32)
    tab[0:ROPE, 0:SEQ] = 1.0
    cos, sin = np.cos(ang).T, np.sin(ang).T
    tab[:, SEQ:] = np.concatenate([cos, cos, -sin, sin], axis=0)
    return tab


def kernel(**inputs):
    import numpy as _np
    import concourse.bacc as _bacc
    from concourse.bass_utils import run_bass_kernel_spmd as _run

    nc = _bacc.Bacc("TRN2", target_bir_lowering=False, num_devices=1)
    drams, arrays = {}, {}
    for name in _INS:
        a = _np.ascontiguousarray(inputs[name])
        arrays["in_" + name] = a
        drams[name] = nc.dram_tensor("in_" + name, a.shape, F32, kind="ExternalInput").ap()
    tab = rope_table()
    arrays["in_rope"] = tab
    drams["rope"] = nc.dram_tensor("in_rope", tab.shape, F32, kind="ExternalInput").ap()
    for name, shape in _OUTS:
        drams[name] = nc.dram_tensor("out_" + name, shape, F32, kind="ExternalOutput").ap()
    build(nc, drams)
    r = _run(nc, [arrays], core_ids=[0])
    return tuple(r.results[0]["out_" + name] for name, _ in _OUTS)
```

```python
from contextlib import ExitStack

import numpy as np

import concourse.bass as bass
from concourse import mybir

F32 = mybir.dt.float32
F32R = mybir.dt.float32r
U32 = mybir.dt.uint32
ACT = mybir.ActivationFunctionType
ALU = mybir.AluOpType
X = mybir.AxisListType.X

P = 128
D = 1024
KD = D // P
SEQ, DEC = 128, 1024
T = SEQ + DEC
NB = T // P
TILE = 384
NT = T // TILE
DEPTH = 2
EPS = 1e-6
HEADS, NOPE, ROPE, VD = 8, 128, 64, 128
QR, KVR = 384, 256
KQ, KKV = QR // P, KVR // P
PAST = 128
KEYS = T + PAST
SAMPLE_KEYS = PAST + DEC
SCALE = (NOPE + ROPE) ** -0.5
GRID_W = 64
THETA = 10000.0
DI = 2048
HD = 64
SH = DI // HD
SG = 4
NS = 128
HPG = SH // SG
GN = SG * NS
CONV = DI + 2 * GN
MC = CONV // P
IN_DIM = DI + CONV + 2 * SH
NE = 16
FF = 1024
CAP_S = 2 * DEC // NE
CAP_P = 2 * SEQ // NE
CAP = CAP_S + CAP_P
V_N1, V_N2, V_CTX, V_C, V_QG, V_KVG, V_SG, V_CB = 0, 16, 32, 40, 48, 51, 53, 69
V_ALL = V_CB + MC


class Steps:

    def __init__(self, eng, sem, turn=0, per_turn=0, before=0):
        self.eng, self.sem, self.base, self.n = eng, sem, turn * per_turn + before, 0

    def did(self, ins):
        ins.then_inc(self.sem, 1)
        self.n += 1

    def settle(self):
        self.eng.wait_ge(self.sem, self.base + self.n)

    def alone(self, ins):
        self.did(ins)
        self.settle()


def wait_alone(eng, sem, value):
    eng.wait_ge(sem, value)
    eng.nop(nofuse=True)


def exact_products(pe, out, left, right, first=True, last=True):
    (lh, ll), (rh, rl) = left, right
    pe.matmul(out, lh, rh, start=first, stop=False)
    pe.matmul(out, lh, rl, start=False, stop=False)
    return pe.matmul(out, ll, rh, start=False, stop=last)


class Stage:

    def __init__(self, nc, name):
        self.nc, self.name = nc, name
        self.ctx = ExitStack()
        self.sems = []

    def __enter__(self):
        return self

    def sb(self, name, shape, dt=F32):
        return self.ctx.enter_context(self.nc.sbuf_tensor(f"{self.name}_{name}", shape, dt))

    def sem(self, name):
        s = self.nc.alloc_semaphore(f"{self.name}_{name}")
        self.sems.append(s)
        return s

    def __exit__(self, *e):
        if e[0] is None:
            self.nc.clear_and_free_semaphores(self.sems)
            self.nc.all_engine_barrier()
        self.ctx.__exit__(*e)


def bcast_rows(ap, n):
    return ap.partition_broadcast(n)


class Modulation:

    CH = 6 * D // 512

    def __init__(self, st, g, io, l):
        self.g, self.io, self.l = g, io, l
        self.w = st.sb("m_w", [P, 4, KD, 512])
        self.row = st.sb("m_row", [2, 4, 512])
        self.rows = st.sb("m_rows", [2, 6 * D])
        self.sel = st.sb("m_sel", [2, 2, P])
        self.w_in = [st.sem(f"m_w_in{i}") for i in range(4)]
        self.row_mm, self.row_ok = st.sem("m_row_mm"), st.sem("m_row_ok")
        self.col_mm, self.col_ok = st.sem("m_col_mm"), st.sem("m_col_ok")
        self.sel_ok, self.gate_mm, self.done = st.sem("m_sel_ok"), st.sem("m_gate_mm"), st.sem("m_done")

    def sync(self, sp):
        def load(u, c0):
            sp.dma_start(self.w[:, u], self.io["w_mod"][self.l].rearrange("(k p) n -> p k n", p=P)[
                :, :, bass.ds(c0 + u * 512, 512)]).then_inc(self.w_in[u], 16)

        for u in range(4):
            load(u, 0)
        with sp.Fori(1, self.CH // 4) as i:
            for u in range(4):
                sp.wait_ge(self.row_mm, 4 * i + u - 3)
                load(u, 2048 * i)

    def tensor(self, pe):
        PS, g = self.g.PS, self.g

        def columns(i, u):
            pe.wait_ge(self.row_ok, 4 * i + u + 1)
            wait_alone(pe, self.col_ok, 4 * i + max(0, u - 1))
            for m in range(4):
                last = pe.transpose(PS[:, 3 + u % 2, 2 * m:2 * m + 2], self.row[:, u, P * m:P * m + P], g.ident[0:2, 0:2])
            last.then_inc(self.col_mm, 1)

        with pe.Fori(0, self.CH // 4) as i:
            for u in range(4):
                pe.wait_ge(self.w_in[u], 16 * i + 16)
                pe.wait_ge(self.row_ok, 4 * i + max(0, u - 1))
                for k in range(KD):
                    last = pe.matmul(PS[0:2, 1 + u % 2, :], g.cond[:, k, :], self.w[:, u, k, :], start=(k == 0), stop=(k == KD - 1))
                last.then_inc(self.row_mm, 1)
                if u:
                    columns(i, u - 1)
            columns(i, 3)
        pe.wait_ge(self.sel_ok, 1)
        pe.wait_ge(self.row_ok, self.CH)
        pe.wait_ge(self.col_ok, self.CH)
        for j in range(2):
            for half in range(2):
                c0 = 2 * D + 512 * half
                pe.matmul(PS[:, 1 + 2 * j + half, :], self.sel[:, j], self.rows[:, c0:c0 + 512], start=True,
                          stop=True).then_inc(self.gate_mm, 1)

    def scalar(self, act):
        PS, g, l = self.g.PS, self.g, self.l

        def rows(i, u):
            act.wait_ge(self.row_mm, 4 * i + u + 1)
            act.wait_ge(self.col_mm, 4 * i)
            act.copy(self.rows[:, bass.ds(2048 * i + 512 * u, 512)], PS[0:2, 1 + u % 2, :])
            act.copy(self.row[:, u], PS[0:2, 1 + u % 2, :]).then_inc(self.row_ok, 1)

        def columns(i, u):
            act.wait_ge(self.col_mm, 4 * i + u + 1)
            for m in range(4):
                n = 16 * i + 4 * u + m
                last = act.activation(g.modc[:, l, bass.ds(n, 1), :].squeeze(1), PS[:, 3 + u % 2, 2 * m:2 * m + 2], ACT.Identity,
                                      bias=g.bcol[:, bass.ds(n + 48 * l, 1)])
            last.then_inc(self.col_ok, 1)

        with act.Fori(0, self.CH // 4) as i:
            for u in range(4):
                rows(i, u)
                if u:
                    columns(i, u - 1)
            columns(i, 3)

    def vector(self, dve):
        PS, g, l = self.g.PS, self.g, self.l
        dve.tensor_copy(self.sel[:], g.ident[0:2, 0:2].unsqueeze(2).to_broadcast([2, 2, P])).then_inc(self.sel_ok, 1)
        dve.wait_ge(self.col_ok, self.CH)
        for w, at in ((0, V_N1), (1, V_N2)):
            for b0, b1, j in ((0, 1, 0), (1, NB, 1)):
                m0, nb = 24 * w, b1 - b0
                dve.scalar_tensor_tensor(
                    out=g.gain[:, l, w, :, b0:b1],
                    in0=g.modc[:, l, m0 + 8:m0 + 16, j:j + 1].to_broadcast([P, KD, nb]), scalar=1.0,
                    in1=g.vcol[:, at + 8 * l:at + 8 * l + 8].unsqueeze(2).to_broadcast([P, KD, nb]),
                    op0=ALU.add, op1=ALU.mult).then_inc(self.done, 1)
                dve.tensor_copy(g.shift[:, l, w, :, b0:b1],
                                g.modc[:, l, m0:m0 + 8, j:j + 1].to_broadcast([P, KD, nb])).then_inc(self.done, 1)
        for n in range(4):
            dve.wait_ge(self.gate_mm, n + 1)
            c0 = 512 * (n % 2)
            dve.tensor_tensor(g.gate_row[:, n // 2, c0:c0 + 512], PS[:, 1 + n, :], g.gate_bias[:, l, c0:c0 + 512],
                              ALU.add).then_inc(self.done, 1)


def start(nc, g, io):
    with Stage(nc, "start") as st:
        rows_a = st.sb("rows_a", [2 * 48, P])
        rows_b = st.sb("rows_b", [V_ALL, P])
        rows_c = st.sb("rows_c", [MC, 3 * P])
        small, copied, made = st.sem("small"), st.sem("copied"), st.sem("made")
        turned, cols, cond_ok = st.sem("turned"), st.sem("cols"), st.sem("cond_ok")
        mod = Modulation(st, g, io, 0)
        PS = g.PS

        with nc.Block(no_gpsimd_drain=True) as block:
            @block.sync
            def _(sp):
                mod.sync(sp)

            @block.scalar
            def _(act):
                act.dma_start(rows_a[:], io["b_mod"].rearrange("l (m p) -> (l m) p", p=P)).then_inc(small, 16)
                for at, name in ((V_N1, "norm1_g"), (V_N2, "norm2_g"), (V_C, "c"), (V_QG, "mla_q_norm_g"),
                                 (V_KVG, "mla_kv_norm_g"), (V_SG, "ssm_norm_g"), (V_CB, "ssm_conv_b")):
                    rows = io[name].rearrange("l (m p) -> (l m) p", p=P)
                    act.dma_start(rows_b[at:at + rows.shape[0], :], rows).then_inc(small, 16)
                act.dma_start(rows_b[V_CTX:V_CTX + KD, :], io["c_ctx"].rearrange("(m p) -> m p", p=P)).then_inc(small, 16)
                act.dma_start(rows_c[:], io["ssm_conv_w"][0].rearrange("(m p) j -> m (p j)", p=P)).then_inc(small, 16)
                for l in range(DEPTH):
                    act.dma_start(g.gate_bias[:, l], io["b_mod"][l, 2 * D:3 * D].partition_broadcast(P)).then_inc(copied, 16)
                act.dma_start(g.res[0:SEQ, :], io["x_prompt"][0]).then_inc(copied, 16)
                act.dma_start(g.res[SEQ:T, :], io["x_sample"][0]).then_inc(copied, 16)
                act.wait_ge(cols, 5)
                act.activation(g.cond[:, :, 0], g.vcol[:, V_CTX:V_CTX + KD], ACT.Silu).then_inc(cond_ok, 1)
                act.activation(g.cond[:, :, 1], g.vcol[:, V_C:V_C + KD], ACT.Silu).then_inc(cond_ok, 1)
                mod.scalar(act)
                act.wait_ge(copied, 64)

            @block.gpsimd
            def _(pool):
                pool.memset(g.ident[:], 0.0).then_inc(made, 1)
                pool.memset(g.ones[:], 1.0).then_inc(made, 1)
                pool.wait_ge(made, 2)
                pool.affine_select(out=g.ident[:], in_=g.ident[:], compare_op=ALU.not_equal, fill=1.0, base=0,
                                   pattern=[[-1, P]], channel_multiplier=1).then_inc(made, 1)
                pool.memset(g.fold[:], 0.0).then_inc(made, 1)
                for n, base in enumerate((0, 64, -64)):
                    pool.wait_ge(made, 4 + n)
                    pool.affine_select(out=g.fold[:], in_=g.fold[:], compare_op=ALU.not_equal, fill=1.0, base=base,
                                       pattern=[[-1, P]], channel_multiplier=1).then_inc(made, 1)
                pool.affine_select(out=g.upper[:], in_=g.ones[:], compare_op=ALU.is_ge, fill=0.0, base=0,
                                   pattern=[[1, P]], channel_multiplier=-1).then_inc(made, 1)
                pool.affine_select(out=g.lower[:], in_=g.ones[:], compare_op=ALU.is_ge, fill=0.0, base=0,
                                   pattern=[[-1, P]], channel_multiplier=1).then_inc(made, 1)

            @block.tensor
            def _(pe):
                pe.wait_ge(small, 16 * 10)
                pe.wait_ge(made, 3)
                pe.transpose(PS[:, 0, 0:96], rows_a[:], g.ident[0:96, 0:96]).then_inc(turned, 1)
                pe.transpose(PS[:, 1, 0:V_ALL], rows_b[:], g.ident[0:V_ALL, 0:V_ALL]).then_inc(turned, 1)
                for j in range(3):
                    pe.transpose(PS[:, 2 + j, 0:MC], rows_c[:, j:3 * P:3], g.ident[0:MC, 0:MC]).then_inc(turned, 1)
                pe.wait_ge(cols, 5)
                pe.wait_ge(cond_ok, 2)
                mod.tensor(pe)

            @block.vector
            def _(dve):
                dve.wait_ge(turned, 5)
                dve.tensor_copy(g.bcol[:], PS[:, 0, 0:96]).then_inc(cols, 1)
                dve.tensor_copy(g.vcol[:], PS[:, 1, 0:V_ALL]).then_inc(cols, 1)
                for j in range(3):
                    dve.tensor_copy(g.convw[:, j, :], PS[:, 2 + j, 0:MC]).then_inc(cols, 1)
                dve.wait_ge(made, 3)
                dve.wait_ge(copied, 64)
                mod.vector(dve)


def norm(nc, g, io, layer, which, hT=None):
    with Stage(nc, f"norm{layer}{which}") as st:
        x = st.sb("x", [P, NB, D])
        junk = st.sb("junk", [P, D])
        ssq = st.sb("ssq", [P, NB])
        root = st.sb("root", [P, NB])
        rstd = st.sb("rstd", [P, NB])
        xn = st.sb("xn", [P, 3, D])
        x_in = st.sem("x_in")
        sq = st.sem("sq")
        ms = st.sem("ms")
        rt = st.sem("rt")
        rs = st.sem("rs")
        xn_ok = st.sem("xn_ok")
        turned = st.sem("turned")
        ev_a = st.sem("ev_a")
        ev_d = st.sem("ev_d")
        PS = g.PS
        router = which == 1
        split = isinstance(hT, tuple)
        if router or split:
            hs = st.sb("hs", [P, 3, KD, P])
        if split:
            hi_ok, lo_ok = st.sem("hi_ok"), st.sem("lo_ok")
        if router:
            wr = st.sb("wr", [P, KD, NE])
            mx = st.sb("mx", [P, 3])
            ex = st.sb("ex", [P, 3, NE])
            tot = st.sb("tot", [P, 3])
            inv = st.sb("inv", [P, 3])
            pr = st.sb("pr", [P, 3, NE])
            wr_in = st.sem("wr_in")
            saved = [st.sem(f"saved{u}") for u in range(3)]
            lg = st.sem("lg")
            less = st.sb("less", [P, 3, NE])
            less_ok = st.sem("less_ok")
            ex_ok = st.sem("ex_ok")
            chain = st.sem("chain")
            pr_ok = st.sem("pr_ok")
            pt = st.sem("pt")
            af = st.sem("af")

        def h_out(u, i, k0, k1):
            if router or split:
                return hs[:, u, k0:k1, :]
            return hT[:, k0:k1, bass.ds(i * 3 * P + u * P, P)]

        with nc.Block(no_gpsimd_drain=True) as block:
            @block.sync
            def _(sp):
                sp.dma_start(x[:], g.res.rearrange("(b p) d -> p b d", p=P)).then_inc(x_in, 16)
                if router:
                    sp.dma_start(wr[:], io["moe_w_router"][layer].rearrange("(k p) e -> p k e", p=P)).then_inc(wr_in, 16)
                    with sp.Fori(0, 3) as i:
                        for u in range(3):
                            sp.wait_ge(xn_ok, 3 * i + u + 1)
                            sp.dma_start(g.normed[bass.ds(i * 3 * P + u * P, P), :], xn[:, u]).then_inc(saved[u], 16)
                    for u in range(3):
                        sp.wait_ge(saved[u], 48)

            @block.scalar
            def _(act):
                act.wait_ge(x_in, 16)
                for b in range(NB):
                    if b:
                        act.wait_ge(sq, b)
                    act.activation(junk[:], x[:, b], ACT.Square, accum_out=ssq[:, b:b + 1]).then_inc(sq, 1)
                act.wait_ge(ms, 1)
                act.activation(root[:], ssq[:], ACT.Sqrt).then_inc(rt, 1)
                act.wait_ge(rs, 1)
                with act.Fori(0, 3) as i:
                    for u in range(3):
                        act.wait_ge(turned, 3 * i)
                        if router:
                            act.wait_ge(saved[u], 16 * i)
                        act.activation(xn[:, u], x[:, bass.ds(3 * i + u, 1), :].squeeze(1), ACT.Copy,
                                       scale=rstd[:, bass.ds(3 * i + u, 1)]).then_inc(xn_ok, 1)
                    for u in range(3):
                        act.wait_ge(turned, 3 * i + u + 1)
                        if router:
                            act.wait_ge(lg, i)
                        if split:
                            act.wait_ge(lo_ok, 3 * i)
                        for k in range(4, KD):
                            act.activation(h_out(u, i, k, k + 1).squeeze(1), PS[:, 2 * u + 1, P * (k - 4):P * (k - 3)],
                                           ACT.Identity,
                                           scale=g.gain[:, layer, which, k, bass.ds(3 * i + u, 1)],
                                           bias=g.shift[:, layer, which, k, bass.ds(3 * i + u, 1)]).then_inc(ev_a, 1)
                        if split:
                            act.wait_ge(ev_a, 12 * i + 4 * u + 4)
                            act.wait_ge(ev_d, 12 * i + 4 * u + 4)
                            act.copy(hT[0][:, :, bass.ds(i * 3 * P + u * P, P)], hs[:, u]).then_inc(hi_ok, 1)
                    if router:
                        act.wait_ge(less_ok, i + 1)
                        act.activation(ex[:], less[:], ACT.Exp).then_inc(ex_ok, 1)

            @block.vector
            def _(dve):
                dve.wait_ge(sq, NB)
                dve.tensor_scalar(ssq[:], ssq[:], 1.0 / D, EPS, ALU.mult, ALU.add).then_inc(ms, 1)
                dve.wait_ge(rt, 1)
                dve.reciprocal(rstd[:], root[:]).then_inc(rs, 1)
                with dve.Fori(0, 3) as i:
                    for u in range(3):
                        dve.wait_ge(turned, 3 * i + u + 1)
                        if router:
                            dve.wait_ge(lg, i)
                        if split:
                            dve.wait_ge(lo_ok, 3 * i)
                        for k in range(4):
                            dve.tensor_scalar(h_out(u, i, k, k + 1).squeeze(1), PS[:, 2 * u, P * k:P * k + P],
                                              g.gain[:, layer, which, k, bass.ds(3 * i + u, 1)],
                                              g.shift[:, layer, which, k, bass.ds(3 * i + u, 1)],
                                              ALU.mult, ALU.add).then_inc(ev_d, 1)
                    if router:
                        steps = Steps(dve, chain, i, 3)
                        logits = PS[:, 6, 0:3 * NE].rearrange("p (u e) -> p u e", e=NE)
                        dve.wait_ge(lg, i + 1)
                        steps.alone(dve.tensor_reduce(mx[:], logits, X, ALU.max))
                        dve.tensor_tensor(less[:], logits, mx[:].unsqueeze(2).to_broadcast([P, 3, NE]),
                                          ALU.subtract).then_inc(less_ok, 1)
                        dve.wait_ge(ex_ok, i + 1)
                        steps.alone(dve.tensor_reduce(tot[:], ex[:], X, ALU.add))
                        steps.alone(dve.reciprocal(inv[:], tot[:]))
                        dve.tensor_tensor(pr[:], ex[:], inv[:].unsqueeze(2).to_broadcast([P, 3, NE]),
                                          ALU.mult).then_inc(pr_ok, 1)
                        dve.wait_ge(pt, i + 1)
                        dve.tensor_copy(g.aff[:, bass.ds(i * 3 * P, 3 * P)], PS[0:NE, 7, 0:3 * P]).then_inc(af, 1)

            if split:
                @block.gpsimd
                def _(pool):
                    with pool.Fori(0, 3) as i:
                        for u in range(3):
                            cols = bass.ds(i * 3 * P + u * P, P)
                            pool.wait_ge(hi_ok, 3 * i + u + 1)
                            pool.tensor_tensor(hT[1][:, :, cols], hs[:, u], hT[0][:, :, cols].bitcast(F32),
                                               ALU.subtract).then_inc(lo_ok, 1)

            @block.tensor
            def _(pe):
                if router:
                    pe.wait_ge(wr_in, 16)
                with pe.Fori(0, 3) as i:
                    for u in range(3):
                        pe.wait_ge(xn_ok, 3 * i + u + 1)
                        pe.wait_ge(ev_a, 12 * i)
                        pe.wait_ge(ev_d, 12 * i)
                        for k in range(KD):
                            last = pe.transpose(PS[:, 2 * u + k // 4, P * (k % 4):P * (k % 4) + P],
                                                xn[:, u, P * k:P * k + P], g.ident[:])
                        last.then_inc(turned, 1)
                    if router:
                        for u in range(3):
                            pe.wait_ge(ev_a, 12 * i + 4 * u + 4)
                            pe.wait_ge(ev_d, 12 * i + 4 * u + 4)
                            pe.wait_ge(less_ok, i)
                            for k in range(KD):
                                last = pe.matmul(PS[:, 6, NE * u:NE * u + NE], hs[:, u, k], wr[:, k],
                                                 start=(k == 0), stop=(k == KD - 1))
                        last.then_inc(lg, 1)
                        pe.wait_ge(pr_ok, i + 1)
                        pe.wait_ge(af, i)
                        for u in range(3):
                            last = pe.transpose(PS[0:NE, 7, P * u:P * u + P], pr[:, u], g.ident[:])
                        last.then_inc(pt, 1)


def mla_project(nc, g, io, hT, m):
    with Stage(nc, "proj") as st:
        w = st.sb("w", [P, KD, QR + KVR + 2 * ROPE])
        sqr = st.sb("sqr", [P, KQ + KKV, TILE])
        root = st.sb("root", [P, 2, TILE])
        rinv = st.sb("rinv", [P, 2, TILE])
        kc = st.sb("kc", [P, TILE])
        cc = st.sb("cc", [P, KVR])
        ckr = st.sb("ckr", [P, 2 * ROPE])
        outs = st.sb("outs", [P, KVR + ROPE])
        epsc = st.sb("epsc", [P, 1])
        w_in, cache_in, eps_ok = st.sem("w_in"), st.sem("cache_in"), st.sem("eps_ok")
        prod, sq, sums, rt, rc = st.sem("prod"), st.sem("sq"), st.sem("sums"), st.sem("rt"), st.sem("rc")
        kc_ok, fold, k2_ok, lat_ok = st.sem("kc_ok"), st.sem("fold"), st.sem("k2_ok"), st.sem("lat_ok")
        tp, cache_ok, out_ok, stored = st.sem("tp"), st.sem("cache_ok"), st.sem("out_ok"), st.sem("stored")
        PS = g.PS
        NM = KQ + KKV

        def cols(i):
            return bass.ds(i * TILE, TILE)

        with nc.Block(no_gpsimd_drain=True) as block:
            @block.sync
            def _(sp):
                dkv = io["mla_w_dkv"][0].rearrange("(k p) n -> p k n", p=P)
                sp.dma_start(w[:, :, 0:QR], io["mla_w_dq"][0].rearrange("(k p) n -> p k n", p=P)).then_inc(w_in, 16)
                sp.dma_start(w[:, :, QR:QR + KVR + ROPE], dkv).then_inc(w_in, 16)
                at, h = QR + KVR + ROPE, ROPE // 2
                sp.dma_start(w[:, :, at:at + h], dkv[:, :, KVR + h:KVR + ROPE]).then_inc(w_in, 16)
                sp.dma_start(w[:, :, at + h:at + ROPE], dkv[:, :, KVR:KVR + h]).then_inc(w_in, 16)
                sp.dma_start(m.rope[:], io["rope"]).then_inc(w_in, 16)
                sp.dma_start(cc[:], io["cache_ckv"][0, 0]).then_inc(cache_in, 16)
                sp.dma_start(ckr[:, 0:ROPE], io["cache_krope"][0, 0]).then_inc(cache_in, 16)
                sp.dma_start(ckr[:, ROPE:2 * ROPE], io["cache_krope"][0, 0]).then_inc(cache_in, 16)
                sp.wait_ge(out_ok, 1)
                sp.dma_start(io["new_ckv"][0, 0], outs[:, 0:KVR]).then_inc(stored, 16)
                sp.dma_start(io["new_krope"][0, 0], outs[:, KVR:KVR + ROPE]).then_inc(stored, 16)
                sp.wait_ge(stored, 32)

            @block.tensor
            def _(pe):
                pe.wait_ge(cache_in, 48)
                for r in range(KKV):
                    pe.transpose(PS[:, 0, P * r:P * r + P], cc[:, P * r:P * r + P], g.ident[:])
                pe.transpose(PS[:, 0, P * KKV:P * KKV + P], ckr[:], g.ident[:]).then_inc(tp, 1)
                pe.wait_ge(w_in, 80)
                pe.wait_ge(cache_ok, 2)
                with pe.Fori(0, NT) as i:
                    pe.wait_ge(lat_ok, NM * i)
                    pe.wait_ge(k2_ok, i)
                    for n in range(NM + 1):
                        for k in range(KD):
                            last = pe.matmul(PS[:, n, 0:TILE], w[:, k, P * n:P * n + P], hT[:, k, cols(i)],
                                             start=(k == 0), stop=(k == KD - 1))
                        last.then_inc(prod, 1)
                    pe.wait_ge(sq, NM * i + NM)
                    for n in range(NM):
                        last = pe.matmul(PS[:, 6 + (n >= KQ), 0:TILE], g.ones[:], sqr[:, n, :],
                                         start=n in (0, KQ), stop=n in (KQ - 1, NM - 1))
                    last.then_inc(sums, 1)
                    pe.wait_ge(kc_ok, i + 1)
                    pe.matmul(PS[:, NM, 0:TILE], g.fold[:], kc[:], start=True, stop=True).then_inc(fold, 1)
                pe.wait_ge(lat_ok, NM * NT)
                pe.wait_ge(k2_ok, NT)
                for r in range(KKV):
                    pe.transpose(PS[:, 0, P * r:P * r + P], m.ckv[:, r, 0:P], g.ident[:])
                pe.transpose(PS[:, 0, P * KKV:P * KKV + ROPE], m.k2[0:ROPE, 0:P], g.ident[0:ROPE, 0:ROPE]).then_inc(tp, 1)

            @block.scalar
            def _(act):
                act.wait_ge(eps_ok, 1)
                with act.Fori(0, NT) as i:
                    act.wait_ge(sums, i)
                    for n in range(NM):
                        act.wait_ge(prod, (NM + 1) * i + n + 1)
                        act.activation(sqr[:, n, :], PS[:, n, 0:TILE], ACT.Square).then_inc(sq, 1)
                    act.wait_ge(sums, i + 1)
                    for j, width in ((0, QR), (1, KVR)):
                        act.activation(root[:, j, :], PS[:, 6 + j, 0:TILE], ACT.Sqrt, scale=1.0 / width,
                                       bias=epsc[:]).then_inc(rt, 1)

            @block.vector
            def _(dve):
                dve.memset(epsc[:], EPS).then_inc(eps_ok, 1)
                dve.wait_ge(tp, 1)
                dve.tensor_copy(m.ckv[:, :, T:KEYS], PS[:, 0, 0:KVR].rearrange("p (r t) -> p r t", r=KKV)).then_inc(cache_ok, 1)
                dve.tensor_copy(m.k2[:, T:KEYS], PS[:, 0, KVR:KVR + P]).then_inc(cache_ok, 1)
                with dve.Fori(0, NT) as i:
                    dve.wait_ge(prod, (NM + 1) * (i + 1))
                    dve.wait_ge(fold, i)
                    dve.tensor_tensor(kc[:], PS[:, NM, 0:TILE], m.rope[:, cols(i)], ALU.mult).then_inc(kc_ok, 1)
                    dve.wait_ge(fold, i + 1)
                    dve.tensor_copy(m.k2[:, cols(i)], PS[:, NM, 0:TILE]).then_inc(k2_ok, 1)
                    for j in range(2):
                        dve.wait_ge(rt, 2 * i + j + 1)
                        dve.reciprocal(rinv[:, j, :], root[:, j, :]).then_inc(rc, 1)
                        dve.wait_ge(rc, 2 * i + j + 1)
                        for n in (range(KQ) if j == 0 else range(KQ, NM)):
                            to = m.qlat[:, n, cols(i)] if j == 0 else m.ckv[:, n - KQ, cols(i)]
                            dve.scalar_tensor_tensor(out=to, in0=PS[:, n, 0:TILE], scalar=g.vcol[:, V_QG + n:V_QG + n + 1],
                                                     in1=rinv[:, j, :], op0=ALU.mult, op1=ALU.mult).then_inc(lat_ok, 1)
                dve.wait_ge(tp, 2)
                dve.tensor_copy(outs[:], PS[:, 0, 0:KVR + ROPE]).then_inc(out_ok, 1)


def mla_heads(nc, g, io, m):
    with Stage(nc, "attn") as st:
        wq = st.sb("wq", [P, KQ, 2 * P])
        wkv = st.sb("wkv", [P, KKV, 2 * P])
        qT = st.sb("qT", [P, T])
        q2 = st.sb("q2", [P, T])
        kT = st.sb("kT", [P, KEYS])
        v = st.sb("v", [P, KEYS // P, P])
        mx = st.sb("mx", [P, NB])
        nm = st.sb("nm", [P, NB])
        rsum = st.sb("rsum", [P, NB])
        rin = st.sb("rin", [P, NB])
        prob = st.sb("prob", [P, 2, SAMPLE_KEYS])
        pT = st.sb("pT", [P, NB, P])
        on = st.sb("on", [P, 2, P])
        w_in, w_used = st.sem("w_in"), st.sem("w_used")
        q_mm, q2_mm, k_mm, v_mm = st.sem("q_mm"), st.sem("q2_mm"), st.sem("k_mm"), st.sem("v_mm")
        q_ok, q2_ok, k_ok, v_ok = st.sem("q_ok"), st.sem("q2_ok"), st.sem("k_ok"), st.sem("v_ok")
        s_mm, mx_ok, nm_ok, p_ok = st.sem("s_mm"), st.sem("mx_ok"), st.sem("nm_ok"), st.sem("p_ok")
        t_mm, pt_a, pt_d = st.sem("t_mm"), st.sem("pt_a"), st.sem("pt_d")
        pv_mm, rin_ok, on_ok, ot_mm, ot_ok = st.sem("pv_mm"), st.sem("rin_ok"), st.sem("on_ok"), st.sem("ot_mm"), st.sem("ot_ok")
        PS = g.PS
        VB = KEYS // P
        blocks = list(range(1, NB)) + [0]

        def key_blocks(j):
            return list(range(1, VB)) if blocks[j] else [0]

        def groups(j):
            kb = key_blocks(j)
            return [(6 + n % 2, kb[3 * n:3 * n + 3]) for n in range((len(kb) + 2) // 3)]

        NG = [len(groups(j)) for j in range(NB)]
        GA = [(n + 1) // 2 for n in NG]
        GD = [n // 2 for n in NG]

        with nc.Block(no_gpsimd_drain=True) as block:
            @block.sync
            def _(sp):
                wuq = io["mla_w_uq"][0].rearrange("(k p) n -> p k n", p=P)
                wukv = io["mla_w_ukv"][0].rearrange("(k p) n -> p k n", p=P)
                hw = NOPE + ROPE
                with sp.Fori(0, HEADS) as h:
                    sp.wait_ge(w_used, h)
                    sp.dma_start(wq[:, :, 0:hw], wuq[:, :, bass.ds(h * hw, hw)]).then_inc(w_in, 16)
                    sp.dma_start(wq[:, :, hw:hw + 32], wuq[:, :, bass.ds(h * hw + NOPE + 32, 32)]).then_inc(w_in, 16)
                    sp.dma_start(wq[:, :, hw + 32:hw + 64], wuq[:, :, bass.ds(h * hw + NOPE, 32)]).then_inc(w_in, 16)
                    sp.dma_start(wkv[:], wukv[:, :, bass.ds(h * 2 * P, 2 * P)]).then_inc(w_in, 16)

            @block.tensor
            def _(pe):
                def scores(h, j, qb):
                    if j == 0:
                        pe.wait_ge(k_ok, h + 1)
                        pe.wait_ge(q2_ok, h + 1)
                    elif j == 1:
                        pe.wait_ge(v_ok, h + 1)
                    else:
                        pe.wait_ge(p_ok, NB * h + j - 1)
                    kb = key_blocks(j)
                    width = min(TILE, P * len(kb))
                    for t in range(P * len(kb) // width):
                        out = PS[:, 3 * (j % 2) + t, 0:width]
                        c0 = P * kb[0] + t * width
                        pe.matmul(out, qT[:, P * qb:P * qb + P], kT[:, c0:c0 + width], start=True, stop=False)
                        last = pe.matmul(out, q2[:, P * qb:P * qb + P], m.k2[:, c0:c0 + width], start=False, stop=True)
                    last.then_inc(s_mm, 1)

                def turn_out(h, j):
                    pe.wait_ge(on_ok, NB * h + j + 1)
                    pe.transpose(PS[:, 6, TILE:TILE + P], on[:, j % 2], g.ident[:]).then_inc(ot_mm, 1)

                def transposes(h, j, n):
                    bank, kbs = groups(j)[n]
                    for a in range(len(kbs)):
                        c0 = P * (3 * n + a)
                        last = pe.transpose(PS[:, bank, P * a:P * a + P], prob[:, j % 2, c0:c0 + P], g.ident[:])
                    last.then_inc(t_mm, 1)

                def first_transposes(h, j):
                    na = sum(GA[:j])
                    pe.wait_ge(p_ok, NB * h + j + 1)
                    pe.wait_ge(pt_a, sum(GA) * h + na)
                    pe.wait_ge(on_ok, NB * h + j)
                    if j:
                        turn_out(h, j - 1)
                    else:
                        pe.wait_ge(ot_ok, NB * h)
                    for n in range(min(2, NG[j])):
                        transposes(h, j, n)

                def values(h, j):
                    na, nd = sum(GA[:j]), sum(GD[:j])
                    if NG[j] == 3:
                        pe.wait_ge(pt_a, sum(GA) * h + na + 1)
                        pe.wait_ge(ot_ok, NB * h + j)
                        transposes(h, j, 2)
                        pe.wait_ge(pt_d, sum(GD) * h + nd + 1)
                    else:
                        pe.wait_ge(pt_a, sum(GA) * h + na + GA[j])
                    kbs = key_blocks(j)
                    for a, kb in enumerate(kbs):
                        if a == 6:
                            pe.wait_ge(pt_a, sum(GA) * h + na + GA[j])
                        last = pe.matmul(PS[:, 7, TILE:TILE + P], pT[:, a], v[:, kb], start=(a == 0),
                                         stop=(a == len(kbs) - 1))
                    last.then_inc(pv_mm, 1)

                with pe.Fori(0, HEADS) as h:
                    pe.wait_ge(w_in, 64 * h + 64)
                    pe.wait_ge(p_ok, NB * h)
                    for t in range(NT):
                        for k in range(KQ):
                            last = pe.matmul(PS[:, t, 0:TILE], wq[:, k, 0:P], m.qlat[:, k, TILE * t:TILE * t + TILE],
                                             start=(k == 0), stop=(k == KQ - 1))
                    last.then_inc(q_mm, 1)
                    for t in range(NT):
                        for k in range(KQ):
                            last = pe.matmul(PS[:, 3 + t, 0:TILE], wq[:, k, P:2 * P],
                                             m.qlat[:, k, TILE * t:TILE * t + TILE], start=(k == 0), stop=(k == KQ - 1))
                    last.then_inc(q2_mm, 1)
                    pe.wait_ge(q_ok, h + 1)
                    for t in range(3):
                        c0, c1 = TILE * t, (TILE * t + TILE if t < 2 else KEYS)
                        for r in range(KKV):
                            last = pe.matmul(PS[:, t, 0:c1 - c0], wkv[:, r, 0:P], m.ckv[:, r, c0:c1],
                                             start=(r == 0), stop=(r == KKV - 1))
                    last.then_inc(k_mm, 1)
                    pe.wait_ge(q2_ok, h + 1)
                    for kb in range(VB):
                        for r in range(KKV):
                            last = pe.matmul(PS[:, 3 + kb // 4, P * (kb % 4):P * (kb % 4) + P],
                                             m.ckv[:, r, P * kb:P * kb + P], wkv[:, r, P:2 * P],
                                             start=(r == 0), stop=(r == KKV - 1))
                    last.then_inc(v_mm, 1)
                    scores(h, 0, blocks[0])
                    scores(h, 1, blocks[1])
                    for j in range(NB):
                        first_transposes(h, j)
                        if j + 2 < NB:
                            scores(h, j + 2, blocks[j + 2])
                        values(h, j)
                    pe.wait_ge(pt_a, sum(GA) * h + sum(GA))
                    turn_out(h, NB - 1)

            @block.scalar
            def _(act):
                def exps(h, j):
                    pe_done = sum(NG[:j - 1]) if j > 1 else 0
                    act.wait_ge(t_mm, sum(NG) * h + pe_done)
                    act.wait_ge(nm_ok, NB * h + j + 1)
                    kb = key_blocks(j)
                    nt, width = max(1, len(kb) // 3), min(TILE, P * len(kb))
                    act.activation(prob[:, j % 2, 0:nt * width].rearrange("p (t k) -> p t k", t=nt),
                                   PS[:, 3 * (j % 2):3 * (j % 2) + nt, 0:width], ACT.Exp, bias=nm[:, j:j + 1],
                                   scale=SCALE, accum_out=rsum[:, j:j + 1]).then_inc(p_ok, 1)

                def out_cols(h, j):
                    act.wait_ge(ot_mm, NB * h + j + 1)
                    act.copy(m.oT[:, bass.ds(h, 1), P * blocks[j]:P * blocks[j] + P].squeeze(1),
                             PS[:, 6, TILE:TILE + P]).then_inc(ot_ok, 1)

                def evacuate(h, j, n):
                    bank, kbs = groups(j)[n]
                    act.wait_ge(t_mm, sum(NG) * h + sum(NG[:j]) + n + 1)
                    if n == 0 and j:
                        out_cols(h, j - 1)
                    act.copy(pT[:, 3 * n:3 * n + len(kbs)], PS[:, bank, 0:P * len(kbs)].rearrange(
                        "p (a k) -> p a k", k=P)).then_inc(pt_a, 1)

                with act.Fori(0, HEADS) as h:
                    act.wait_ge(q_mm, h + 1)
                    act.copy(qT[:].rearrange("p (t n) -> p t n", t=NT), PS[:, 0:NT, 0:TILE]).then_inc(q_ok, 1)
                    act.wait_ge(k_mm, h + 1)
                    act.copy(kT[:, 0:2 * TILE].rearrange("p (t n) -> p t n", t=2), PS[:, 0:2, 0:TILE])
                    act.copy(kT[:, 2 * TILE:KEYS], PS[:, 2, 0:KEYS - 2 * TILE]).then_inc(k_ok, 1)
                    exps(h, 0)
                    exps(h, 1)
                    for j in range(NB):
                        evacuate(h, j, 0)
                        if NG[j] == 3:
                            evacuate(h, j, 2)
                        if j + 2 < NB:
                            exps(h, j + 2)
                    out_cols(h, NB - 1)

            @block.vector
            def _(dve):
                def maxima(h, j):
                    dve.wait_ge(s_mm, NB * h + j + 1)
                    kb = key_blocks(j)
                    nt, width = max(1, len(kb) // 3), min(TILE, P * len(kb))
                    src = PS[:, 3 * (j % 2):3 * (j % 2) + nt, 0:width]
                    dve.tensor_reduce(mx[:, j:j + 1], src, mybir.AxisListType.XY, ALU.max).then_inc(mx_ok, 1)
                    dve.wait_ge(mx_ok, NB * h + j + 1)
                    dve.tensor_scalar(nm[:, j:j + 1], mx[:, j:j + 1], -SCALE, None, ALU.mult).then_inc(nm_ok, 1)

                def copy_group(h, j):
                    for n, (bank, kbs) in enumerate(groups(j)):
                        if n % 2:
                            dve.wait_ge(t_mm, sum(NG) * h + sum(NG[:j]) + n + 1)
                            dve.tensor_copy(pT[:, 3 * n:3 * n + len(kbs)], PS[:, bank, 0:P * len(kbs)].rearrange(
                                "p (a k) -> p a k", k=P)).then_inc(pt_d, 1)

                def finish(h, j):
                    dve.wait_ge(p_ok, NB * h + j + 1)
                    dve.reciprocal(rin[:, j:j + 1], rsum[:, j:j + 1]).then_inc(rin_ok, 1)
                    dve.wait_ge(pv_mm, NB * h + j + 1)
                    dve.wait_ge(rin_ok, NB * h + j + 1)
                    dve.tensor_scalar(on[:, j % 2], PS[:, 7, TILE:TILE + P], rin[:, j:j + 1], None,
                                      ALU.mult).then_inc(on_ok, 1)

                with dve.Fori(0, HEADS) as h:
                    dve.wait_ge(q2_mm, h + 1)
                    dve.tensor_tensor(q2[:].rearrange("p (t n) -> p t n", t=NT), PS[:, 3:6, 0:TILE],
                                      m.rope[:].rearrange("p (t n) -> p t n", t=NT), ALU.mult).then_inc(q2_ok, 1)
                    dve.wait_ge(v_mm, h + 1)
                    vf = v[:].rearrange("p a b -> p (a b)")
                    dve.tensor_copy(vf[:, 0:1024].rearrange("p (t n) -> p t n", t=2), PS[:, 3:5, :])
                    dve.tensor_copy(vf[:, 1024:1280], PS[:, 5, 0:256]).then_inc(v_ok, 1)
                    maxima(h, 0)
                    maxima(h, 1)
                    for j in range(NB):
                        copy_group(h, j)
                        if j + 2 < NB:
                            maxima(h, j + 2)
                        finish(h, j)

            @block.gpsimd
            def _(pool):
                with pool.Fori(0, HEADS) as h:
                    pool.wait_ge(v_mm, h + 1)
                    pool.sem_inc(w_used, 1)


def block_loop(eng, body):
    with eng.Fori(0, DEC // P // 2) as i:
        for u in range(2):
            body(2 * i + u, u, 2 * i + u + 1, 1)
    body(DEC // P, 0, 0, 0)


def project_out(nc, g, name, layer, kd, w_dram, take):
    with Stage(nc, name) as st:
        w = st.sb("w", [P, kd, D])
        x = st.sb("x", [P, 2, D])
        t = st.sb("t", [P, 2, D])
        w_in = [st.sem(f"w_in{c}") for c in range(4)]
        x_in = [st.sem("x_in0"), st.sem("x_in1")]
        saved = [st.sem("saved0"), st.sem("saved1")]
        mm, gated, added = st.sem("mm"), st.sem("gated"), st.sem("added")
        src, src_ok, engines = take(st, mm)
        PS = g.PS

        with nc.Block(no_gpsimd_drain=True) as block:
            @block.sync
            def _(sp):
                for c in range(4):
                    ks, cs = slice(kd // 2 * (c % 2), kd // 2 * (c % 2 + 1)), slice(512 * (c // 2), 512 * (c // 2) + 512)
                    sp.dma_start(w[:, ks, cs], w_dram.rearrange("(k p) n -> p k n", p=P)[:, ks, cs]).then_inc(w_in[c], 16)

                def body(n, u, b, grp):
                    if engines.get("sync"):
                        engines["sync"](sp, n, u, b, grp)
                    if u == 0:
                        sp.wait_ge(saved[0], 8 * n)
                    else:
                        sp.wait_ge(saved[1], 8 * n - 8)
                    rows = bass.ds(b * P, P) if grp else slice(0, P)
                    sp.dma_start(x[:, u], g.res[rows, :]).then_inc(x_in[u], 16)
                block_loop(sp, body)
                sp.wait_ge(saved[0], 16 * (DEC // P // 2 + 1))
                sp.wait_ge(saved[1], 16 * (DEC // P // 2))

            @block.tensor
            def _(pe):
                pe.sem_inc(mm, 1)
                if engines.get("tensor"):
                    engines["tensor"](pe, 0, 0)

                def body(n, u, b, grp):
                    if engines.get("tensor") and grp:
                        engines["tensor"](pe, n + 1, 1 - u)
                    pe.wait_ge(src_ok, n + 1)
                    pe.wait_ge(gated, n)
                    for half in range(2):
                        for k in range(kd):
                            if k % (kd // 2) == 0:
                                pe.wait_ge(w_in[2 * half + 2 * k // kd], 16)
                            last = pe.matmul(PS[:, 2 * u + half, :], src[:, u, k, :], w[:, k, 512 * half:512 * half + 512],
                                             start=(k == 0), stop=(k == kd - 1))
                    last.then_inc(mm, 1)
                block_loop(pe, body)

            @block.scalar
            def _(act):
                if engines.get("before_scalar"):
                    engines["before_scalar"](act)

                def body(n, u, b, grp):
                    engines["scalar"](act, n, u, b, grp)
                block_loop(act, body)

            @block.vector
            def _(dve):
                dve.sem_inc(gated, 1)
                if engines.get("before_vector"):
                    engines["before_vector"](dve)
                if engines.get("vector"):
                    engines["vector"](dve, 0, 0)

                def body(n, u, b, grp):
                    if engines.get("vector") and grp:
                        engines["vector"](dve, n + 1, 1 - u)
                    dve.wait_ge(mm, n + 2)
                    dve.wait_ge(x_in[u], 8 * n + 16 - 8 * u)
                    dve.tensor_tensor(t[:, u].rearrange("p (h n) -> p h n", h=2), PS[:, 2 * u:2 * u + 2, :],
                                      g.gate_row[:, grp].rearrange("p (h n) -> p h n", h=2),
                                      ALU.mult).then_inc(gated, 1)
                    dve.wait_ge(gated, n + 2)
                    dve.tensor_tensor(x[:, u], x[:, u], t[:, u], ALU.add).then_inc(added, 1)
                block_loop(dve, body)

            @block.gpsimd
            def _(pool):
                def body(n, u, b, grp):
                    pool.wait_ge(added, n + 1)
                    rows = bass.ds(b * P, P) if grp else slice(0, P)
                    pool.dma_start(g.res[rows, :], x[:, u]).then_inc(saved[u], 16)
                block_loop(pool, body)


def mla_out(nc, g, io, m):
    def take(st, mm):
        oc = st.sb("oc", [P, 2, HEADS, P])
        oc_ok = st.sem("oc_ok")

        def scalar(act, n, u, b, grp):
            act.wait_ge(mm, n)
            cols = bass.ds(b * P, P) if grp else slice(0, P)
            act.copy(oc[:, u], m.oT[:, :, cols]).then_inc(oc_ok, 1)
        return oc, oc_ok, {"scalar": scalar}
    project_out(nc, g, "wo", 0, HEADS, io["mla_w_o"][0], take)

def choose(nc, g, io, layer):
    with Stage(nc, f"topk{layer}") as st:
        best = st.sb("best", [NE, 8])
        at = st.sb("at", [NE, 8], U32)
        vals = st.sb("vals", [NE, CAP])
        rows = st.sb("rows", [NE, CAP])
        chain, picked, tp, out = st.sem("chain"), st.sem("picked"), st.sem("tp"), st.sem("out")
        PS = g.PS
        mod = Modulation(st, g, io, layer + 1) if layer + 1 < DEPTH else None
        with nc.Block(no_gpsimd_drain=True) as block:
            if mod:
                @block.sync
                def _(sp):
                    mod.sync(sp)

                @block.scalar
                def _(act):
                    mod.scalar(act)

            @block.vector
            def _(dve):
                def rounds(values, first, count, before):
                    with dve.Fori(0, count) as i:
                        steps = Steps(dve, chain, i, 5, before)
                        steps.did(dve.max(best[:], values))
                        wait_alone(dve, chain, steps.base + 1)
                        steps.did(dve.max_index(at[:], best[:], values))
                        steps.did(dve.tensor_copy(vals[:, bass.ds(first + i * 8, 8)], best[:]))
                        wait_alone(dve, chain, steps.base + 2)
                        steps.did(dve.match_replace(values, best[:], values, -1.0))
                        steps.did(dve.tensor_copy(rows[:, bass.ds(first + i * 8, 8)], at[:]))
                        steps.settle()
                rounds(g.aff[:, SEQ:T], 0, CAP_S // 8, 0)
                rounds(g.aff[:, 0:SEQ], CAP_S, CAP_P // 8, 5 * CAP_S // 8)
                dve.tensor_scalar(rows[:, 0:CAP_S], rows[:, 0:CAP_S], float(SEQ), None, ALU.add).then_inc(picked, 1)
                if mod:
                    mod.vector(dve)
                dve.wait_ge(tp, 1)
                dve.tensor_copy(g.row_s[:], PS[:, 0, 0:NE]).then_inc(out, 1)
                dve.tensor_copy(g.gate_s[:], PS[:, 0, NE:2 * NE]).then_inc(out, 1)
                dve.tensor_copy(g.row_p[:], PS[0:CAP_P, 0, 2 * NE:3 * NE]).then_inc(out, 1)
                dve.tensor_copy(g.gate_p[:], PS[0:CAP_P, 0, 3 * NE:4 * NE]).then_inc(out, 1)

            @block.tensor
            def _(pe):
                if mod:
                    mod.tensor(pe)
                pe.wait_ge(picked, 1)
                ident = g.ident[0:NE, 0:NE]
                pe.transpose(PS[:, 0, 0:NE], rows[:, 0:CAP_S], ident)
                pe.transpose(PS[:, 0, NE:2 * NE], vals[:, 0:CAP_S], ident)
                pe.transpose(PS[0:CAP_P, 0, 2 * NE:3 * NE], rows[:, CAP_S:CAP], ident)
                pe.transpose(PS[0:CAP_P, 0, 3 * NE:4 * NE], vals[:, CAP_S:CAP], ident).then_inc(tp, 1)


def experts(nc, g, io, layer):
    with Stage(nc, f"moe{layer}") as st:
        HB = 512
        wg = st.sb("wg", [P, 2, KD, HB])
        wu = st.sb("wu", [P, 2, KD, HB])
        wd = st.sb("wd", [P, 2, KD, HB])
        x_s = st.sb("x_s", [P, D])
        x_p = st.sb("x_p", [CAP_P, D])
        id_s = st.sb("id_s", [P, 2], U32)
        id_p = st.sb("id_p", [CAP_P, 2], U32)
        xT = st.sb("xT", [P, KD, CAP])
        sg = st.sb("sg", [P, KD, CAP])
        hid = st.sb("hid", [P, KD, CAP])
        ye = st.sb("ye", [P, KD, CAP])
        y_s = st.sb("y_s", [P, D])
        y_p = st.sb("y_p", [CAP_P, D])
        wg_in = [st.sem("wg_in0"), st.sem("wg_in1")]
        wu_in = [st.sem("wu_in0"), st.sem("wu_in1")]
        wd_in = [st.sem("wd_in0"), st.sem("wd_in1")]
        xs_in, xp_in = st.sem("xs_in"), st.sem("xp_in")
        id_ok, ys_out, yp_out = st.sem("id_ok"), st.sem("ys_out"), st.sem("yp_out")
        x_mm, xa_ok, xd_ok = st.sem("x_mm"), st.sem("xa_ok"), st.sem("xd_ok")
        half_gu, gu_mm, sg_ok, hid_ok = st.sem("half_gu"), st.sem("gu_mm"), st.sem("sg_ok"), st.sem("hid_ok")
        half_d, d_mm, ye_ok = st.sem("half_d"), st.sem("d_mm"), st.sem("ye_ok")
        back, ys_ok, yp_ok = st.sem("back"), st.sem("ys_ok"), st.sem("yp_ok")
        PS = g.PS
        TRIOS = [(0, 3), (3, 6), (6, 8)]

        def turns(eng, body):
            with eng.Fori(0, NE - 1) as e:
                body(e, True)
            body(NE - 1, False)

        def trio(bank, a, b):
            return PS[:, bank, 0:(b - a) * CAP].rearrange("p (m c) -> p m c", c=CAP)

        with nc.Block(no_gpsimd_drain=True) as block:
            @block.sync
            def _(sp):
                def view(w):
                    return w[layer].rearrange("e (k p) n -> p e k n", p=P)

                with sp.Fori(0, NE) as e:
                    for half in range(2):
                        sp.wait_ge(half_gu if half == 0 else gu_mm, e if half == 0 else 3 * e)
                        for buf, w, s in ((wg, io["moe_w_gate"], wg_in), (wu, io["moe_w_up"], wu_in)):
                            sp.dma_start(buf[:, half], view(w)[:, bass.ds(e, 1), :, HB * half:HB * half + HB].squeeze(1)
                                         ).then_inc(s[half], 16)
                    for half in range(2):
                        sp.wait_ge(half_d if half == 0 else d_mm, e if half == 0 else 3 * e)
                        sp.dma_start(wd[:, half], view(io["moe_w_down"])[:, bass.ds(e, 1), :, HB * half:HB * half + HB].squeeze(1)
                                     ).then_inc(wd_in[half], 16)

            @block.gpsimd
            def _(pool):
                def gather(e, n_ids):
                    pool.tensor_copy(id_s[:, 0:1], g.row_s[:, bass.ds(e, 1)]).then_inc(id_ok, 1)
                    pool.tensor_copy(id_p[:, 0:1], g.row_p[:, bass.ds(e, 1)]).then_inc(id_ok, 1)
                    wait_alone(pool, id_ok, n_ids + 2)
                    pool.indirect_dma_start(x_s[:], None, g.normed, bass.IndirectOffsetOnAxis(ap=id_s[:, 0:1], axis=0),
                                            bounds_check=T - 1, oob_is_err=False).then_inc(xs_in, 16)
                    pool.indirect_dma_start(x_p[:], None, g.normed, bass.IndirectOffsetOnAxis(ap=id_p[:, 0:1], axis=0),
                                            bounds_check=T - 1, oob_is_err=False).then_inc(xp_in, 16)

                def scatter(e, n_ids):
                    wait_alone(pool, ys_out, 16 * e)
                    pool.wait_ge(yp_out, 16 * e)
                    pool.tensor_copy(id_s[:, 1:2], g.row_s[:, bass.ds(e, 1)]).then_inc(id_ok, 1)
                    pool.tensor_copy(id_p[:, 1:2], g.row_p[:, bass.ds(e, 1)]).then_inc(id_ok, 1)
                    wait_alone(pool, id_ok, n_ids + 2)
                    wait_alone(pool, ys_ok, 2 * e + 2)
                    pool.indirect_dma_start(g.res, bass.IndirectOffsetOnAxis(ap=id_s[:, 1:2], axis=0), y_s[:], None,
                                            bounds_check=T - 1, compute_op=ALU.add).then_inc(ys_out, 16)
                    wait_alone(pool, yp_ok, e + 1)
                    pool.indirect_dma_start(g.res, bass.IndirectOffsetOnAxis(ap=id_p[:, 1:2], axis=0), y_p[:], None,
                                            bounds_check=T - 1, compute_op=ALU.add).then_inc(yp_out, 16)

                gather(0, 0)

                def body(e, more):
                    if more:
                        pool.wait_ge(x_mm, 3 * e + 3)
                        gather(e + 1, 4 * e + 2)
                        scatter(e, 4 * e + 4)
                    else:
                        scatter(e, 4 * e + 2)
                turns(pool, body)
                pool.wait_ge(ys_out, 16 * NE)
                pool.wait_ge(yp_out, 16 * NE)

            @block.tensor
            def _(pe):
                def tokens(e, rows_read, up_read):
                    pe.wait_ge(ys_ok, rows_read)
                    pe.wait_ge(xs_in, 16 * e + 16)
                    for k in range(KD):
                        last = pe.transpose(PS[:, 6 + k // 4, P * (k % 4):P * (k % 4) + P], x_s[:, P * k:P * k + P], g.ident[:])
                        if k % 4 == 3:
                            last.then_inc(x_mm, 1)
                    pe.wait_ge(hid_ok, up_read)
                    wait_alone(pe, xp_in, 16 * e + 16)
                    for k in range(KD):
                        last = pe.transpose(PS[:, 3, CAP_P * k:CAP_P * k + CAP_P], x_p[:, P * k:P * k + P],
                                            g.ident[0:CAP_P, 0:CAP_P])
                    last.then_inc(x_mm, 1)

                def rows_back(a, b):
                    for k in range(a, b):
                        pe.transpose(PS[:, 6 + k // 4, P * (k % 4):P * (k % 4) + P], ye[:, k, 0:CAP_S], g.ident[:])
                        last = pe.transpose(PS[0:CAP_P, 4 + k // 4, P * (k % 4):P * (k % 4) + P], ye[:, k, CAP_S:CAP], g.ident[:])
                    return last

                tokens(0, 0, 0)

                def body(e, more):
                    pe.wait_ge(xa_ok, 4 * e + 4)
                    pe.wait_ge(xd_ok, 6 * e + 6)
                    pe.wait_ge(ye_ok, 6 * e)
                    for q, (a, b) in enumerate(TRIOS):
                        for w, w_in, bank in ((wg, wg_in, q), (wu, wu_in, 3 + q)):
                            if bank == 4:
                                pe.wait_ge(yp_ok, e)
                            for f in range(a, b):
                                if f % 4 == 0:
                                    pe.wait_ge(w_in[f // 4], 16 * e + 16)
                                for k in range(KD):
                                    last = pe.matmul(PS[:, bank, CAP * (f - a):CAP * (f - a + 1)],
                                                     w[:, f // 4, k, P * (f % 4):P * (f % 4) + P], xT[:, k, :],
                                                     start=(k == 0), stop=(k == KD - 1))
                                if f == 3 and bank == 4:
                                    last.then_inc(half_gu, 1)
                        last.then_inc(gu_mm, 1)
                    if more:
                        tokens(e + 1, 2 * e, 3 * e + 1)
                    pe.wait_ge(hid_ok, 3 * e + 3)
                    for q, (a, b) in enumerate(TRIOS):
                        if q == 2:
                            if more:
                                pe.wait_ge(xa_ok, 4 * e + 8)
                                pe.wait_ge(xd_ok, 6 * e + 12)
                            else:
                                pe.wait_ge(ys_ok, 2 * e)
                            pe.wait_ge(ye_ok, 6 * e + 2)
                            rows_back(*TRIOS[0])
                        for f in range(a, b):
                            if f % 4 == 0:
                                pe.wait_ge(wd_in[f // 4], 16 * e + 16)
                            for k in range(KD):
                                last = pe.matmul(PS[:, q, CAP * (f - a):CAP * (f - a + 1)],
                                                 wd[:, f // 4, k, P * (f % 4):P * (f % 4) + P], hid[:, k, :],
                                                 start=(k == 0), stop=(k == KD - 1))
                            if f == 3:
                                last.then_inc(half_d, 1)
                        last.then_inc(d_mm, 1)
                    pe.wait_ge(ye_ok, 6 * e + 4)
                    rows_back(*TRIOS[1])
                    pe.wait_ge(ye_ok, 6 * e + 6)
                    rows_back(*TRIOS[2]).then_inc(back, 1)
                turns(pe, body)

            @block.scalar
            def _(act):
                def tokens(e):
                    act.wait_ge(x_mm, 3 * e + 2)
                    for k in range(4, KD):
                        act.activation(xT[:, k, 0:CAP_S], PS[:, 7, P * (k - 4):P * (k - 3)], ACT.Identity,
                                       scale=g.gain[:, layer, 1, k, 1:2], bias=g.shift[:, layer, 1, k, 1:2]).then_inc(xa_ok, 1)
                tokens(0)

                def body(e, more):
                    for q, (a, b) in enumerate(TRIOS):
                        act.wait_ge(gu_mm, 3 * e + q + 1)
                        act.activation(sg[:, a:b], trio(q, a, b), ACT.Silu).then_inc(sg_ok, 1)
                    if more:
                        tokens(e + 1)
                    act.wait_ge(back, e + 1)
                    act.wait_ge(ys_out, 16 * e)
                    for half in range(2):
                        act.activation(y_s[:, 512 * half:512 * half + 512], PS[:, 6 + half, :], ACT.Copy,
                                       scale=g.gate_s[:, bass.ds(e, 1)]).then_inc(ys_ok, 1)
                turns(act, body)

            @block.vector
            def _(dve):
                def tokens(e):
                    dve.wait_ge(x_mm, 3 * e + 1)
                    for k in range(4):
                        dve.tensor_scalar(xT[:, k, 0:CAP_S], PS[:, 6, P * k:P * k + P], g.gain[:, layer, 1, k, 1:2],
                                          g.shift[:, layer, 1, k, 1:2], ALU.mult, ALU.add).then_inc(xd_ok, 1)
                    dve.wait_ge(x_mm, 3 * e + 3)
                    dve.tensor_tensor(xT[:, :, CAP_S:CAP], PS[:, 3, 0:P].rearrange("p (k c) -> p k c", k=KD),
                                      g.gain[:, layer, 1, :, 0:1].to_broadcast([P, KD, CAP_P]), ALU.mult).then_inc(xd_ok, 1)
                    dve.wait_ge(xd_ok, 6 * e + 5)
                    dve.tensor_tensor(xT[:, :, CAP_S:CAP], xT[:, :, CAP_S:CAP],
                                      g.shift[:, layer, 1, :, 0:1].to_broadcast([P, KD, CAP_P]), ALU.add).then_inc(xd_ok, 1)
                tokens(0)

                def body(e, more):
                    for q, (a, b) in enumerate(TRIOS):
                        dve.wait_ge(sg_ok, 3 * e + q + 1)
                        dve.tensor_tensor(hid[:, a:b], sg[:, a:b], trio(3 + q, a, b), ALU.mult).then_inc(hid_ok, 1)
                    if more:
                        tokens(e + 1)
                    for q, (a, b) in enumerate(TRIOS):
                        dve.wait_ge(d_mm, 3 * e + q + 1)
                        for c0, c1, j in ((0, CAP_S, 1), (CAP_S, CAP, 0)):
                            dve.tensor_tensor(ye[:, a:b, c0:c1], trio(q, a, b)[:, :, c0:c1],
                                              g.modc[:, layer, 40 + a:40 + b, j:j + 1].to_broadcast([P, b - a, c1 - c0]),
                                              ALU.mult).then_inc(ye_ok, 1)
                    dve.wait_ge(back, e + 1)
                    dve.wait_ge(yp_out, 16 * e)
                    dve.tensor_scalar(y_p[:].rearrange("p (h n) -> p h n", h=2), PS[0:CAP_P, 4:6, :],
                                      g.gate_p[:, bass.ds(e, 1)], None, ALU.mult).then_inc(yp_ok, 1)
                turns(dve, body)

def ssm_gate_and_steps(nc, g, io, hT, q):
    with Stage(nc, "ssmz") as st:
        WZ = 256
        w = st.sb("w", [P, 2, KD, WZ])
        w_hi = st.sb("w_hi", [P, 2, KD, WZ], F32R)
        w_lo = st.sb("w_lo", [P, 2, KD, WZ], F32R)
        zs = st.sb("zs", [P, 3, WZ])
        wdt = st.sb("wdt", [P, KD, 2 * SH])
        wdt_hi = st.sb("wdt_hi", [P, KD, 2 * SH], F32R)
        wdt_lo = st.sb("wdt_lo", [P, KD, 2 * SH], F32R)
        bias = st.sb("bias", [P, 2 * SH])
        alog = st.sb("alog", [P, 2 * SH])
        a = st.sb("a", [P, 2 * SH])
        N2 = 2 * NB * SH
        v, e, s2, q2, pw = (st.sb(n, [P, N2]) for n in ("v", "e", "s2", "q2", "pw"))
        diff = st.sb("diff", [P, 2, NB, SH])
        w_in = [st.sem("w_in0"), st.sem("w_in1")]
        hi_ok, lo_ok, dt_hi, dt_lo = st.sem("hi_ok"), st.sem("lo_ok"), st.sem("dt_hi"), st.sem("dt_lo")
        small, z_mm, z_ok = st.sem("small"), st.sem("z_mm"), st.sem("z_ok")
        z_out = [st.sem(f"z_out{i}") for i in range(3)]
        dt_mm, v_ok, e_ok, a_ok = st.sem("dt_mm"), st.sem("v_ok"), st.sem("e_ok"), st.sem("a_ok")
        chain, power, cum, exps = st.sem("chain"), st.sem("power"), st.sem("cum"), st.sem("exps")
        PS = g.PS
        w_dram = io["ssm_w_in"][0].rearrange("(k p) n -> p k n", p=P)
        NC_ = DI // WZ
        h_hi, h_lo = hT

        def chunks(eng, body):
            with eng.Fori(0, NC_ // 2 - 1) as i:
                for u in range(2):
                    body(i, u, True)
            body(NC_ // 2 - 1, 0, True)
            body(NC_ // 2 - 1, 1, False)

        def tokens(k, b):
            return h_hi[:, k, P * b:P * b + P], h_lo[:, k, P * b:P * b + P]

        with nc.Block(no_gpsimd_drain=True) as block:
            @block.sync
            def _(sp):
                sp.dma_start(wdt[:], w_dram[:, :, DI + CONV:IN_DIM]).then_inc(small, 16)
                sp.dma_start(bias[:], io["ssm_dt_bias"][0].rearrange("d h -> (d h)").partition_broadcast(P)).then_inc(small, 16)
                sp.dma_start(alog[:], io["ssm_a_log"][0].rearrange("d h -> (d h)").partition_broadcast(P)).then_inc(small, 16)
                sp.dma_start(q.skip[:], io["ssm_d_skip"][0].partition_broadcast(P)).then_inc(small, 16)
                for u in range(2):
                    sp.dma_start(w[:, u], w_dram[:, :, WZ * u:WZ * u + WZ]).then_inc(w_in[u], 16)
                with sp.Fori(1, NC_ // 2) as i:
                    for u in range(2):
                        sp.wait_ge(lo_ok, 2 * i + u - 1)
                        sp.dma_start(w[:, u], w_dram[:, :, bass.ds(i * 2 * WZ + WZ * u, WZ)]).then_inc(w_in[u], 16)

            @block.gpsimd
            def _(pool):
                with pool.Fori(0, NC_ // 2) as i:
                    for u in range(2):
                        for b in range(NB):
                            pool.wait_ge(z_ok, 2 * NB * i + NB * u + b + 1)
                            pool.dma_start(g.z[P * b:P * b + P, bass.ds(i * 2 * WZ + WZ * u, WZ)], zs[:, b % 3]
                                           ).then_inc(z_out[b % 3], 16)
                for s in z_out:
                    pool.wait_ge(s, 16 * NC_ * NB // 3)

            @block.tensor
            def _(pe):
                pe.wait_ge(dt_lo, 1)
                for b in range(NB):
                    for k in range(KD):
                        last = exact_products(pe, PS[:, 4 + b // 8, 64 * (b % 8):64 * (b % 8) + 64], tokens(k, b),
                                              (wdt_hi[:, k], wdt_lo[:, k]), k == 0, k == KD - 1)
                last.then_inc(dt_mm, 1)
                pe.wait_ge(v_ok, 4)
                with pe.Fori(0, NC_ // 2) as i:
                    for u in range(2):
                        pe.wait_ge(lo_ok, 2 * i + u + 1)
                        for b in range(NB):
                            if b < 4:
                                pe.wait_ge(z_ok, 2 * NB * i)
                            else:
                                pe.wait_ge(z_ok, 2 * NB * i + NB * u + b - 3)
                            for k in range(KD):
                                last = exact_products(pe, PS[:, 4 * u + b % 4, 0:WZ], tokens(k, b),
                                                      (w_hi[:, u, k], w_lo[:, u, k]), k == 0, k == KD - 1)
                            last.then_inc(z_mm, 1)
                pe.wait_ge(chain, 12)
                pe.wait_ge(z_ok, NC_ * NB)
                f = q.da[:].rearrange("p d b h -> p d (b h)")
                for d in range(2):
                    pe.matmul(PS[:, 6, 0:NB * SH], (g.upper, g.lower)[d][:], f[:, d], start=True, stop=True).then_inc(cum, 1)
                    pe.matmul(PS[:, 7, 0:NB * SH], g.ones[:], f[:, d], start=True, stop=True).then_inc(cum, 1)
                    pe.wait_ge(exps, 2 * d + 2)
                    pe.wait_ge(chain, 13 + d)

            @block.scalar
            def _(act):
                def rounded(turn, slot, used):
                    act.wait_ge(w_in[slot], 16 * turn + 16)
                    act.wait_ge(z_mm, used)
                    act.copy(w_hi[:, slot], w[:, slot]).then_inc(hi_ok, 1)

                act.wait_ge(small, 64)
                act.copy(wdt_hi[:], wdt[:]).then_inc(dt_hi, 1)
                act.activation(a[:], alog[:], ACT.Exp).then_inc(a_ok, 1)
                rounded(0, 0, 0)
                act.wait_ge(v_ok, 4)
                act.activation(e[:], v[:], ACT.Abs).then_inc(e_ok, 1)
                act.wait_ge(e_ok, 1)
                act.activation(e[:], e[:], ACT.Exp, scale=-1.0).then_inc(e_ok, 1)

                def body(i, u, more):
                    if more:
                        rounded(i + u, 1 - u, 2 * NB * i + NB * u)
                    for b in range(NB):
                        act.wait_ge(z_mm, 2 * NB * i + NB * u + b + 1)
                        act.wait_ge(z_out[b % 3], i * 96 + 48 * u + 16 * (b // 3))
                        act.activation(zs[:, b % 3], PS[:, 4 * u + b % 4, 0:WZ], ACT.Silu).then_inc(z_ok, 1)
                chunks(act, body)
                for d in range(2):
                    act.wait_ge(cum, 2 * d + 2)
                    ps = PS[:, 6:8, 0:NB * SH]
                    act.activation(q.grow[:, d].rearrange("p b h -> p (b h)"), ps[:, 0], ACT.Exp).then_inc(exps, 1)
                    act.activation(q.dec[:, d].rearrange("p b h -> p (b h)"), ps[:, 1], ACT.Exp).then_inc(exps, 1)
                act.wait_ge(chain, 14)
                act.activation(diff[:], diff[:], ACT.Exp).then_inc(exps, 1)

            @block.vector
            def _(dve):
                def rest(c, slot):
                    dve.wait_ge(hi_ok, c + 1)
                    dve.tensor_tensor(w_lo[:, slot], w[:, slot], w_hi[:, slot].bitcast(F32), ALU.subtract).then_inc(lo_ok, 1)

                dve.wait_ge(dt_hi, 1)
                dve.tensor_tensor(wdt_lo[:], wdt[:], wdt_hi[:].bitcast(F32), ALU.subtract).then_inc(dt_lo, 1)
                rest(0, 0)
                dve.wait_ge(dt_mm, 1)
                vv = v[:].rearrange("p (d b h) -> p d b h", d=2, b=NB)
                for d in range(2):
                    for b0, b1, bank in ((0, 8, 4), (8, 9, 5)):
                        dve.tensor_tensor(vv[:, d, b0:b1],
                                          PS[:, bank, 0:64 * (b1 - b0)].rearrange("p (b d h) -> p b d h", d=2, h=SH)[:, :, d],
                                          bias[:, SH * d:SH * d + SH].unsqueeze(1).to_broadcast([P, b1 - b0, SH]),
                                          ALU.add).then_inc(v_ok, 1)
                steps, powers = Steps(dve, chain), Steps(dve, power)
                dve.wait_ge(e_ok, 2)
                steps.alone(dve.tensor_scalar(s2[:], e[:], 2.0, None, ALU.add))
                steps.alone(dve.reciprocal(s2[:], s2[:]))
                steps.alone(dve.tensor_tensor(s2[:], s2[:], e[:], ALU.mult))
                steps.alone(dve.tensor_tensor(q2[:], s2[:], s2[:], ALU.mult))
                steps.alone(dve.tensor_scalar(pw[:], q2[:], 1.0 / 15, 1.0 / 13, ALU.mult, ALU.add))
                for c in (11, 9, 7, 5, 3):
                    powers.alone(dve.tensor_tensor(pw[:], pw[:], q2[:], ALU.mult))
                    powers.alone(dve.tensor_scalar(pw[:], pw[:], 1.0 / c, None, ALU.add))
                steps.alone(dve.tensor_tensor(pw[:], pw[:], q2[:], ALU.mult))
                steps.alone(dve.scalar_tensor_tensor(out=pw[:], in0=pw[:], scalar=1.0, in1=s2[:], op0=ALU.add, op1=ALU.mult))
                steps.alone(dve.tensor_scalar(v[:], v[:], 0.0, None, ALU.max))
                dt = q.dt[:].rearrange("p d b h -> p (d b h)")
                steps.alone(dve.scalar_tensor_tensor(out=dt, in0=pw[:], scalar=2.0, in1=v[:], op0=ALU.mult, op1=ALU.add))
                dve.wait_ge(a_ok, 1)
                steps.alone(dve.tensor_scalar(a[:], a[:], -1.0, None, ALU.mult))
                for d in range(2):
                    steps.did(dve.tensor_tensor(q.da[:, d], q.dt[:, d],
                                                a[:, SH * d:SH * d + SH].unsqueeze(1).to_broadcast([P, NB, SH]), ALU.mult))
                steps.settle()
                assert steps.n == 12
                with dve.Fori(0, NC_ // 2 - 1) as i:
                    rest(2 * i + 1, 1)
                    rest(2 * i + 2, 0)
                rest(NC_ - 1, 1)
                for d in range(2):
                    dve.wait_ge(exps, 2 * d + 2)
                    dd = diff[:, d].rearrange("p b h -> p (b h)")
                    powers.alone(dve.tensor_copy(dd, PS[:, 7, 0:NB * SH]))
                    steps.alone(dve.tensor_tensor(dd, dd, PS[:, 6, 0:NB * SH], ALU.subtract))
                dve.wait_ge(exps, 5)
                dve.tensor_tensor(q.toend[:], diff[:], q.dt[:], ALU.mult).then_inc(a_ok, 1)


def ssm_conv(nc, g, io, hT):
    with Stage(nc, "conv") as st:
        w = st.sb("w", [P, 2, KD, P])
        w_hi = st.sb("w_hi", [P, 2, KD, P], F32R)
        w_lo = st.sb("w_lo", [P, 2, KD, P], F32R)
        W = T + 4
        at_p, at_s = 1, SEQ + 3
        pre = st.sb("pre", [P, 2, W])
        acc = st.sb("acc", [P, 2, W])
        acc2 = st.sb("acc2", [P, W])
        act_ = st.sb("act", [P, 2, W])
        tok = st.sb("tok", [P, 2, NB, P])
        w_in = [st.sem("w_in0"), st.sem("w_in1")]
        hi_ok, lo_ok = st.sem("hi_ok"), st.sem("lo_ok")
        zero, mm, pre_ok, chain = st.sem("zero"), st.sem("mm"), st.sem("pre_ok"), st.sem("chain")
        acc_ok, silu_ok, tp, ta_ok, td_ok = st.sem("acc_ok"), st.sem("silu_ok"), st.sem("tp"), st.sem("ta_ok"), st.sem("td_ok")
        saved_t = [st.sem("saved_t0"), st.sem("saved_t1")]
        saved_c = [st.sem("saved_c0"), st.sem("saved_c1")]
        PS = g.PS
        w_dram = io["ssm_w_in"][0].rearrange("(k p) n -> p k n", p=P)

        h_hi, h_lo = hT

        def turns(eng, body):
            with eng.Fori(0, DI // 512) as i:
                body(4 * i, "x", i)
            body(DI // P, "b", DI // 512)
            body(DI // P + 4, "c", DI // 512 + 1)

        def cols(b):
            return slice(at_p, at_p + P) if b == 0 else slice(at_s + P * (b - 1), at_s + P * b)

        with nc.Block(no_gpsimd_drain=True) as block:
            @block.sync
            def _(sp):
                def load(m, s):
                    sp.dma_start(w[:, s], w_dram[:, :, bass.ds(m * P + DI, P)]).then_inc(w_in[s], 16)

                load(0, 0)
                load(1, 1)
                with sp.Fori(1, MC // 2) as i:
                    for s in range(2):
                        sp.wait_ge(lo_ok, 2 * i + s - 1)
                        load(2 * i + s, s)

            @block.gpsimd
            def _(pool):
                for s in range(2):
                    pool.memset(pre[:, s], 0.0).then_inc(zero, 1)

                def body(m0, kind, i):
                    for v in range(4):
                        if kind != "c":
                            pool.wait_ge(ta_ok, 4 * i + v + 1)
                            pool.wait_ge(td_ok, 8 * i + 2 * v + 2)
                            out = g.xs if kind == "x" else g.btok
                            c = bass.ds(m0 * P + P * v, P) if kind == "x" else slice(P * v, P * v + P)
                            pool.dma_start(out.rearrange("(b p) c -> p b c", p=P)[:, :, c], tok[:, v % 2]
                                           ).then_inc(saved_t[v % 2], 16)
                        if kind != "x":
                            pool.wait_ge(silu_ok, 4 * i + v + 1)
                            out = g.bT if kind == "b" else g.cT
                            s = saved_c[v % 2]
                            pool.dma_start(out[P * v:P * v + P, 0:SEQ], act_[:, v % 2, at_p:at_p + SEQ]).then_inc(s, 16)
                            pool.dma_start(out[P * v:P * v + P, SEQ:T], act_[:, v % 2, at_s:at_s + DEC]).then_inc(s, 16)
                turns(pool, body)
                for s in saved_t:
                    pool.wait_ge(s, 16 * 10)
                for s in saved_c:
                    pool.wait_ge(s, 16 * 8)

            @block.tensor
            def _(pe):
                def project(i, v, first=False):
                    pe.wait_ge(lo_ok, 4 * i + v + 1)
                    if not first:
                        pe.wait_ge(pre_ok, 4 * i + v - 1)
                    for t in range(NT):
                        c = slice(TILE * t, TILE * t + TILE)
                        for k in range(KD):
                            last = exact_products(pe, PS[:, 3 * (v % 2) + t, 0:TILE], (w_hi[:, v % 2, k], w_lo[:, v % 2, k]),
                                                  (h_hi[:, k, c], h_lo[:, k, c]), k == 0, k == KD - 1)
                    last.then_inc(mm, 1)

                def turn(i, v):
                    pe.wait_ge(silu_ok, 4 * i + v + 1)
                    pe.wait_ge(td_ok, 8 * i + 2 * v)
                    pe.wait_ge(ta_ok, 4 * i + v)
                    for b in range(NB):
                        if b == 8:
                            pe.wait_ge(td_ok, 8 * i + 2 * v + 1)
                        last = pe.transpose(PS[:, 6 + b // 4 % 2, P * (b % 4):P * (b % 4) + P], act_[:, v % 2, cols(b)], g.ident[:])
                        if b in (3, 7, 8):
                            last.then_inc(tp, 1)

                def body(m0, kind, i):
                    for v in range(1, 4):
                        project(i, v)
                        if kind != "c":
                            turn(i, v - 1)
                    if kind != "c":
                        project(i + 1, 0)
                        turn(i, 3)
                project(0, 0, first=True)
                turns(pe, body)

            @block.scalar
            def _(act):

                def rounded(i, v, first=False):
                    act.wait_ge(w_in[v % 2], 32 * i + 16 * (v // 2) + 16)
                    if not first:
                        act.wait_ge(mm, 4 * i + v - 1)
                    act.copy(w_hi[:, v % 2], w[:, v % 2]).then_inc(hi_ok, 1)

                def take(i, v, first=False):
                    act.wait_ge(mm, 4 * i + v + 1)
                    if not first:
                        act.wait_ge(acc_ok, 4 * i + v - 1)
                    s, b0 = v % 2, 3 * (v % 2)
                    act.copy(pre[:, s, at_p:at_p + SEQ], PS[:, b0, 0:SEQ])
                    act.copy(pre[:, s, at_s:at_s + TILE - SEQ], PS[:, b0, SEQ:TILE])
                    act.copy(pre[:, s, at_s + TILE - SEQ:at_s + DEC].rearrange("p (t n) -> p t n", t=2),
                             PS[:, b0 + 1:b0 + 3, 0:TILE]).then_inc(pre_ok, 1)

                def silu(i, v, kind, first=False):
                    act.wait_ge(acc_ok, 4 * i + v + 1)
                    if kind != "c" and not first:
                        act.wait_ge(tp, 12 * i + 3 * (v - 1))
                    if kind == "b" and v >= 2:
                        act.wait_ge(saved_c[v % 2], 32)
                    if kind == "c":
                        act.wait_ge(saved_c[v % 2], 64 + 32 * (v // 2))
                    act.activation(act_[:, v % 2, 1:W - 1], acc[:, v % 2, 1:W - 1], ACT.Silu).then_inc(silu_ok, 1)

                def turned(i, v):
                    act.wait_ge(tp, 12 * i + 3 * v + 2)
                    act.wait_ge(saved_t[v % 2], 32 * i + 16 * (v // 2))
                    act.copy(tok[:, v % 2, 4:8], PS[:, 7, :].rearrange("p (b c) -> p b c", c=P)).then_inc(ta_ok, 1)

                def body(m0, kind, i):
                    for v in range(1, 4):
                        if kind != "c" or v < 3:
                            rounded(i + (v + 1) // 4, (v + 1) % 4)
                        take(i, v)
                        if kind != "c":
                            turned(i, v - 1)
                        silu(i, v, kind)
                    if kind != "c":
                        rounded(i + 1, 1)
                        take(i + 1, 0)
                        turned(i, 3)
                        silu(i + 1, 0, "c" if kind == "b" else "x")
                rounded(0, 0, first=True)
                rounded(0, 1, first=True)
                act.wait_ge(zero, 2)
                take(0, 0, first=True)
                silu(0, 0, "x", first=True)
                turns(act, body)

            @block.vector
            def _(dve):
                def rest(i, v):
                    dve.wait_ge(hi_ok, 4 * i + v + 1)
                    dve.tensor_tensor(w_lo[:, v % 2], w[:, v % 2], w_hi[:, v % 2].bitcast(F32), ALU.subtract).then_inc(lo_ok, 1)

                def convolve(m0, i, v, first=False):
                    s = v % 2
                    m = m0 + v
                    n = slice(1, W - 1)
                    wj = [g.convw[:, j, bass.ds(m, 1)] for j in range(3)]
                    steps = Steps(dve, chain, i, 8, 2 * v)
                    dve.wait_ge(pre_ok, 4 * i + v + 1)
                    if not first:
                        dve.wait_ge(silu_ok, 4 * i + v - 1)
                    steps.alone(dve.tensor_scalar(acc[:, s, n], pre[:, s, n], wj[1], g.vcol[:, bass.ds(m + V_CB, 1)],
                                                  ALU.mult, ALU.add))
                    steps.alone(dve.scalar_tensor_tensor(out=acc2[:, n], in0=pre[:, s, 0:W - 2], scalar=wj[0],
                                                         in1=acc[:, s, n], op0=ALU.mult, op1=ALU.add))
                    dve.scalar_tensor_tensor(out=acc[:, s, n], in0=pre[:, s, 2:W], scalar=wj[2],
                                             in1=acc2[:, n], op0=ALU.mult, op1=ALU.add).then_inc(acc_ok, 1)

                def turned(i, v):
                    dve.wait_ge(tp, 12 * i + 3 * v + 1)
                    dve.wait_ge(saved_t[v % 2], 32 * i + 16 * (v // 2))
                    dve.tensor_copy(tok[:, v % 2, 0:4], PS[:, 6, :].rearrange("p (b c) -> p b c", c=P)).then_inc(td_ok, 1)
                    dve.wait_ge(tp, 12 * i + 3 * v + 3)
                    dve.tensor_copy(tok[:, v % 2, 8], PS[:, 6, 0:P]).then_inc(td_ok, 1)

                def body(m0, kind, i):
                    for v in range(1, 4):
                        if kind != "c" or v < 3:
                            rest(i + (v + 1) // 4, (v + 1) % 4)
                        if kind != "c":
                            turned(i, v - 1)
                        convolve(m0, i, v)
                    if kind != "c":
                        rest(i + 1, 1)
                        turned(i, 3)
                        convolve(m0 + 4, i + 1, 0)
                rest(0, 0)
                rest(0, 1)
                convolve(0, 0, 0, first=True)
                turns(dve, body)


def ssm_states(nc, g, io, q):
    NQ = DEC // P
    with Stage(nc, "states") as st:
        x = st.sb("x", [P, 2, 2, DI])
        b_ = st.sb("b", [P, 2, 2, GN])
        xw = st.sb("xw", [P, 2, DI])
        h = st.sb("h", [P, 2, 2, DI])
        raw = st.sb("raw", [P, 2, DI // P, NS])
        fin = st.sb("fin", [P, 2, DI // P, NS])
        x_in = [[st.sem(f"x_in{d}{u}") for u in range(2)] for d in range(2)]
        raw_in, init_mm, init_ok = st.sem("raw_in"), st.sem("init_mm"), st.sem("init_ok")
        xw_ok = [st.sem("xw_ok0"), st.sem("xw_ok1")]
        s_mm = [st.sem("s_mm0"), st.sem("s_mm1")]
        h_ok = [st.sem("h_ok0"), st.sem("h_ok1")]
        dec_ok = [st.sem("dec_ok0"), st.sem("dec_ok1")]
        h_out = [[st.sem(f"h_out{d}{u}") for u in range(2)] for d in range(2)]
        fin_mm, fin_ok, fin_out, zero = st.sem("fin_mm"), st.sem("fin_ok"), st.sem("fin_out"), st.sem("zero")
        PS = g.PS
        NBK = DI // P

        def loop(eng, body):
            with eng.Fori(0, NQ // 2) as i:
                for u in range(2):
                    body(2 * i + u, u, (2 * i + u + 1, i * -2 + NQ - u))
            body(NQ, 0, (0, 0))

        def rows(b, n):
            return bass.ds(b * P, P) if n is not NQ else slice(0, P)

        with nc.Block(no_gpsimd_drain=True) as block:
            @block.sync
            def _(sp):
                for d in range(2):
                    sp.dma_start(raw[:, d], io["state_ssm"][0, 0, d].rearrange("h p n -> (h p) n").rearrange(
                        "(m q) n -> q m n", q=P)).then_inc(raw_in, 16)

                def body(n, u, bs):
                    for d in range(2):
                        sp.wait_ge(s_mm[d], n)
                        sp.dma_start(x[:, d, u], g.xs[rows(bs[d], n), :]).then_inc(x_in[d][u], 16)
                        sp.dma_start(b_[:, d, u], g.btok[rows(bs[d], n), :]).then_inc(x_in[d][u], 16)
                loop(sp, body)

            @block.gpsimd
            def _(pool):
                def body(n, u, bs):
                    for d in range(2):
                        pool.wait_ge(x_in[d][u], 16 * n + 32 - 16 * u)
                        pool.wait_ge(s_mm[d], n + 1)
                        te = q.toend[:, d, bass.ds(bs[d], 1)] if n is not NQ else q.toend[:, d, 0:1]
                        pool.tensor_tensor(xw[:, d].rearrange("p (h c) -> p h c", c=HD),
                                           x[:, d, u].rearrange("p (h c) -> p h c", c=HD),
                                           te.squeeze(1).unsqueeze(2).to_broadcast([P, SH, HD]), ALU.mult).then_inc(xw_ok[d], 1)
                loop(pool, body)

            @block.tensor
            def _(pe):
                pe.wait_ge(raw_in, 32)
                for d in range(2):
                    pe.sem_inc(s_mm[d], 1)
                for d in range(2):
                    for m in range(NBK):
                        last = pe.transpose(PS[:, 4 * d + m // 4, P * (m % 4):P * (m % 4) + P], raw[:, d, m], g.ident[:])
                    last.then_inc(init_mm, 1)

                def body(n, u, bs):
                    for d in range(2):
                        pe.wait_ge(xw_ok[d], n + 1)
                        pe.wait_ge(h_ok[d], n + 1)
                        for k in range(SG):
                            last = pe.matmul(PS[:, 4 * d + k, :], b_[:, d, u, NS * k:NS * k + NS], xw[:, d, 512 * k:512 * k + 512],
                                             start=True, stop=True)
                        last.then_inc(s_mm[d], 1)
                loop(pe, body)
                for d in range(2):
                    pe.wait_ge(h_ok[d], NQ + 3)
                    for m in range(NBK):
                        last = pe.transpose(PS[:, 4 * d + m // 4, P * (m % 4):P * (m % 4) + P], h[:, d, 1, P * m:P * m + P], g.ident[:])
                    last.then_inc(fin_mm, 1)

            @block.vector
            def _(dve):
                for d in range(2):
                    dve.wait_ge(init_mm, d + 1)
                    dve.tensor_copy(h[:, d, 0].rearrange("p (b c) -> p b c", b=4), PS[:, 4 * d:4 * d + 4, :]).then_inc(h_ok[d], 1)

                def body(n, u, bs):
                    for d in range(2):
                        if n is NQ:
                            dve.wait_ge(h_out[d][1], 16 * (NQ // 2))
                            dve.memset(h[:, d, 0], 0.0).then_inc(h_ok[d], 1)
                            dve.wait_ge(h_ok[d], NQ + 2)
                            dec = q.dec[:, d, 0]
                            ready = n + 3
                        else:
                            dec = q.dec[:, d, bass.ds(bs[d], 1)].squeeze(1)
                            dve.wait_ge(h_ok[d], n + 1)
                            ready = n + 2
                            if u == 0:
                                dve.wait_ge(h_out[d][1], 8 * n)
                            else:
                                dve.wait_ge(h_out[d][0], 8 * n + 8)
                        new = h[:, d, 1 - u].rearrange("p (h c) -> p h c", c=HD)
                        dve.tensor_tensor(new, h[:, d, u].rearrange("p (h c) -> p h c", c=HD),
                                          dec.unsqueeze(2).to_broadcast([P, SH, HD]), ALU.mult).then_inc(dec_ok[d], 1)
                        dve.wait_ge(dec_ok[d], n + 1)
                        dve.wait_ge(s_mm[d], n + 2)
                        hb = h[:, d, 1 - u].rearrange("p (b c) -> p b c", b=4)
                        dve.tensor_tensor(hb, hb, PS[:, 4 * d:4 * d + 4, :], ALU.add).then_inc(h_ok[d], 1)
                loop(dve, body)
                for d in range(2):
                    dve.wait_ge(fin_mm, d + 1)
                    dve.tensor_copy(fin[:, d].rearrange("p (b m) n -> p b (m n)", b=4), PS[:, 4 * d:4 * d + 4, :]).then_inc(fin_ok, 1)

            @block.scalar
            def _(act):
                def body(n, u, bs):
                    for d in range(2):
                        if n is NQ:
                            act.wait_ge(h_ok[d], n + 2)
                            act.dma_start(g.hin[d, 0], h[:, d, u]).then_inc(h_out[d][u], 16)
                        else:
                            act.wait_ge(h_ok[d], n + 1)
                            act.dma_start(g.hin[d, bass.ds(bs[d], 1)].squeeze(0), h[:, d, u]).then_inc(h_out[d][u], 16)
                loop(act, body)
                for d in range(2):
                    act.wait_ge(fin_ok, d + 1)
                    act.dma_start(io["new_ssm"][0, 0, d].rearrange("h p n -> (h p) n").rearrange("(m q) n -> q m n", q=P),
                                  fin[:, d]).then_inc(fin_out, 16)
                for d in range(2):
                    act.wait_ge(h_out[d][0], 16 * (NQ // 2 + 1))
                    act.wait_ge(h_out[d][1], 16 * (NQ // 2))
                act.wait_ge(fin_out, 32)


def ssm_outputs(nc, g, io, q):
    with Stage(nc, "ssd") as st:
        x = st.sb("x", [P, 2, DI])
        z = st.sb("z", [P, 2, DI])
        hin = st.sb("hin", [P, 2, 2, DI])
        bT = st.sb("bT", [P, 2, SG, P])
        cT = st.sb("cT", [P, 2, SG, P])
        tri = st.sb("tri", [P, 2, P])
        cb = st.sb("cb", [P, 2, 2, SG, P])
        seg = st.sb("seg", [P, 2, 2, HPG, P])
        ex = st.sb("ex", [P, 2, 2, HPG, P])
        wt = st.sb("wt", [P, 2, 2, HPG, P])
        t1 = st.sb("t1", [P, 2, 512])
        t2 = st.sb("t2", [P, 2, 512])
        t3 = st.sb("t3", [P, 512])
        y = st.sb("y", [P, 2, DI])
        junk = st.sb("junk", [P, DI])
        ld = [st.sem("ld0"), st.sem("ld1")]
        tri_ok, cb_mm, cb_ok = st.sem("tri_ok"), st.sem("cb_mm"), st.sem("cb_ok")
        seg_ok, seg_mm, ex_ok, wt_ok = st.sem("seg_ok"), st.sem("seg_mm"), st.sem("ex_ok"), st.sem("wt_ok")
        yd_mm, off_mm, t_ok, u_ok = st.sem("yd_mm"), st.sem("off_mm"), st.sem("t_ok"), st.sem("u_ok")
        p_ok, y_ok, gt_ok, sq_ok = st.sem("p_ok"), st.sem("y_ok"), st.sem("gt_ok"), st.sem("sq_ok")
        y_out = [st.sem("y_out0"), st.sem("y_out1")]
        PS = g.PS

        def heads(ap):
            return ap.rearrange("p (h c) -> p h c", c=HD)

        def at(t, d, n, h0=0, h1=SH):
            return t[:, d, bass.ds(n, 1), h0:h1].squeeze(1)

        def chunks(eng, body):
            with eng.Fori(0, NB // 2) as i:
                for u in range(2):
                    body(2 * i + u, u, True)
            body(NB - 1, 0, False)

        def loaded(eng, n, u):
            wait_alone(eng, ld[u], 48 * n + 96 - 48 * u)

        with nc.Block(no_gpsimd_drain=True) as block:
            @block.sync
            def _(sp):
                def body(n, u, more):
                    rows = bass.ds(n * P, P)
                    sp.wait_ge(gt_ok, 4 * n)
                    sp.dma_start(bT[:, u], g.bT.rearrange("(k p) t -> p k t", p=P)[:, :, rows]).then_inc(ld[u], 16)
                    sp.dma_start(cT[:, u], g.cT.rearrange("(k p) t -> p k t", p=P)[:, :, rows]).then_inc(ld[u], 16)
                    sp.dma_start(x[:, u], g.xs[rows, :]).then_inc(ld[u], 16)
                    for d in range(2):
                        sp.dma_start(hin[:, u, d], g.hin[d, bass.ds(n, 1)].squeeze(0)).then_inc(ld[u], 16)
                    sp.dma_start(z[:, u], g.z[rows, :]).then_inc(ld[u], 16)
                chunks(sp, body)

            @block.tensor
            def _(pe):
                def products(n, u):
                    loaded(pe, n, u)
                    for k in range(SG):
                        last = pe.matmul(PS[:, 5, P * k:P * k + P], bT[:, u, k], cT[:, u, k], start=True, stop=True)
                    last.then_inc(cb_mm, 1)

                def segments(n, k):
                    for d in range(2):
                        c = 8 * n + 2 * k + d
                        pe.wait_ge(seg_ok, c + 1)
                        if k or d:
                            pe.wait_ge(ex_ok, c - 1)
                        else:
                            pe.wait_ge(ex_ok, 8 * n)
                        for half in range(2):
                            last = pe.matmul(PS[:, 1 + 2 * d + half, :], tri[:, d],
                                             seg[:, k % 2, d, 4 * half:4 * half + 4].rearrange("p h i -> p (h i)"),
                                             start=True, stop=True)
                        last.then_inc(seg_mm, 1)

                pe.wait_ge(tri_ok, 2)
                products(0, 0)
                segments(0, 0)

                def body(n, u, more):
                    for k in range(SG):
                        if k + 1 < SG:
                            segments(n, k + 1)
                        pe.wait_ge(t_ok, 12 * n + max(0, 3 * k - 1))
                        for d in range(2):
                            last = pe.matmul(PS[:, 6 + d, :], cT[:, u, k], hin[:, u, d, 512 * k:512 * k + 512], start=True, stop=True)
                        last.then_inc(off_mm, 1)
                        if more and k == SG - 1:
                            pe.wait_ge(t_ok, 12 * n + 9)
                            products(n + 1, 1 - u)
                            segments(n + 1, 0)
                        pe.wait_ge(wt_ok, 8 * n + 2 * k + 2)
                        for h in range(HPG):
                            for d in range(2):
                                c0 = 512 * k + HD * h
                                last = pe.matmul(PS[:, 5 - 5 * (k % 2), HD * h:HD * h + HD], wt[:, k % 2, d, h],
                                                 x[:, u, c0:c0 + HD], start=(d == 0), stop=(d == 1))
                        last.then_inc(yd_mm, 1)
                chunks(pe, body)

            @block.gpsimd
            def _(pool):
                pool.affine_select(out=tri[:, 0], in_=g.ones[:], compare_op=ALU.is_gt, fill=0.0, base=0,
                                   pattern=[[-1, P]], channel_multiplier=1).then_inc(tri_ok, 1)
                pool.affine_select(out=tri[:, 1], in_=g.ones[:], compare_op=ALU.is_gt, fill=0.0, base=0,
                                   pattern=[[1, P]], channel_multiplier=-1).then_inc(tri_ok, 1)

                def build(n, k, first=False):
                    for d in range(2):
                        c = 8 * n + 2 * k + d
                        if not first:
                            pool.wait_ge(seg_mm, c - 3)
                        pool.tensor_tensor(seg[:, k % 2, d], (g.upper, g.lower)[d][:].unsqueeze(1).to_broadcast([P, HPG, P]),
                                           at(q.da, d, n, HPG * k, HPG * k + HPG).unsqueeze(2).to_broadcast([P, HPG, P]),
                                           ALU.mult).then_inc(seg_ok, 1)

                def finish(n, u, k):
                    c = 4 * n + k
                    if k == 0:
                        loaded(pool, n, u)
                        pool.wait_ge(y_out[u], 8 * n if u == 0 else 8 * n - 8)
                    cs = slice(512 * k, 512 * k + 512)
                    pool.wait_ge(y_ok, c)
                    pool.tensor_tensor(heads(t3[:]), heads(x[:, u, cs]),
                                       q.skip[:, HPG * k:HPG * k + HPG].unsqueeze(2).to_broadcast([P, HPG, HD]),
                                       ALU.mult).then_inc(p_ok, 1)
                    pool.wait_ge(p_ok, 2 * c + 1)
                    pool.wait_ge(t_ok, 3 * c + 2)
                    pool.tensor_tensor(t3[:], t3[:], t2[:, k % 2], ALU.add).then_inc(p_ok, 1)
                    pool.wait_ge(p_ok, 2 * c + 2)
                    pool.wait_ge(t_ok, 3 * c + 3)
                    pool.tensor_tensor(y[:, u, cs], t3[:], t1[:, k % 2], ALU.add).then_inc(y_ok, 1)

                build(0, 0, first=True)
                build(0, 1, first=True)

                def body(n, u, more):
                    for k in range(SG):
                        if k + 2 < SG:
                            build(n, k + 2)
                        elif more:
                            build(n + 1, k - 2)
                        finish(n, u, k)
                chunks(pool, body)

            @block.scalar
            def _(act):
                def exps(n, k, first=False):
                    for d in range(2):
                        c = 8 * n + 2 * k + d
                        act.wait_ge(seg_mm, c + 1)
                        if not first:
                            act.wait_ge(wt_ok, c - 3 if k > 1 else 8 * n)
                        act.activation(ex[:, k % 2, d].rearrange("p (b h) i -> p b (h i)", b=2), PS[:, 1 + 2 * d:3 + 2 * d, :],
                                       ACT.Exp).then_inc(ex_ok, 1)

                exps(0, 0, first=True)

                def body(n, u, more):
                    for k in range(1, SG):
                        exps(n, k)
                    if more:
                        exps_next(n + 1)
                    act.wait_ge(gt_ok, 4 * n + 8)
                    act.wait_ge(sq_ok, n)
                    act.activation(junk[:], y[:, u], ACT.Square, accum_out=q.ssq[:, bass.ds(n, 1)]).then_inc(sq_ok, 1)
                    act.dma_start(g.y[bass.ds(n * P, P), :], y[:, u]).then_inc(y_out[u], 16)

                def exps_next(n):
                    for d in range(2):
                        c = 8 * n + d
                        act.wait_ge(seg_mm, c + 1)
                        act.wait_ge(wt_ok, c - 3)
                        act.activation(ex[:, 0, d].rearrange("p (b h) i -> p b (h i)", b=2), PS[:, 1 + 2 * d:3 + 2 * d, :],
                                       ACT.Exp).then_inc(ex_ok, 1)
                chunks(act, body)
                act.wait_ge(y_out[0], 16 * 5)
                act.wait_ge(y_out[1], 16 * 4)

            @block.vector
            def _(dve):
                def masked(n, u):
                    dve.wait_ge(cb_mm, n + 1)
                    for d in range(2):
                        dve.tensor_tensor(cb[:, u, d], PS[:, 5, :].rearrange("p (k i) -> p k i", k=SG),
                                          (g.upper, g.lower)[d][:].unsqueeze(1).to_broadcast([P, SG, P]), ALU.mult).then_inc(cb_ok, 1)

                def weights(n, u, k, free):
                    dve.wait_ge(cb_ok, 2 * n + 2)
                    dve.wait_ge(yd_mm, free)
                    for d in range(2):
                        c = 8 * n + 2 * k + d
                        dve.wait_ge(ex_ok, c + 1)
                        for h in range(HPG):
                            hh = HPG * k + h
                            last = dve.scalar_tensor_tensor(out=wt[:, k % 2, d, h], in0=ex[:, k % 2, d, h],
                                                            scalar=at(q.dt, d, n, hh, hh + 1), in1=cb[:, u, d, k],
                                                            op0=ALU.mult, op1=ALU.mult)
                        last.then_inc(wt_ok, 1)

                def parts(n, k):
                    c = 4 * n + k
                    dve.wait_ge(off_mm, c + 1)
                    if k < 2:
                        dve.wait_ge(y_ok, 4 * n)
                    else:
                        dve.wait_ge(y_ok, c - 1)
                    for d, t in ((0, t1), (1, t2)):
                        dve.tensor_tensor(heads(t[:, k % 2]), heads(PS[:, 6 + d, :]),
                                          at(q.grow, d, n, HPG * k, HPG * k + HPG).unsqueeze(2).to_broadcast([P, HPG, HD]),
                                          ALU.mult).then_inc(t_ok, 1)
                    dve.wait_ge(yd_mm, c + 1)
                    dve.wait_ge(t_ok, 3 * c + 2)
                    dve.tensor_tensor(t1[:, k % 2], t1[:, k % 2], PS[:, 5 - 5 * (k % 2), :], ALU.add).then_inc(t_ok, 1)

                def gate(n, u, k):
                    cs = slice(512 * k, 512 * k + 512)
                    dve.wait_ge(y_ok, 4 * n + k + 1)
                    dve.tensor_tensor(y[:, u, cs], y[:, u, cs], z[:, u, cs], ALU.mult).then_inc(gt_ok, 1)

                dve.sem_inc(gt_ok, SG)
                masked(0, 0)
                weights(0, 0, 0, 0)

                def body(n, u, more):
                    for k in range(SG):
                        if k + 1 < SG:
                            weights(n, u, k + 1, 4 * n + max(0, k))
                        elif more:
                            masked(n + 1, 1 - u)
                            weights(n + 1, 1 - u, 0, 4 * n + 3)
                        parts(n, k)
                        if k:
                            gate(n, u, k - 1)
                    gate(n, u, SG - 1)
                chunks(dve, body)


def ssm_out(nc, g, io, q):
    def take(st, mm):
        KI = DI // P
        y = st.sb("y", [P, 2, DI])
        yT = st.sb("yT", [P, 2, KI, P])
        root = st.sb("root", [P, NB])
        rstd = st.sb("rstd", [P, NB])
        ms_ok, root_ok, rstd_ok = st.sem("ms_ok"), st.sem("root_ok"), st.sem("rstd_ok")
        y_in = [st.sem("y_in0"), st.sem("y_in1")]
        yn_ok, tp, ya_ok, yT_ok = st.sem("yn_ok"), st.sem("tp"), st.sem("ya_ok"), st.sem("yT_ok")
        PS = g.PS

        def sync(sp, n, u, b, grp):
            rows = bass.ds(b * P, P) if grp else slice(0, P)
            sp.wait_ge(tp, 2 * n)
            sp.dma_start(y[:, u], g.y[rows, :]).then_inc(y_in[u], 16)

        def scalar(act, n, u, b, grp):
            act.wait_ge(rstd_ok, 1)
            act.wait_ge(y_in[u], 8 * n + 16 - 8 * u)
            sc = rstd[:, bass.ds(b, 1)] if grp else rstd[:, 0:1]
            act.activation(y[:, u], y[:, u], ACT.Copy, scale=sc).then_inc(yn_ok, 1)
            act.wait_ge(tp, 2 * n + 4)
            act.wait_ge(mm, n)
            for k in range(KI // 2, KI):
                last = act.activation(yT[:, u, k], PS[:, 4 + k // 4, P * (k % 4):P * (k % 4) + P], ACT.Copy,
                                      scale=g.vcol[:, V_SG + k:V_SG + k + 1])
            last.then_inc(ya_ok, 1)

        def tensor(pe, n, u):
            if isinstance(n, int) and n == 0:
                pe.sem_inc(tp, 2)
            wait_alone(pe, yn_ok, n + 1)
            pe.wait_ge(yT_ok, n)
            for k in range(KI):
                last = pe.transpose(PS[:, 4 + k // 4, P * (k % 4):P * (k % 4) + P], y[:, u, P * k:P * k + P], g.ident[:])
                if k % 8 == 7:
                    last.then_inc(tp, 1)

        def vector(dve, n, u):
            dve.wait_ge(tp, 2 * n + 3)
            dve.wait_ge(mm, n)
            for k in range(KI // 2):
                last = dve.tensor_scalar(yT[:, u, k], PS[:, 4 + k // 4, P * (k % 4):P * (k % 4) + P],
                                         g.vcol[:, V_SG + k:V_SG + k + 1], None, ALU.mult)
            last.then_inc(ms_ok, 1)
            dve.wait_ge(ms_ok, n + 2)
            dve.wait_ge(ya_ok, n + 1)
            dve.sem_inc(yT_ok, 1)

        def before_vector(dve):
            dve.tensor_scalar(q.ssq[:], q.ssq[:], 1.0 / DI, EPS, ALU.mult, ALU.add).then_inc(ms_ok, 1)
            dve.wait_ge(root_ok, 1)
            dve.reciprocal(rstd[:], root[:]).then_inc(rstd_ok, 1)

        def before_scalar(act):
            act.wait_ge(ms_ok, 1)
            act.activation(root[:], q.ssq[:], ACT.Sqrt).then_inc(root_ok, 1)
        return yT, yT_ok, {"sync": sync, "scalar": scalar, "tensor": tensor, "vector": vector,
                           "before_vector": before_vector, "before_scalar": before_scalar}
    project_out(nc, g, "wout", 1, DI // P, io["ssm_w_out"][0], take)


def final_norm(nc, g, io):
    with Stage(nc, "final") as st:
        x = st.sb("x", [P, NB, D])
        junk = st.sb("junk", [P, D])
        gain = st.sb("gain", [P, D])
        ssq = st.sb("ssq", [P, NB])
        root = st.sb("root", [P, NB])
        x_in, sq, ms, rt, rs = st.sem("x_in"), st.sem("sq"), st.sem("ms"), st.sem("rt"), st.sem("rs")
        y_ok, y_out = st.sem("y_ok"), st.sem("y_out")
        with nc.Block(no_gpsimd_drain=True) as block:
            @block.sync
            def _(sp):
                sp.dma_start(x[:], g.res.rearrange("(b p) d -> p b d", p=P)).then_inc(x_in, 16)
                sp.dma_start(gain[:], io["final_norm_g"].partition_broadcast(P)).then_inc(x_in, 16)
                sp.wait_ge(y_ok, 1)
                sp.dma_start(io["y_prompt"][0], x[:, 0]).then_inc(y_out, 16)
                for b in range(1, NB):
                    sp.wait_ge(y_ok, b + 1)
                    sp.dma_start(io["y_sample"][0, P * (b - 1):P * b], x[:, b]).then_inc(y_out, 16)
                sp.wait_ge(y_out, 16 * NB)

            @block.scalar
            def _(act):
                act.wait_ge(x_in, 32)
                for b in range(NB):
                    if b:
                        act.wait_ge(sq, b)
                    act.activation(junk[:], x[:, b], ACT.Square, accum_out=ssq[:, b:b + 1]).then_inc(sq, 1)
                act.wait_ge(ms, 1)
                act.activation(root[:], ssq[:], ACT.Sqrt).then_inc(rt, 1)

            @block.vector
            def _(dve):
                dve.wait_ge(sq, NB)
                dve.tensor_scalar(ssq[:], ssq[:], 1.0 / D, EPS, ALU.mult, ALU.add).then_inc(ms, 1)
                dve.wait_ge(rt, 1)
                dve.reciprocal(root[:], root[:]).then_inc(rs, 1)
                dve.wait_ge(rs, 1)
                for b in range(NB):
                    dve.scalar_tensor_tensor(out=x[:, b], in0=x[:, b], scalar=root[:, b:b + 1], in1=gain[:],
                                             op0=ALU.mult, op1=ALU.mult).then_inc(y_ok, 1)


class Shared:
    pass


def build(nc, io):
    g = Shared()
    ctx = ExitStack()
    with ctx:
        def sb(name, shape, dt=F32):
            return ctx.enter_context(nc.sbuf_tensor(name, shape, dt))
        g.PS = ctx.enter_context(nc.psum_tensor("banks", [P, 8, 512], F32))
        g.ident = sb("ident", [P, P])
        g.ones = sb("ones", [P, P])
        g.fold = sb("fold", [P, P])
        g.upper = sb("upper", [P, P])
        g.lower = sb("lower", [P, P])
        g.vcol = sb("vcol", [P, V_ALL])
        g.convw = sb("convw", [P, 3, MC])
        g.modc = sb("modc", [P, DEPTH, 48, 2])
        g.gain = sb("gain", [P, DEPTH, 2, KD, NB])
        g.shift = sb("shift", [P, DEPTH, 2, KD, NB])
        g.gate_row = sb("gate_row", [P, 2, D])
        g.gate_bias = sb("gate_bias", [P, DEPTH, D])
        g.cond = sb("cond", [P, KD, 2])
        g.bcol = sb("bcol", [P, 96])
        g.aff = sb("aff", [NE, T])
        g.row_s = sb("row_s", [P, NE], U32)
        g.row_p = sb("row_p", [CAP_P, NE], U32)
        g.gate_s = sb("gate_s", [P, NE])
        g.gate_p = sb("gate_p", [CAP_P, NE])
        g.res = nc.dram_tensor("res", [T, D], F32, kind="Internal").ap()
        g.normed = nc.dram_tensor("normed", [T, D], F32, kind="Internal").ap()
        g.z, g.xs, g.y, g.btok, g.bT, g.cT, g.hin = (
            nc.dram_tensor("d_" + name, shape, F32, kind="Internal").ap()
            for name, shape in (("z", [T, DI]), ("xs", [T, DI]), ("y", [T, DI]), ("btok", [T, GN]),
                                ("bT", [GN, T]), ("cT", [GN, T]), ("hin", [2, NB, P, DI])))

        start(nc, g, io)
        m = Shared()
        with ExitStack() as c:
            def mb(name, shape):
                return c.enter_context(nc.sbuf_tensor(name, shape, F32))
            m.oT = mb("oT", [P, HEADS, T])
            m.qlat = mb("qlat", [P, KQ, T])
            m.ckv = mb("ckv", [P, KKV, KEYS])
            m.k2 = mb("k2", [P, KEYS])
            m.rope = mb("rope", [P, T])
            with nc.sbuf_tensor("hT0", [P, KD, T], F32) as hT:
                norm(nc, g, io, 0, 0, hT)
                mla_project(nc, g, io, hT, m)
            mla_heads(nc, g, io, m)
            mla_out(nc, g, io, m)
        norm(nc, g, io, 0, 1)
        choose(nc, g, io, 0)
        experts(nc, g, io, 0)
        q = Shared()
        with ExitStack() as c:
            def qb(name, shape):
                return c.enter_context(nc.sbuf_tensor(name, shape, F32))
            q.dt, q.da, q.grow, q.toend, q.dec = (qb("q" + n, [P, 2, NB, SH]) for n in ("dt", "da", "grow", "toend", "dec"))
            q.skip = qb("qskip", [P, SH])
            q.ssq = qb("qssq", [P, NB])
            with nc.sbuf_tensor("h_hi", [P, KD, T], F32R) as h_hi, nc.sbuf_tensor("h_lo", [P, KD, T], F32R) as h_lo:
                hT = (h_hi, h_lo)
                norm(nc, g, io, 1, 0, hT)
                ssm_gate_and_steps(nc, g, io, hT, q)
                ssm_conv(nc, g, io, hT)
            ssm_states(nc, g, io, q)
            ssm_outputs(nc, g, io, q)
            ssm_out(nc, g, io, q)
        norm(nc, g, io, 1, 1)
        choose(nc, g, io, 1)
        experts(nc, g, io, 1)
        final_norm(nc, g, io)


_INS = ["x_prompt", "x_sample", "cache_ckv", "cache_krope", "state_ssm", "c", "c_ctx", "w_mod", "b_mod", "norm1_g",
        "norm2_g", "final_norm_g", "mla_w_dq", "mla_q_norm_g", "mla_w_uq", "mla_w_dkv", "mla_kv_norm_g", "mla_w_ukv",
        "mla_w_o", "ssm_w_in", "ssm_conv_w", "ssm_conv_b", "ssm_dt_bias", "ssm_a_log", "ssm_d_skip", "ssm_norm_g",
        "ssm_w_out", "moe_w_router", "moe_w_gate", "moe_w_up", "moe_w_down"]
_OUTS = [("y_prompt", (1, SEQ, D)), ("y_sample", (1, DEC, D)), ("new_ckv", (1, 1, SEQ, KVR)),
         ("new_krope", (1, 1, SEQ, ROPE)), ("new_ssm", (1, 1, 2, SH, HD, NS))]


def rope_table():
    rows = DEC // GRID_W
    row = np.repeat(np.arange(rows), GRID_W).astype(np.float32)
    col = np.tile(np.arange(GRID_W), rows).astype(np.float32)
    pairs = ROPE // 4
    inv = np.float32(THETA) ** (-np.arange(pairs, dtype=np.float32) / np.float32(pairs))
    ang = np.concatenate([row[:, None] * inv, col[:, None] * inv], axis=-1).astype(np.float32)
    tab = np.zeros((P, T), np.float32)
    tab[0:ROPE, 0:SEQ] = 1.0
    cos, sin = np.cos(ang).T, np.sin(ang).T
    tab[:, SEQ:] = np.concatenate([cos, cos, -sin, sin], axis=0)
    return tab


def kernel(**inputs):
    import numpy as _np
    import concourse.bacc as _bacc
    from concourse.bass_utils import run_bass_kernel_spmd as _run

    nc = _bacc.Bacc("TRN2", target_bir_lowering=False, num_devices=1)
    drams, arrays = {}, {}
    for name in _INS:
        a = _np.ascontiguousarray(inputs[name])
        arrays["in_" + name] = a
        drams[name] = nc.dram_tensor("in_" + name, a.shape, F32, kind="ExternalInput").ap()
    tab = rope_table()
    arrays["in_rope"] = tab
    drams["rope"] = nc.dram_tensor("in_rope", tab.shape, F32, kind="ExternalInput").ap()
    for name, shape in _OUTS:
        drams[name] = nc.dram_tensor("out_" + name, shape, F32, kind="ExternalOutput").ap()
    build(nc, drams)
    r = _run(nc, [arrays], core_ids=[0])
    return tuple(r.results[0]["out_" + name] for name, _ in _OUTS)
```

```python
from contextlib import ExitStack

import numpy as np

import concourse.bass as bass
from concourse import mybir

F32 = mybir.dt.float32
F32R = mybir.dt.float32r
U32 = mybir.dt.uint32
ACT = mybir.ActivationFunctionType
ALU = mybir.AluOpType
X = mybir.AxisListType.X

P = 128
D = 1024
KD = D // P
SEQ, DEC = 128, 1024
T = SEQ + DEC
NB = T // P
TILE = 384
NT = T // TILE
DEPTH = 2
EPS = 1e-6
HEADS, NOPE, ROPE, VD = 8, 128, 64, 128
QR, KVR = 384, 256
KQ, KKV = QR // P, KVR // P
PAST = 128
KEYS = T + PAST
SAMPLE_KEYS = PAST + DEC
SCALE = (NOPE + ROPE) ** -0.5
GRID_W = 64
THETA = 10000.0
DI = 2048
HD = 64
SH = DI // HD
SG = 4
NS = 128
HPG = SH // SG
GN = SG * NS
CONV = DI + 2 * GN
MC = CONV // P
IN_DIM = DI + CONV + 2 * SH
NE = 16
FF = 1024
CAP_S = 2 * DEC // NE
CAP_P = 2 * SEQ // NE
CAP = CAP_S + CAP_P
V_N1, V_N2, V_CTX, V_C, V_QG, V_KVG, V_SG, V_CB = 0, 16, 32, 40, 48, 51, 53, 69
V_ALL = V_CB + MC


class Steps:

    def __init__(self, eng, sem, turn=0, per_turn=0, before=0):
        self.eng, self.sem, self.base, self.n = eng, sem, turn * per_turn + before, 0

    def did(self, ins):
        ins.then_inc(self.sem, 1)
        self.n += 1

    def settle(self):
        self.eng.wait_ge(self.sem, self.base + self.n)

    def alone(self, ins):
        self.did(ins)
        self.settle()


def wait_alone(eng, sem, value):
    eng.wait_ge(sem, value)
    eng.nop(nofuse=True)


def exact_products(pe, out, left, right, first=True, last=True):
    (lh, ll), (rh, rl) = left, right
    pe.matmul(out, lh, rh, start=first, stop=False)
    pe.matmul(out, lh, rl, start=False, stop=False)
    return pe.matmul(out, ll, rh, start=False, stop=last)


class Stage:

    def __init__(self, nc, name):
        self.nc, self.name = nc, name
        self.ctx = ExitStack()
        self.sems = []

    def __enter__(self):
        return self

    def sb(self, name, shape, dt=F32):
        return self.ctx.enter_context(self.nc.sbuf_tensor(f"{self.name}_{name}", shape, dt))

    def sem(self, name):
        s = self.nc.alloc_semaphore(f"{self.name}_{name}")
        self.sems.append(s)
        return s

    def __exit__(self, *e):
        if e[0] is None:
            self.nc.clear_and_free_semaphores(self.sems)
            self.nc.all_engine_barrier()
        self.ctx.__exit__(*e)


def bcast_rows(ap, n):
    return ap.partition_broadcast(n)


class Modulation:

    CH = 6 * D // 512

    def __init__(self, st, g, io, l):
        self.g, self.io, self.l = g, io, l
        self.w = st.sb("m_w", [P, 4, KD, 512])
        self.row = st.sb("m_row", [2, 4, 512])
        self.rows = st.sb("m_rows", [2, 6 * D])
        self.sel = st.sb("m_sel", [2, 2, P])
        self.w_in = [st.sem(f"m_w_in{i}") for i in range(4)]
        self.row_mm, self.row_ok = st.sem("m_row_mm"), st.sem("m_row_ok")
        self.col_mm, self.col_ok = st.sem("m_col_mm"), st.sem("m_col_ok")
        self.sel_ok, self.gate_mm, self.done = st.sem("m_sel_ok"), st.sem("m_gate_mm"), st.sem("m_done")

    def sync(self, sp):
        def load(u, c0):
            sp.dma_start(self.w[:, u], self.io["w_mod"][self.l].rearrange("(k p) n -> p k n", p=P)[
                :, :, bass.ds(c0 + u * 512, 512)]).then_inc(self.w_in[u], 16)

        for u in range(4):
            load(u, 0)
        with sp.Fori(1, self.CH // 4) as i:
            for u in range(4):
                sp.wait_ge(self.row_mm, 4 * i + u - 3)
                load(u, 2048 * i)

    def tensor(self, pe):
        PS, g = self.g.PS, self.g

        def columns(i, u):
            pe.wait_ge(self.row_ok, 4 * i + u + 1)
            wait_alone(pe, self.col_ok, 4 * i + max(0, u - 1))
            for m in range(4):
                last = pe.transpose(PS[:, 3 + u % 2, 2 * m:2 * m + 2], self.row[:, u, P * m:P * m + P], g.ident[0:2, 0:2])
            last.then_inc(self.col_mm, 1)

        with pe.Fori(0, self.CH // 4) as i:
            for u in range(4):
                pe.wait_ge(self.w_in[u], 16 * i + 16)
                pe.wait_ge(self.row_ok, 4 * i + max(0, u - 1))
                for k in range(KD):
                    last = pe.matmul(PS[0:2, 1 + u % 2, :], g.cond[:, k, :], self.w[:, u, k, :], start=(k == 0), stop=(k == KD - 1))
                last.then_inc(self.row_mm, 1)
                if u:
                    columns(i, u - 1)
            columns(i, 3)
        pe.wait_ge(self.sel_ok, 1)
        pe.wait_ge(self.row_ok, self.CH)
        pe.wait_ge(self.col_ok, self.CH)
        for j in range(2):
            for half in range(2):
                c0 = 2 * D + 512 * half
                pe.matmul(PS[:, 1 + 2 * j + half, :], self.sel[:, j], self.rows[:, c0:c0 + 512], start=True,
                          stop=True).then_inc(self.gate_mm, 1)

    def scalar(self, act):
        PS, g, l = self.g.PS, self.g, self.l

        def rows(i, u):
            act.wait_ge(self.row_mm, 4 * i + u + 1)
            act.wait_ge(self.col_mm, 4 * i)
            act.copy(self.rows[:, bass.ds(2048 * i + 512 * u, 512)], PS[0:2, 1 + u % 2, :])
            act.copy(self.row[:, u], PS[0:2, 1 + u % 2, :]).then_inc(self.row_ok, 1)

        def columns(i, u):
            act.wait_ge(self.col_mm, 4 * i + u + 1)
            for m in range(4):
                n = 16 * i + 4 * u + m
                last = act.activation(g.modc[:, l, bass.ds(n, 1), :].squeeze(1), PS[:, 3 + u % 2, 2 * m:2 * m + 2], ACT.Identity,
                                      bias=g.bcol[:, bass.ds(n + 48 * l, 1)])
            last.then_inc(self.col_ok, 1)

        with act.Fori(0, self.CH // 4) as i:
            for u in range(4):
                rows(i, u)
                if u:
                    columns(i, u - 1)
            columns(i, 3)

    def vector(self, dve):
        PS, g, l = self.g.PS, self.g, self.l
        dve.tensor_copy(self.sel[:], g.ident[0:2, 0:2].unsqueeze(2).to_broadcast([2, 2, P])).then_inc(self.sel_ok, 1)
        dve.wait_ge(self.col_ok, self.CH)
        for w, at in ((0, V_N1), (1, V_N2)):
            for b0, b1, j in ((0, 1, 0), (1, NB, 1)):
                m0, nb = 24 * w, b1 - b0
                dve.scalar_tensor_tensor(
                    out=g.gain[:, l, w, :, b0:b1],
                    in0=g.modc[:, l, m0 + 8:m0 + 16, j:j + 1].to_broadcast([P, KD, nb]), scalar=1.0,
                    in1=g.vcol[:, at + 8 * l:at + 8 * l + 8].unsqueeze(2).to_broadcast([P, KD, nb]),
                    op0=ALU.add, op1=ALU.mult).then_inc(self.done, 1)
                dve.tensor_copy(g.shift[:, l, w, :, b0:b1],
                                g.modc[:, l, m0:m0 + 8, j:j + 1].to_broadcast([P, KD, nb])).then_inc(self.done, 1)
        for n in range(4):
            dve.wait_ge(self.gate_mm, n + 1)
            c0 = 512 * (n % 2)
            dve.tensor_tensor(g.gate_row[:, n // 2, c0:c0 + 512], PS[:, 1 + n, :], g.gate_bias[:, l, c0:c0 + 512],
                              ALU.add).then_inc(self.done, 1)


def start(nc, g, io):
    with Stage(nc, "start") as st:
        rows_a = st.sb("rows_a", [2 * 48, P])
        rows_b = st.sb("rows_b", [V_ALL, P])
        rows_c = st.sb("rows_c", [MC, 3 * P])
        small, copied, made = st.sem("small"), st.sem("copied"), st.sem("made")
        turned, cols, cond_ok = st.sem("turned"), st.sem("cols"), st.sem("cond_ok")
        mod = Modulation(st, g, io, 0)
        PS = g.PS

        with nc.Block(no_gpsimd_drain=True) as block:
            @block.sync
            def _(sp):
                sp.wait_ge(small, 16 * 10)
                mod.sync(sp)

            @block.scalar
            def _(act):
                act.dma_start(rows_a[:], io["b_mod"].rearrange("l (m p) -> (l m) p", p=P)).then_inc(small, 16)
                for at, name in ((V_N1, "norm1_g"), (V_N2, "norm2_g"), (V_C, "c"), (V_QG, "mla_q_norm_g"),
                                 (V_KVG, "mla_kv_norm_g"), (V_SG, "ssm_norm_g"), (V_CB, "ssm_conv_b")):
                    rows = io[name].rearrange("l (m p) -> (l m) p", p=P)
                    act.dma_start(rows_b[at:at + rows.shape[0], :], rows).then_inc(small, 16)
                act.dma_start(rows_b[V_CTX:V_CTX + KD, :], io["c_ctx"].rearrange("(m p) -> m p", p=P)).then_inc(small, 16)
                act.dma_start(rows_c[:], io["ssm_conv_w"][0].rearrange("(m p) j -> m (p j)", p=P)).then_inc(small, 16)
                act.wait_ge(small, 16 * 10)
                for l in range(DEPTH):
                    act.dma_start(g.gate_bias[:, l], io["b_mod"][l, 2 * D:3 * D].partition_broadcast(P)).then_inc(copied, 16)
                act.wait_ge(cols, 5)
                act.activation(g.cond[:, :, 0], g.vcol[:, V_CTX:V_CTX + KD], ACT.Silu).then_inc(cond_ok, 1)
                act.activation(g.cond[:, :, 1], g.vcol[:, V_C:V_C + KD], ACT.Silu).then_inc(cond_ok, 1)
                mod.scalar(act)
                act.wait_ge(copied, 32)

            @block.gpsimd
            def _(pool):
                pool.memset(g.ident[:], 0.0).then_inc(made, 1)
                pool.memset(g.ones[:], 1.0).then_inc(made, 1)
                pool.wait_ge(made, 2)
                pool.affine_select(out=g.ident[:], in_=g.ident[:], compare_op=ALU.not_equal, fill=1.0, base=0,
                                   pattern=[[-1, P]], channel_multiplier=1).then_inc(made, 1)
                pool.memset(g.fold[:], 0.0).then_inc(made, 1)
                for n, base in enumerate((0, 64, -64)):
                    pool.wait_ge(made, 4 + n)
                    pool.affine_select(out=g.fold[:], in_=g.fold[:], compare_op=ALU.not_equal, fill=1.0, base=base,
                                       pattern=[[-1, P]], channel_multiplier=1).then_inc(made, 1)
                pool.affine_select(out=g.upper[:], in_=g.ones[:], compare_op=ALU.is_ge, fill=0.0, base=0,
                                   pattern=[[1, P]], channel_multiplier=-1).then_inc(made, 1)
                pool.affine_select(out=g.lower[:], in_=g.ones[:], compare_op=ALU.is_ge, fill=0.0, base=0,
                                   pattern=[[-1, P]], channel_multiplier=1).then_inc(made, 1)

            @block.tensor
            def _(pe):
                pe.wait_ge(small, 16 * 10)
                pe.wait_ge(made, 3)
                pe.transpose(PS[:, 0, 0:96], rows_a[:], g.ident[0:96, 0:96]).then_inc(turned, 1)
                pe.transpose(PS[:, 1, 0:V_ALL], rows_b[:], g.ident[0:V_ALL, 0:V_ALL]).then_inc(turned, 1)
                for j in range(3):
                    pe.transpose(PS[:, 2 + j, 0:MC], rows_c[:, j:3 * P:3], g.ident[0:MC, 0:MC]).then_inc(turned, 1)
                pe.wait_ge(cols, 5)
                pe.wait_ge(cond_ok, 2)
                mod.tensor(pe)

            @block.vector
            def _(dve):
                dve.wait_ge(turned, 5)
                dve.tensor_copy(g.bcol[:], PS[:, 0, 0:96]).then_inc(cols, 1)
                dve.tensor_copy(g.vcol[:], PS[:, 1, 0:V_ALL]).then_inc(cols, 1)
                for j in range(3):
                    dve.tensor_copy(g.convw[:, j, :], PS[:, 2 + j, 0:MC]).then_inc(cols, 1)
                dve.wait_ge(made, 3)
                dve.wait_ge(copied, 32)
                mod.vector(dve)


def norm(nc, g, io, layer, which, hT=None):
    with Stage(nc, f"norm{layer}{which}") as st:
        x = st.sb("x", [P, NB, D])
        junk = st.sb("junk", [P, D])
        ssq = st.sb("ssq", [P, NB])
        root = st.sb("root", [P, NB])
        rstd = st.sb("rstd", [P, NB])
        xn = st.sb("xn", [P, 3, D])
        x_in = [st.sem(f"x_in{i}") for i in range(3)]
        sq = st.sem("sq")
        ms = st.sem("ms")
        rt = st.sem("rt")
        rs = st.sem("rs")
        xn_ok = st.sem("xn_ok")
        turned = st.sem("turned")
        ev_a = st.sem("ev_a")
        ev_d = st.sem("ev_d")
        PS = g.PS
        router = which == 1
        first = layer == 0 and not router
        split = isinstance(hT, tuple)
        if router or split:
            hs = st.sb("hs", [P, 3, KD, P])
        if split:
            hi_ok, lo_ok = st.sem("hi_ok"), st.sem("lo_ok")
        if router:
            wr = st.sb("wr", [P, KD, NE])
            mx = st.sb("mx", [P, NB])
            ex = st.sb("ex", [P, NB, NE])
            tot = st.sb("tot", [P, NB])
            inv = st.sb("inv", [P, NB])
            pr = st.sb("pr", [P, NB, NE])
            wr_in = st.sem("wr_in")
            saved = [st.sem(f"saved{u}") for u in range(3)]
            lg = st.sem("lg")
            less = st.sb("less", [P, NB, NE])
            less_ok = st.sem("less_ok")
            ex_ok = st.sem("ex_ok")
            chain = st.sem("chain")
            pr_ok = st.sem("pr_ok")
            pt = st.sem("pt")
            af = st.sem("af")

        def h_out(u, i, k0, k1):
            if router or split:
                return hs[:, u, k0:k1, :]
            return hT[:, k0:k1, bass.ds(i * 3 * P + u * P, P)]

        with nc.Block(no_gpsimd_drain=True) as block:
            @block.sync
            def _(sp):
                for i in range(3):
                    if first:
                        if i == 0:
                            sp.dma_start(x[:, 0], io["x_prompt"][0]).then_inc(x_in[0], 16)
                        b0 = max(1, 3 * i)
                        sp.dma_start(x[:, b0:3 * i + 3], io["x_sample"][0].rearrange("(b p) d -> p b d", p=P)[:, b0 - 1:3 * i + 2]
                                     ).then_inc(x_in[i], 16)
                    else:
                        sp.dma_start(x[:, 3 * i:3 * i + 3], g.res.rearrange("(b p) d -> p b d", p=P)[:, 3 * i:3 * i + 3]
                                     ).then_inc(x_in[i], 16)
                if router:
                    sp.dma_start(wr[:], io["moe_w_router"][layer].rearrange("(k p) e -> p k e", p=P)).then_inc(wr_in, 16)
                    with sp.Fori(0, 3) as i:
                        for u in range(3):
                            sp.wait_ge(xn_ok, 3 * i + u + 1)
                            sp.dma_start(g.normed[bass.ds(i * 3 * P + u * P, P), :], xn[:, u]).then_inc(saved[u], 16)
                    for u in range(3):
                        sp.wait_ge(saved[u], 48)

            @block.scalar
            def _(act):
                for b in range(NB):
                    if b % 3 == 0:
                        act.wait_ge(x_in[b // 3], 32 if first and b == 0 else 16)
                    if b:
                        act.wait_ge(sq, b)
                    act.activation(junk[:], x[:, b], ACT.Square, accum_out=ssq[:, b:b + 1]).then_inc(sq, 1)
                act.wait_ge(ms, 1)
                act.activation(root[:], ssq[:], ACT.Sqrt).then_inc(rt, 1)
                with act.Fori(0, 3) as i:
                    for u in range(3):
                        act.wait_ge(turned, 3 * i + u + 1)
                        if router:
                            act.wait_ge(lg, i)
                        if split:
                            act.wait_ge(lo_ok, 3 * i)
                        for k in range(4, KD):
                            act.activation(h_out(u, i, k, k + 1).squeeze(1), PS[:, 2 * u + 1, P * (k - 4):P * (k - 3)],
                                           ACT.Identity,
                                           scale=g.gain[:, layer, which, k, bass.ds(3 * i + u, 1)],
                                           bias=g.shift[:, layer, which, k, bass.ds(3 * i + u, 1)]).then_inc(ev_a, 1)
                        if split:
                            act.wait_ge(ev_a, 12 * i + 4 * u + 4)
                            act.wait_ge(ev_d, 12 * i + 4 * u + 4)
                            act.copy(hT[0][:, :, bass.ds(i * 3 * P + u * P, P)], hs[:, u]).then_inc(hi_ok, 1)
                if router:
                    act.wait_ge(less_ok, 1)
                    act.activation(ex[:], less[:], ACT.Exp).then_inc(ex_ok, 1)
                    act.wait_ge(pt, 2)
                    act.copy(g.aff[:, 4 * P:8 * P], PS[0:NE, 1, :]).then_inc(af, 1)

            @block.vector
            def _(dve):
                dve.wait_ge(sq, NB)
                dve.tensor_scalar(ssq[:], ssq[:], 1.0 / D, EPS, ALU.mult, ALU.add).then_inc(ms, 1)
                dve.wait_ge(rt, 1)
                dve.reciprocal(rstd[:], root[:]).then_inc(rs, 1)
                dve.wait_ge(rs, 1)
                with dve.Fori(0, 3) as i:
                    for u in range(3):
                        dve.wait_ge(turned, 3 * i)
                        if router:
                            dve.wait_ge(saved[u], 16 * i)
                        dve.tensor_scalar(xn[:, u], x[:, bass.ds(3 * i + u, 1), :].squeeze(1),
                                          rstd[:, bass.ds(3 * i + u, 1)], None, ALU.mult).then_inc(xn_ok, 1)
                    for u in range(3):
                        dve.wait_ge(turned, 3 * i + u + 1)
                        if router:
                            dve.wait_ge(lg, i)
                        if split:
                            dve.wait_ge(lo_ok, 3 * i)
                        for k in range(4):
                            dve.tensor_scalar(h_out(u, i, k, k + 1).squeeze(1), PS[:, 2 * u, P * k:P * k + P],
                                              g.gain[:, layer, which, k, bass.ds(3 * i + u, 1)],
                                              g.shift[:, layer, which, k, bass.ds(3 * i + u, 1)],
                                              ALU.mult, ALU.add).then_inc(ev_d, 1)
                if router:
                    steps = Steps(dve, chain)
                    logits = PS[:, 6, 0:NB * NE].rearrange("p (b e) -> p b e", e=NE)
                    dve.wait_ge(lg, 3)
                    steps.alone(dve.tensor_reduce(mx[:], logits, X, ALU.max))
                    dve.tensor_tensor(less[:], logits, mx[:].unsqueeze(2).to_broadcast([P, NB, NE]),
                                      ALU.subtract).then_inc(less_ok, 1)
                    dve.wait_ge(ex_ok, 1)
                    steps.alone(dve.tensor_reduce(tot[:], ex[:], X, ALU.add))
                    steps.alone(dve.reciprocal(inv[:], tot[:]))
                    dve.tensor_tensor(pr[:], ex[:], inv[:].unsqueeze(2).to_broadcast([P, NB, NE]),
                                      ALU.mult).then_inc(pr_ok, 1)
                    dve.wait_ge(pt, 1)
                    dve.tensor_copy(g.aff[:, 0:4 * P], PS[0:NE, 0, :]).then_inc(af, 1)
                    dve.wait_ge(pt, 3)
                    dve.tensor_copy(g.aff[:, 8 * P:T], PS[0:NE, 2, 0:P]).then_inc(af, 1)

            if split:
                @block.gpsimd
                def _(pool):
                    with pool.Fori(0, 3) as i:
                        for u in range(3):
                            cols = bass.ds(i * 3 * P + u * P, P)
                            pool.wait_ge(hi_ok, 3 * i + u + 1)
                            pool.tensor_tensor(hT[1][:, :, cols], hs[:, u], hT[0][:, :, cols].bitcast(F32),
                                               ALU.subtract).then_inc(lo_ok, 1)

            @block.tensor
            def _(pe):
                if router:
                    pe.wait_ge(wr_in, 16)
                with pe.Fori(0, 3) as i:
                    for u in range(3):
                        pe.wait_ge(xn_ok, 3 * i + u + 1)
                        pe.wait_ge(ev_a, 12 * i)
                        pe.wait_ge(ev_d, 12 * i)
                        for k in range(KD):
                            last = pe.transpose(PS[:, 2 * u + k // 4, P * (k % 4):P * (k % 4) + P],
                                                xn[:, u, P * k:P * k + P], g.ident[:])
                        last.then_inc(turned, 1)
                    if router:
                        for u in range(3):
                            pe.wait_ge(ev_a, 12 * i + 4 * u + 4)
                            pe.wait_ge(ev_d, 12 * i + 4 * u + 4)
                            for k in range(KD):
                                last = pe.matmul(PS[:, 6, bass.ds(i * 3 * NE + NE * u, NE)], hs[:, u, k], wr[:, k],
                                                 start=(k == 0), stop=(k == KD - 1))
                        last.then_inc(lg, 1)
                if router:
                    pe.wait_ge(pr_ok, 1)
                    for b in range(NB):
                        last = pe.transpose(PS[0:NE, b // 4, P * (b % 4):P * (b % 4) + P], pr[:, b], g.ident[:])
                        if b in (3, 7, 8):
                            last.then_inc(pt, 1)


def mla_project(nc, g, io, hT, m):
    with Stage(nc, "proj") as st:
        w = st.sb("w", [P, KD, QR + KVR + 2 * ROPE])
        sqr = st.sb("sqr", [P, KQ + KKV, TILE])
        root = st.sb("root", [P, 2, TILE])
        rinv = st.sb("rinv", [P, 2, TILE])
        kc = st.sb("kc", [P, TILE])
        qf = st.sb("qf", [P, KQ, TILE])
        k2 = st.sb("k2", [P, KEYS])
        cc = st.sb("cc", [P, KVR])
        ckr = st.sb("ckr", [P, 2 * ROPE])
        outs = st.sb("outs", [P, KVR + ROPE])
        epsc = st.sb("epsc", [P, 1])
        wq_in = st.sem("wq_in")
        w_in, cache_in, eps_ok = st.sem("w_in"), st.sem("cache_in"), st.sem("eps_ok")
        prod, sq, sums, rt, rc = st.sem("prod"), st.sem("sq"), st.sem("sums"), st.sem("rt"), st.sem("rc")
        kc_ok, fold, k2_ok, lat_ok = st.sem("kc_ok"), st.sem("fold"), st.sem("k2_ok"), st.sem("lat_ok")
        tp, cache_ok, out_ok, stored = st.sem("tp"), st.sem("cache_ok"), st.sem("out_ok"), st.sem("stored")
        hi_ok, lo_ok = st.sem("hi_ok"), st.sem("lo_ok")
        PS = g.PS
        NM = KQ + KKV

        def cols(i):
            return bass.ds(i * TILE, TILE)

        def to_split(i):
            if i is None:
                c = slice(T, KEYS)
                return [(m.ckv_pair, c, m.ckv[:, :, c]), (m.k2_pair, c, k2[:, c])]
            c = cols(i)
            return [(m.ckv_pair, c, m.ckv[:, :, c]), (m.k2_pair, c, k2[:, c]), (m.q_pair, c, qf[:])]

        def part(t, c):
            return t[:, c] if len(t.shape) == 2 else t[:, :, c]

        with nc.Block(no_gpsimd_drain=True) as block:
            @block.sync
            def _(sp):
                dkv = io["mla_w_dkv"][0].rearrange("(k p) n -> p k n", p=P)
                sp.dma_start(cc[:], io["cache_ckv"][0, 0]).then_inc(cache_in, 16)
                sp.dma_start(ckr[:, 0:ROPE], io["cache_krope"][0, 0]).then_inc(cache_in, 16)
                sp.dma_start(ckr[:, ROPE:2 * ROPE], io["cache_krope"][0, 0]).then_inc(cache_in, 16)
                sp.dma_start(w[:, :, 0:QR], io["mla_w_dq"][0].rearrange("(k p) n -> p k n", p=P)).then_inc(wq_in, 16)
                sp.dma_start(w[:, :, QR:QR + KVR + ROPE], dkv).then_inc(w_in, 16)
                at, h = QR + KVR + ROPE, ROPE // 2
                sp.dma_start(w[:, :, at:at + h], dkv[:, :, KVR + h:KVR + ROPE]).then_inc(w_in, 16)
                sp.dma_start(w[:, :, at + h:at + ROPE], dkv[:, :, KVR:KVR + h]).then_inc(w_in, 16)
                sp.dma_start(m.rope[:], io["rope"]).then_inc(w_in, 16)
                sp.wait_ge(out_ok, 1)
                sp.dma_start(io["new_ckv"][0, 0], outs[:, 0:KVR]).then_inc(stored, 16)
                sp.dma_start(io["new_krope"][0, 0], outs[:, KVR:KVR + ROPE]).then_inc(stored, 16)
                sp.wait_ge(stored, 32)

            @block.tensor
            def _(pe):
                pe.wait_ge(cache_in, 48)
                for r in range(KKV):
                    pe.transpose(PS[:, 0, P * r:P * r + P], cc[:, P * r:P * r + P], g.ident[:])
                pe.transpose(PS[:, 0, P * KKV:P * KKV + P], ckr[:], g.ident[:]).then_inc(tp, 1)
                pe.wait_ge(wq_in, 16)
                pe.wait_ge(cache_ok, 2)
                with pe.Fori(0, NT) as i:
                    def project(n):
                        if n == NM:
                            pe.wait_ge(k2_ok, i)
                        else:
                            pe.wait_ge(lat_ok, NM * i + n + 1)
                        for k in range(KD):
                            last = pe.matmul(PS[:, n, 0:TILE], w[:, k, P * n:P * n + P], hT[:, k, cols(i)],
                                             start=(k == 0), stop=(k == KD - 1))
                        last.then_inc(prod, 1)

                    def sum_up(j, n0, n1):
                        pe.wait_ge(sq, NM * i + n1)
                        for n in range(n0, n1):
                            last = pe.matmul(PS[:, 6 + j, 0:TILE], g.ones[:], sqr[:, n, :], start=(n == n0), stop=(n == n1 - 1))
                        last.then_inc(sums, 1)

                    for n in range(KQ):
                        project(n)
                    pe.wait_ge(w_in, 64)
                    project(KQ)
                    sum_up(0, 0, KQ)
                    for n in range(KQ + 1, NM + 1):
                        project(n)
                    sum_up(1, KQ, NM)
                    pe.wait_ge(kc_ok, i + 1)
                    pe.matmul(PS[:, NM, 0:TILE], g.fold[:], kc[:], start=True, stop=True).then_inc(fold, 1)
                pe.wait_ge(lat_ok, NM * NT + NM)
                pe.wait_ge(k2_ok, NT)
                for r in range(KKV):
                    pe.transpose(PS[:, 0, P * r:P * r + P], m.ckv[:, r, 0:P], g.ident[:])
                pe.transpose(PS[:, 0, P * KKV:P * KKV + ROPE], k2[0:ROPE, 0:P], g.ident[0:ROPE, 0:ROPE]).then_inc(tp, 1)

            @block.scalar
            def _(act):
                def rounded(i):
                    for pair, c, values in to_split(i):
                        act.copy(part(pair[0], c), values).then_inc(hi_ok, 1)

                act.wait_ge(cache_ok, 2)
                rounded(None)
                act.wait_ge(eps_ok, 1)
                with act.Fori(0, NT) as i:
                    act.wait_ge(sums, 2 * i)

                    def square(n):
                        act.wait_ge(prod, (NM + 1) * i + n + 1)
                        act.activation(sqr[:, n, :], PS[:, n, 0:TILE], ACT.Square).then_inc(sq, 1)

                    def take_root(j, width):
                        act.wait_ge(sums, 2 * i + j + 1)
                        act.activation(root[:, j, :], PS[:, 6 + j, 0:TILE], ACT.Sqrt, scale=1.0 / width,
                                       bias=epsc[:]).then_inc(rt, 1)

                    for n in range(KQ + 1):
                        square(n)
                    take_root(0, QR)
                    for n in range(KQ + 1, NM):
                        square(n)
                    take_root(1, KVR)
                    act.wait_ge(lat_ok, NM * i + 2 * NM)
                    act.wait_ge(k2_ok, i + 1)
                    rounded(i)

            @block.gpsimd
            def _(pool):
                def rest(i, before):
                    for n, (pair, c, values) in enumerate(to_split(i)):
                        pool.wait_ge(hi_ok, before + n + 1)
                        pool.tensor_tensor(part(pair[1], c), values, part(pair[0], c).bitcast(F32), ALU.subtract).then_inc(lo_ok, 1)

                rest(None, 0)
                with pool.Fori(0, NT) as i:
                    rest(i, 3 * i + 2)

            @block.vector
            def _(dve):
                dve.memset(epsc[:], EPS).then_inc(eps_ok, 1)
                dve.wait_ge(tp, 1)
                dve.tensor_copy(m.ckv[:, :, T:KEYS], PS[:, 0, 0:KVR].rearrange("p (r t) -> p r t", r=KKV)).then_inc(cache_ok, 1)
                dve.tensor_copy(k2[:, T:KEYS], PS[:, 0, KVR:KVR + P]).then_inc(cache_ok, 1)
                dve.sem_inc(lat_ok, NM)
                with dve.Fori(0, NT) as i:
                    def latents(j, n0, n1):
                        dve.wait_ge(rt, 2 * i + j + 1)
                        dve.reciprocal(rinv[:, j, :], root[:, j, :]).then_inc(rc, 1)
                        dve.wait_ge(rc, 2 * i + j + 1)
                        for n in range(n0, n1):
                            to = qf[:, n] if j == 0 else m.ckv[:, n - KQ, cols(i)]
                            dve.scalar_tensor_tensor(out=to, in0=PS[:, n, 0:TILE], scalar=g.vcol[:, V_QG + n:V_QG + n + 1],
                                                     in1=rinv[:, j, :], op0=ALU.mult, op1=ALU.mult).then_inc(lat_ok, 1)

                    dve.wait_ge(lo_ok, 3 * i + 2)
                    latents(0, 0, KQ)
                    dve.wait_ge(prod, (NM + 1) * (i + 1))
                    dve.wait_ge(fold, i)
                    dve.tensor_tensor(kc[:], PS[:, NM, 0:TILE], m.rope[:, cols(i)], ALU.mult).then_inc(kc_ok, 1)
                    dve.wait_ge(fold, i + 1)
                    dve.tensor_copy(k2[:, cols(i)], PS[:, NM, 0:TILE]).then_inc(k2_ok, 1)
                    latents(1, KQ, NM)
                dve.wait_ge(tp, 2)
                dve.tensor_copy(outs[:], PS[:, 0, 0:KVR + ROPE]).then_inc(out_ok, 1)


def mla_heads(nc, g, io, m):
    with Stage(nc, "attn") as st:
        wq = st.sb("wq", [P, KQ, 2 * P])
        wkv = st.sb("wkv", [P, KKV, 2 * P])
        def pair(name, shape):
            return [st.sb(name + half, shape, F32R) for half in ("_hi", "_lo")]

        wq_pair, wk_pair = pair("wq", [P, KQ, 2 * P]), pair("wk", [P, KKV, P])
        qT, q2, kT = pair("qT", [P, T]), pair("q2", [P, T]), pair("kT", [P, KEYS])
        q2f = st.sb("q2f", [P, T])
        v = st.sb("v", [P, KEYS // P, P])
        mx = st.sb("mx", [P, NB])
        nm = st.sb("nm", [P, NB])
        rsum = st.sb("rsum", [P, NB])
        rin = st.sb("rin", [P, NB])
        prob = st.sb("prob", [P, 2, SAMPLE_KEYS])
        pT = st.sb("pT", [P, NB, P])
        on = st.sb("on", [P, 2, P])
        wq_in, wkv_in, w_hi, w_lo = st.sem("wq_in"), st.sem("wkv_in"), st.sem("w_hi"), st.sem("w_lo")
        q_hi, q2f_ok, q2_hi, k_hi = st.sem("q_hi"), st.sem("q2f_ok"), st.sem("q2_hi"), st.sem("k_hi")
        q_mm, q2_mm, k_mm, v_mm = st.sem("q_mm"), st.sem("q2_mm"), st.sem("k_mm"), st.sem("v_mm")
        q_ok, q2_ok, k_ok, v_ok = st.sem("q_ok"), st.sem("q2_ok"), st.sem("k_ok"), st.sem("v_ok")
        s_mm, mx_ok, nm_ok, p_ok = st.sem("s_mm"), st.sem("mx_ok"), st.sem("nm_ok"), st.sem("p_ok")
        t_mm, pt_a, pt_d = st.sem("t_mm"), st.sem("pt_a"), st.sem("pt_d")
        pv_mm, rin_ok, on_ok, ot_mm, ot_ok = st.sem("pv_mm"), st.sem("rin_ok"), st.sem("on_ok"), st.sem("ot_mm"), st.sem("ot_ok")
        PS = g.PS
        VB = KEYS // P
        blocks = list(range(1, NB)) + [0]

        def key_blocks(j):
            return list(range(1, VB)) if blocks[j] else [0]

        def groups(j):
            kb = key_blocks(j)
            return [(6 + n % 2, kb[3 * n:3 * n + 3]) for n in range((len(kb) + 2) // 3)]

        NG = [len(groups(j)) for j in range(NB)]
        GA = [(n + 1) // 2 for n in NG]
        GD = [n // 2 for n in NG]

        def turns(eng, body):
            with eng.Fori(0, HEADS - 1) as h:
                body(h, True)
            body(HEADS - 1, False)

        def tiles(ap):
            return ap.rearrange("p (t n) -> p t n", t=NT)

        def both(pair, *at):
            return pair[0][(slice(None),) + at], pair[1][(slice(None),) + at]

        with nc.Block(no_gpsimd_drain=True) as block:
            @block.sync
            def _(sp):
                wuq = io["mla_w_uq"][0].rearrange("(k p) n -> p k n", p=P)
                wukv = io["mla_w_ukv"][0].rearrange("(k p) n -> p k n", p=P)
                hw = NOPE + ROPE

                def load_q(h):
                    for c0, c1, at in ((0, hw, 0), (hw, hw + 32, NOPE + 32), (hw + 32, hw + 64, NOPE)):
                        sp.dma_start(wq[:, :, c0:c1], wuq[:, :, bass.ds(h * hw + at, c1 - c0)]).then_inc(wq_in, 16)

                def load_kv(h):
                    sp.dma_start(wkv[:], wukv[:, :, bass.ds(h * 2 * P, 2 * P)]).then_inc(wkv_in, 16)

                load_q(0)
                load_kv(0)
                with sp.Fori(1, HEADS) as h:
                    sp.wait_ge(w_lo, 2 * h)
                    load_q(h)
                    sp.wait_ge(v_mm, h)
                    load_kv(h)

            @block.tensor
            def _(pe):
                def scores(h, j, qb):
                    if j == 0:
                        pe.wait_ge(k_ok, h + 1)
                        pe.wait_ge(q2_ok, h + 1)
                    elif j == 1:
                        pe.wait_ge(v_ok, h + 1)
                    else:
                        pe.wait_ge(p_ok, NB * h + j - 1)
                    kb = key_blocks(j)
                    width = min(TILE, P * len(kb))
                    for t in range(P * len(kb) // width):
                        out = PS[:, 3 * (j % 2) + t, 0:width]
                        c0 = P * kb[0] + t * width
                        qs, ks = slice(P * qb, P * qb + P), slice(c0, c0 + width)
                        exact_products(pe, out, both(qT, qs), both(kT, ks), True, False)
                        last = exact_products(pe, out, both(q2, qs), both(m.k2_pair, ks), False, True)
                    last.then_inc(s_mm, 1)

                def turn_out(h, j):
                    pe.wait_ge(on_ok, NB * h + j + 1)
                    pe.transpose(PS[:, 6, TILE:TILE + P], on[:, j % 2], g.ident[:]).then_inc(ot_mm, 1)

                def transposes(h, j, n):
                    bank, kbs = groups(j)[n]
                    for a in range(len(kbs)):
                        c0 = P * (3 * n + a)
                        last = pe.transpose(PS[:, bank, P * a:P * a + P], prob[:, j % 2, c0:c0 + P], g.ident[:])
                    last.then_inc(t_mm, 1)

                def first_transposes(h, j):
                    pe.wait_ge(p_ok, NB * h + j + 1)
                    pe.wait_ge(pt_a, sum(GA) * h + sum(GA[:j]))
                    pe.wait_ge(ot_ok, NB * h + max(0, j - 1))
                    transposes(h, j, 0)

                def values(h, j):
                    na, nd = sum(GA[:j]), sum(GD[:j])
                    pe.wait_ge(on_ok, NB * h + j)
                    if NG[j] == 3:
                        transposes(h, j, 1)
                        pe.wait_ge(pt_a, sum(GA) * h + na + 1)
                        transposes(h, j, 2)
                    if j:
                        turn_out(h, j - 1)
                    pe.wait_ge(pt_a, sum(GA) * h + na + 1)
                    pe.wait_ge(pt_d, sum(GD) * h + nd + GD[j])
                    kbs = key_blocks(j)
                    for a, kb in enumerate(kbs):
                        if a == 6:
                            pe.wait_ge(pt_a, sum(GA) * h + na + GA[j])
                        last = pe.matmul(PS[:, 7, TILE:TILE + P], pT[:, a], v[:, kb], start=(a == 0),
                                         stop=(a == len(kbs) - 1))
                    last.then_inc(pv_mm, 1)

                def body(h, more):
                    pe.wait_ge(w_lo, 2 * h + 2)
                    pe.wait_ge(p_ok, NB * h)
                    for t in range(NT):
                        for k in range(KQ):
                            last = exact_products(pe, PS[:, t, 0:TILE], both(wq_pair, k, slice(0, P)),
                                                  both(m.q_pair, k, slice(TILE * t, TILE * t + TILE)), k == 0, k == KQ - 1)
                    last.then_inc(q_mm, 1)
                    for t in range(NT):
                        for k in range(KQ):
                            last = exact_products(pe, PS[:, 3 + t, 0:TILE], both(wq_pair, k, slice(P, 2 * P)),
                                                  both(m.q_pair, k, slice(TILE * t, TILE * t + TILE)), k == 0, k == KQ - 1)
                    last.then_inc(q2_mm, 1)
                    pe.wait_ge(q_ok, h + 1)
                    for t in range(3):
                        c0, c1 = TILE * t, (TILE * t + TILE if t < 2 else KEYS)
                        for r in range(KKV):
                            last = exact_products(pe, PS[:, t, 0:c1 - c0], both(wk_pair, r), both(m.ckv_pair, r, slice(c0, c1)),
                                                  r == 0, r == KKV - 1)
                    last.then_inc(k_mm, 1)
                    pe.wait_ge(q2f_ok, h + 1)
                    for kb in range(VB):
                        for r in range(KKV):
                            last = pe.matmul(PS[:, 3 + kb // 4, P * (kb % 4):P * (kb % 4) + P],
                                             m.ckv[:, r, P * kb:P * kb + P], wkv[:, r, P:2 * P],
                                             start=(r == 0), stop=(r == KKV - 1))
                    last.then_inc(v_mm, 1)
                    scores(h, 0, blocks[0])
                    scores(h, 1, blocks[1])
                    for j in range(NB):
                        first_transposes(h, j)
                        if j + 2 < NB:
                            scores(h, j + 2, blocks[j + 2])
                        values(h, j)
                    pe.wait_ge(pt_a, sum(GA) * h + sum(GA))
                    pe.wait_ge(ot_ok, NB * h + NB - 1)
                    turn_out(h, NB - 1)
                turns(pe, body)

            @block.scalar
            def _(act):
                def exps(h, j):
                    pe_done = sum(NG[:j - 1]) if j > 1 else 0
                    act.wait_ge(t_mm, sum(NG) * h + pe_done)
                    act.wait_ge(nm_ok, NB * h + j + 1)
                    kb = key_blocks(j)
                    nt, width = max(1, len(kb) // 3), min(TILE, P * len(kb))
                    act.activation(prob[:, j % 2, 0:nt * width].rearrange("p (t k) -> p t k", t=nt),
                                   PS[:, 3 * (j % 2):3 * (j % 2) + nt, 0:width], ACT.Exp, bias=nm[:, j:j + 1],
                                   scale=SCALE, accum_out=rsum[:, j:j + 1]).then_inc(p_ok, 1)

                def out_cols(h, j):
                    act.wait_ge(ot_mm, NB * h + j + 1)
                    act.copy(m.oT[:, bass.ds(h, 1), P * blocks[j]:P * blocks[j] + P].squeeze(1),
                             PS[:, 6, TILE:TILE + P]).then_inc(ot_ok, 1)

                def evacuate(h, j):
                    for n in range(0, NG[j], 2):
                        bank, kbs = groups(j)[n]
                        act.wait_ge(t_mm, sum(NG) * h + sum(NG[:j]) + n + 1)
                        if n == NG[j] - 1 and j:
                            act.wait_ge(ot_mm, NB * h + j)
                        act.copy(pT[:, 3 * n:3 * n + len(kbs)], PS[:, bank, 0:P * len(kbs)].rearrange(
                            "p (a k) -> p a k", k=P)).then_inc(pt_a, 1)
                    if j:
                        out_cols(h, j - 1)

                def rounded_weights(h):
                    act.wait_ge(wq_in, 48 * h + 48)
                    act.copy(wq_pair[0][:], wq[:]).then_inc(w_hi, 1)
                    act.wait_ge(wkv_in, 16 * h + 16)
                    act.copy(wk_pair[0][:], wkv[:, :, 0:P]).then_inc(w_hi, 1)

                rounded_weights(0)

                def body(h, more):
                    act.wait_ge(q_mm, h + 1)
                    act.copy(tiles(qT[0][:]), PS[:, 0:NT, 0:TILE]).then_inc(q_hi, 1)
                    act.wait_ge(q2f_ok, h + 1)
                    act.copy(q2[0][:], q2f[:]).then_inc(q2_hi, 1)
                    act.wait_ge(k_mm, h + 1)
                    act.copy(kT[0][:, 0:2 * TILE].rearrange("p (t n) -> p t n", t=2), PS[:, 0:2, 0:TILE])
                    act.copy(kT[0][:, 2 * TILE:KEYS], PS[:, 2, 0:KEYS - 2 * TILE]).then_inc(k_hi, 1)
                    exps(h, 0)
                    exps(h, 1)
                    for j in range(NB):
                        evacuate(h, j)
                        if j + 2 < NB:
                            exps(h, j + 2)
                        if more and j == 4:
                            rounded_weights(h + 1)
                    out_cols(h, NB - 1)
                turns(act, body)

            @block.vector
            def _(dve):
                def maxima(h, j):
                    dve.wait_ge(s_mm, NB * h + j + 1)
                    kb = key_blocks(j)
                    nt, width = max(1, len(kb) // 3), min(TILE, P * len(kb))
                    src = PS[:, 3 * (j % 2):3 * (j % 2) + nt, 0:width]
                    dve.tensor_reduce(mx[:, j:j + 1], src, mybir.AxisListType.XY, ALU.max).then_inc(mx_ok, 1)
                    dve.wait_ge(mx_ok, NB * h + j + 1)
                    dve.tensor_scalar(nm[:, j:j + 1], mx[:, j:j + 1], -SCALE, None, ALU.mult).then_inc(nm_ok, 1)

                def copy_group(h, j):
                    for n, (bank, kbs) in enumerate(groups(j)):
                        if n % 2:
                            dve.wait_ge(t_mm, sum(NG) * h + sum(NG[:j]) + n + 1)
                            dve.tensor_copy(pT[:, 3 * n:3 * n + len(kbs)], PS[:, bank, 0:P * len(kbs)].rearrange(
                                "p (a k) -> p a k", k=P)).then_inc(pt_d, 1)

                def finish(h, j):
                    dve.wait_ge(p_ok, NB * h + j + 1)
                    dve.reciprocal(rin[:, j:j + 1], rsum[:, j:j + 1]).then_inc(rin_ok, 1)
                    dve.wait_ge(pv_mm, NB * h + j + 1)
                    dve.wait_ge(rin_ok, NB * h + j + 1)
                    dve.tensor_scalar(on[:, j % 2], PS[:, 7, TILE:TILE + P], rin[:, j:j + 1], None,
                                      ALU.mult).then_inc(on_ok, 1)

                def rest_of_weights(h):
                    dve.wait_ge(w_hi, 2 * h + 2)
                    dve.tensor_tensor(wq_pair[1][:], wq[:], wq_pair[0][:].bitcast(F32), ALU.subtract).then_inc(w_lo, 1)
                    dve.tensor_tensor(wk_pair[1][:], wkv[:, :, 0:P], wk_pair[0][:].bitcast(F32), ALU.subtract).then_inc(w_lo, 1)

                rest_of_weights(0)

                def body(h, more):
                    dve.wait_ge(q_hi, h + 1)
                    dve.tensor_tensor(tiles(qT[1][:]), PS[:, 0:NT, 0:TILE], tiles(qT[0][:]).bitcast(F32),
                                      ALU.subtract).then_inc(q_ok, 1)
                    dve.wait_ge(q2_mm, h + 1)
                    dve.tensor_tensor(tiles(q2f[:]), PS[:, 3:6, 0:TILE], tiles(m.rope[:]), ALU.mult).then_inc(q2f_ok, 1)
                    dve.wait_ge(q2f_ok, h + 1)
                    dve.wait_ge(q2_hi, h + 1)
                    dve.tensor_tensor(q2[1][:], q2f[:], q2[0][:].bitcast(F32), ALU.subtract).then_inc(q2_ok, 1)
                    dve.wait_ge(k_hi, h + 1)
                    for c0, c1, src in ((0, 2 * TILE, PS[:, 0:2, 0:TILE]), (2 * TILE, KEYS, PS[:, 2:3, 0:KEYS - 2 * TILE])):
                        nt = 2 if c0 == 0 else 1
                        last = dve.tensor_tensor(kT[1][:, c0:c1].rearrange("p (t n) -> p t n", t=nt), src,
                                                 kT[0][:, c0:c1].rearrange("p (t n) -> p t n", t=nt).bitcast(F32), ALU.subtract)
                    last.then_inc(k_ok, 1)
                    dve.wait_ge(v_mm, h + 1)
                    vf = v[:].rearrange("p a b -> p (a b)")
                    dve.tensor_copy(vf[:, 0:1024].rearrange("p (t n) -> p t n", t=2), PS[:, 3:5, :])
                    dve.tensor_copy(vf[:, 1024:1280], PS[:, 5, 0:256]).then_inc(v_ok, 1)
                    maxima(h, 0)
                    maxima(h, 1)
                    for j in range(NB):
                        copy_group(h, j)
                        if j + 2 < NB:
                            maxima(h, j + 2)
                        finish(h, j)
                        if more and j == 5:
                            rest_of_weights(h + 1)
                turns(dve, body)


def block_loop(eng, body):
    with eng.Fori(0, DEC // P // 2) as i:
        for u in range(2):
            body(2 * i + u, u, 2 * i + u + 1, 1)
    body(DEC // P, 0, 0, 0)


def project_out(nc, g, io, name, layer, kd, ks, w_dram, take):
    with Stage(nc, name) as st:
        KG = 4
        w = st.sb("w", [P, max(1, kd - ks), D])
        w_hi, w_lo = st.sb("w_hi", [P, ks, D], F32R), st.sb("w_lo", [P, ks, D], F32R)
        whole = st.sb("whole", [P, 2 * ks // KG, KG, 512])
        x = st.sb("x", [P, 2, D])
        t = st.sb("t", [P, 2, D])
        pieces = [(half, k0) for half in range(2) for k0 in range(0, kd, KG)]
        to_split = [p for p in pieces if p[1] < ks]
        w_in = {p: st.sem(f"w_in{n}") for n, p in enumerate(pieces)}
        hi_ok, lo_ok = st.sem("hi_ok"), st.sem("lo_ok")
        x_in = [st.sem("x_in0"), st.sem("x_in1")]
        saved = [st.sem("saved0"), st.sem("saved1")]
        mm, gated, added = st.sem("mm"), st.sem("gated"), st.sem("added")
        src, src_ok, engines = take(st, mm)
        PS = g.PS

        with nc.Block(no_gpsimd_drain=True) as block:
            @block.sync
            def _(sp):
                def body(n, u, b, grp):
                    if engines.get("sync"):
                        engines["sync"](sp, n, u, b, grp)
                    if u == 0:
                        sp.wait_ge(saved[0], 8 * n)
                    else:
                        sp.wait_ge(saved[1], 8 * n - 8)
                    rows = bass.ds(b * P, P) if grp else slice(0, P)
                    if layer:
                        sp.dma_start(x[:, u], g.res[rows, :]).then_inc(x_in[u], 16)
                    elif grp:
                        sp.dma_start(x[:, u], io["x_sample"][0, bass.ds(b * P - P, P), :]).then_inc(x_in[u], 16)
                    else:
                        sp.dma_start(x[:, u], io["x_prompt"][0]).then_inc(x_in[u], 16)
                block_loop(sp, body)
                sp.wait_ge(saved[0], 16 * (DEC // P // 2 + 1))
                sp.wait_ge(saved[1], 16 * (DEC // P // 2))

            @block.tensor
            def _(pe):
                pe.sem_inc(mm, 1)
                if engines.get("tensor"):
                    engines["tensor"](pe, 0, 0)

                def body(n, u, b, grp):
                    if engines.get("tensor") and grp:
                        engines["tensor"](pe, n + 1, 1 - u)
                    pe.wait_ge(src_ok, n + 1)
                    pe.wait_ge(gated, n)
                    for half in range(2):
                        cs = slice(512 * half, 512 * half + 512)
                        for k in range(kd):
                            if k % KG == 0:
                                if k < ks:
                                    pe.wait_ge(lo_ok, to_split.index((half, k)) + 1)
                                else:
                                    pe.wait_ge(w_in[half, k], 16)
                            if k < ks:
                                last = exact_products(pe, PS[:, 2 * u + half, :], (src[0][:, u, k], src[1][:, u, k]),
                                                      (w_hi[:, k, cs], w_lo[:, k, cs]), k == 0, k == kd - 1)
                            else:
                                last = pe.matmul(PS[:, 2 * u + half, :], src[2][:, u, k - ks, :], w[:, k - ks, cs],
                                                 start=(k == 0), stop=(k == kd - 1))
                    last.then_inc(mm, 1)
                block_loop(pe, body)

            @block.scalar
            def _(act):
                for half, k0 in pieces:
                    rows, cs = slice(k0, k0 + KG), slice(512 * half, 512 * half + 512)
                    if k0 < ks:
                        to = whole[:, to_split.index((half, k0))]
                    else:
                        to = w[:, k0 - ks:k0 - ks + KG, cs]
                    act.dma_start(to, w_dram.rearrange("(k p) n -> p k n", p=P)[:, rows, cs]).then_inc(w_in[half, k0], 16)
                if engines.get("before_scalar"):
                    engines["before_scalar"](act)
                for n, (half, k0) in enumerate(to_split):
                    act.wait_ge(w_in[half, k0], 16)
                    act.copy(w_hi[:, k0:k0 + KG, 512 * half:512 * half + 512], whole[:, n]).then_inc(hi_ok, 1)

                def body(n, u, b, grp):
                    engines["scalar"](act, n, u, b, grp)
                block_loop(act, body)

            @block.vector
            def _(dve):
                dve.sem_inc(gated, 1)
                if engines.get("before_vector"):
                    engines["before_vector"](dve)
                if engines.get("vector"):
                    engines["vector"](dve, 0, 0)

                def body(n, u, b, grp):
                    factor = engines["factor"](dve, n, u, b, grp) if engines.get("factor") else None
                    if engines.get("vector") and grp:
                        engines["vector"](dve, n + 1, 1 - u)
                    dve.wait_ge(mm, n + 2)
                    dve.wait_ge(x_in[u], 8 * n + 16 - 8 * u)
                    out, gate = (ap.rearrange("p (h n) -> p h n", h=2) for ap in (t[:, u], g.gate_row[:, grp]))
                    rows = PS[:, 2 * u:2 * u + 2, :]
                    if factor is None:
                        dve.tensor_tensor(out, rows, gate, ALU.mult).then_inc(gated, 1)
                    else:
                        dve.scalar_tensor_tensor(out=out, in0=rows, scalar=factor, in1=gate, op0=ALU.mult,
                                                 op1=ALU.mult).then_inc(gated, 1)
                    dve.wait_ge(gated, n + 2)
                    dve.tensor_tensor(x[:, u], x[:, u], t[:, u], ALU.add).then_inc(added, 1)
                block_loop(dve, body)

            @block.gpsimd
            def _(pool):
                for n, (half, k0) in enumerate(to_split):
                    rows, cs = slice(k0, k0 + KG), slice(512 * half, 512 * half + 512)
                    pool.wait_ge(hi_ok, n + 1)
                    pool.tensor_tensor(w_lo[:, rows, cs], whole[:, n], w_hi[:, rows, cs].bitcast(F32),
                                       ALU.subtract).then_inc(lo_ok, 1)

                def body(n, u, b, grp):
                    pool.wait_ge(added, n + 1)
                    rows = bass.ds(b * P, P) if grp else slice(0, P)
                    pool.dma_start(g.res[rows, :], x[:, u]).then_inc(saved[u], 16)
                block_loop(pool, body)


def mla_out(nc, g, io, m):
    def take(st, mm):
        oc = st.sb("oc", [P, 2, HEADS, P])
        oc_hi, oc_lo = (st.sb("oc" + half, [P, 2, HEADS, P], F32R) for half in ("_hi", "_lo"))
        oc_hi_ok, oc_ok = st.sem("oc_hi_ok"), st.sem("oc_ok")

        def scalar(act, n, u, b, grp):
            act.wait_ge(mm, n)
            cols = bass.ds(b * P, P) if grp else slice(0, P)
            act.copy(oc[:, u], m.oT[:, :, cols])
            act.copy(oc_hi[:, u], m.oT[:, :, cols]).then_inc(oc_hi_ok, 1)

        def vector(dve, n, u):
            dve.wait_ge(oc_hi_ok, n + 1)
            dve.tensor_tensor(oc_lo[:, u], oc[:, u], oc_hi[:, u].bitcast(F32), ALU.subtract).then_inc(oc_ok, 1)
        return (oc_hi, oc_lo), oc_ok, {"scalar": scalar, "vector": vector}
    project_out(nc, g, io, "wo", 0, HEADS, HEADS, io["mla_w_o"][0], take)


def mixture(nc, g, io, layer):
    with Stage(nc, f"mix{layer}") as st:
        mw = Shared()
        mw.wg = st.sb("wg", [P, 2, KD, 512])
        mw.wu = st.sb("wu", [P, 2, KD, 512])
        mw.wg_in = [st.sem("wg_in0"), st.sem("wg_in1")]
        mw.wu_in = [st.sem("wu_in0"), st.sem("wu_in1")]

        def load(sp, e, half):
            for buf, w, s in ((mw.wg, io["moe_w_gate"], mw.wg_in), (mw.wu, io["moe_w_up"], mw.wu_in)):
                view = w[layer].rearrange("e (k p) n -> p e k n", p=P)
                sp.dma_start(buf[:, half], view[:, bass.ds(e, 1), :, 512 * half:512 * half + 512].squeeze(1)
                             ).then_inc(s[half], 16)
        mw.load = load
        choose(nc, g, io, layer, mw)
        experts(nc, g, io, layer, mw)


def choose(nc, g, io, layer, mw):
    with Stage(nc, f"topk{layer}") as st:
        best = st.sb("best", [NE, 8])
        at = st.sb("at", [NE, 8], U32)
        vals = st.sb("vals", [NE, CAP])
        rows = st.sb("rows", [NE, CAP])
        chain, picked, tp, out = st.sem("chain"), st.sem("picked"), st.sem("tp"), st.sem("out")
        PS = g.PS
        mod = Modulation(st, g, io, layer + 1) if layer + 1 < DEPTH else None
        with nc.Block(no_gpsimd_drain=True) as block:
            @block.sync
            def _(sp):
                if mod:
                    mod.sync(sp)
                mw.load(sp, 0, 0)
                mw.load(sp, 0, 1)

            if mod:
                @block.scalar
                def _(act):
                    mod.scalar(act)

            @block.vector
            def _(dve):
                def rounds(values, first, count, before):
                    with dve.Fori(0, count) as i:
                        steps = Steps(dve, chain, i, 5, before)
                        steps.did(dve.max(best[:], values))
                        wait_alone(dve, chain, steps.base + 1)
                        steps.did(dve.max_index(at[:], best[:], values))
                        steps.did(dve.tensor_copy(vals[:, bass.ds(first + i * 8, 8)], best[:]))
                        wait_alone(dve, chain, steps.base + 2)
                        steps.did(dve.match_replace(values, best[:], values, -1.0))
                        steps.did(dve.tensor_copy(rows[:, bass.ds(first + i * 8, 8)], at[:]))
                        steps.settle()
                rounds(g.aff[:, SEQ:T], 0, CAP_S // 8, 0)
                rounds(g.aff[:, 0:SEQ], CAP_S, CAP_P // 8, 5 * CAP_S // 8)
                dve.tensor_scalar(rows[:, 0:CAP_S], rows[:, 0:CAP_S], float(SEQ), None, ALU.add).then_inc(picked, 1)
                if mod:
                    mod.vector(dve)
                dve.wait_ge(tp, 1)
                dve.tensor_copy(g.row_s[:], PS[:, 0, 0:NE]).then_inc(out, 1)
                dve.tensor_copy(g.gate_s[:], PS[:, 0, NE:2 * NE]).then_inc(out, 1)
                dve.tensor_copy(g.row_p[:], PS[0:CAP_P, 0, 2 * NE:3 * NE]).then_inc(out, 1)
                dve.tensor_copy(g.gate_p[:], PS[0:CAP_P, 0, 3 * NE:4 * NE]).then_inc(out, 1)

            @block.tensor
            def _(pe):
                if mod:
                    mod.tensor(pe)
                pe.wait_ge(picked, 1)
                ident = g.ident[0:NE, 0:NE]
                pe.transpose(PS[:, 0, 0:NE], rows[:, 0:CAP_S], ident)
                pe.transpose(PS[:, 0, NE:2 * NE], vals[:, 0:CAP_S], ident)
                pe.transpose(PS[0:CAP_P, 0, 2 * NE:3 * NE], rows[:, CAP_S:CAP], ident)
                pe.transpose(PS[0:CAP_P, 0, 3 * NE:4 * NE], vals[:, CAP_S:CAP], ident).then_inc(tp, 1)


def experts(nc, g, io, layer, mw):
    with Stage(nc, f"moe{layer}") as st:
        HB = 512
        wg, wu, wg_in, wu_in = mw.wg, mw.wu, mw.wg_in, mw.wu_in
        wd = st.sb("wd", [P, 2, KD, HB])
        x_s = st.sb("x_s", [P, D])
        x_p = st.sb("x_p", [CAP_P, D])
        id_s = st.sb("id_s", [P, 2], U32)
        id_p = st.sb("id_p", [CAP_P, 2], U32)
        xT = st.sb("xT", [P, KD, CAP])
        sg = st.sb("sg", [P, KD, CAP])
        hid = st.sb("hid", [P, KD, CAP])
        ye = st.sb("ye", [P, KD, CAP])
        y_s = st.sb("y_s", [P, D])
        y_p = st.sb("y_p", [CAP_P, D])
        wd_in = [st.sem("wd_in0"), st.sem("wd_in1")]
        xs_in, xp_in = st.sem("xs_in"), st.sem("xp_in")
        id_ok, ys_out, yp_out = st.sem("id_ok"), st.sem("ys_out"), st.sem("yp_out")
        x_mm, xa_ok, xd_ok = st.sem("x_mm"), st.sem("xa_ok"), st.sem("xd_ok")
        half_gu, gu_mm, sg_ok, hid_ok = st.sem("half_gu"), st.sem("gu_mm"), st.sem("sg_ok"), st.sem("hid_ok")
        half_d, d_mm, ye_ok = st.sem("half_d"), st.sem("d_mm"), st.sem("ye_ok")
        back, ys_ok, yp_ok = st.sem("back"), st.sem("ys_ok"), st.sem("yp_ok")
        PS = g.PS
        TRIOS = [(0, 3), (3, 6), (6, 8)]

        def turns(eng, body):
            with eng.Fori(0, NE - 1) as e:
                body(e, True)
            body(NE - 1, False)

        def trio(bank, a, b):
            return PS[:, bank, 0:(b - a) * CAP].rearrange("p (m c) -> p m c", c=CAP)

        with nc.Block(no_gpsimd_drain=True) as block:
            @block.sync
            def _(sp):
                down = io["moe_w_down"][layer].rearrange("e (k p) n -> p e k n", p=P)

                def load_down(e, half):
                    sp.dma_start(wd[:, half], down[:, bass.ds(e, 1), :, HB * half:HB * half + HB].squeeze(1)
                                 ).then_inc(wd_in[half], 16)

                load_down(0, 0)
                load_down(0, 1)
                with sp.Fori(1, NE) as e:
                    for half in range(2):
                        sp.wait_ge(half_gu if half == 0 else gu_mm, e if half == 0 else 3 * e)
                        mw.load(sp, e, half)
                    for half in range(2):
                        sp.wait_ge(half_d if half == 0 else d_mm, e if half == 0 else 3 * e)
                        load_down(e, half)

            @block.gpsimd
            def _(pool):
                def gather(e, n_ids):
                    pool.tensor_copy(id_s[:, 0:1], g.row_s[:, bass.ds(e, 1)]).then_inc(id_ok, 1)
                    pool.tensor_copy(id_p[:, 0:1], g.row_p[:, bass.ds(e, 1)]).then_inc(id_ok, 1)
                    wait_alone(pool, id_ok, n_ids + 2)
                    pool.indirect_dma_start(x_s[:], None, g.normed, bass.IndirectOffsetOnAxis(ap=id_s[:, 0:1], axis=0),
                                            bounds_check=T - 1, oob_is_err=False).then_inc(xs_in, 16)
                    pool.indirect_dma_start(x_p[:], None, g.normed, bass.IndirectOffsetOnAxis(ap=id_p[:, 0:1], axis=0),
                                            bounds_check=T - 1, oob_is_err=False).then_inc(xp_in, 16)

                def scatter(e, n_ids):
                    wait_alone(pool, ys_out, 16 * e)
                    pool.wait_ge(yp_out, 16 * e)
                    pool.tensor_copy(id_s[:, 1:2], g.row_s[:, bass.ds(e, 1)]).then_inc(id_ok, 1)
                    pool.tensor_copy(id_p[:, 1:2], g.row_p[:, bass.ds(e, 1)]).then_inc(id_ok, 1)
                    wait_alone(pool, id_ok, n_ids + 2)
                    wait_alone(pool, ys_ok, 2 * e + 2)
                    pool.indirect_dma_start(g.res, bass.IndirectOffsetOnAxis(ap=id_s[:, 1:2], axis=0), y_s[:], None,
                                            bounds_check=T - 1, compute_op=ALU.add).then_inc(ys_out, 16)
                    wait_alone(pool, yp_ok, e + 1)
                    pool.indirect_dma_start(g.res, bass.IndirectOffsetOnAxis(ap=id_p[:, 1:2], axis=0), y_p[:], None,
                                            bounds_check=T - 1, compute_op=ALU.add).then_inc(yp_out, 16)

                gather(0, 0)

                def body(e, more):
                    if more:
                        pool.wait_ge(x_mm, 3 * e + 3)
                        gather(e + 1, 4 * e + 2)
                        scatter(e, 4 * e + 4)
                    else:
                        scatter(e, 4 * e + 2)
                turns(pool, body)
                pool.wait_ge(ys_out, 16 * NE)
                pool.wait_ge(yp_out, 16 * NE)

            @block.tensor
            def _(pe):
                def tokens(e, rows_read, up_read):
                    pe.wait_ge(ys_ok, rows_read)
                    pe.wait_ge(xs_in, 16 * e + 16)
                    for k in range(KD):
                        last = pe.transpose(PS[:, 6 + k // 4, P * (k % 4):P * (k % 4) + P], x_s[:, P * k:P * k + P], g.ident[:])
                        if k % 4 == 3:
                            last.then_inc(x_mm, 1)
                    pe.wait_ge(hid_ok, up_read)
                    wait_alone(pe, xp_in, 16 * e + 16)
                    for k in range(KD):
                        last = pe.transpose(PS[:, 3, CAP_P * k:CAP_P * k + CAP_P], x_p[:, P * k:P * k + P],
                                            g.ident[0:CAP_P, 0:CAP_P])
                    last.then_inc(x_mm, 1)

                def rows_back(a, b):
                    for k in range(a, b):
                        pe.transpose(PS[:, 6 + k // 4, P * (k % 4):P * (k % 4) + P], ye[:, k, 0:CAP_S], g.ident[:])
                        last = pe.transpose(PS[0:CAP_P, 4 + k // 4, P * (k % 4):P * (k % 4) + P], ye[:, k, CAP_S:CAP], g.ident[:])
                    return last

                tokens(0, 0, 0)

                def body(e, more):
                    pe.wait_ge(xa_ok, 4 * e + 4)
                    pe.wait_ge(xd_ok, 6 * e + 6)
                    pe.wait_ge(ye_ok, 6 * e)
                    for q, (a, b) in enumerate(TRIOS):
                        for w, w_in, bank in ((wg, wg_in, q), (wu, wu_in, 3 + q)):
                            if bank == 4:
                                pe.wait_ge(yp_ok, e)
                            for f in range(a, b):
                                if f % 4 == 0:
                                    pe.wait_ge(w_in[f // 4], 16 * e + 16)
                                for k in range(KD):
                                    last = pe.matmul(PS[:, bank, CAP * (f - a):CAP * (f - a + 1)],
                                                     w[:, f // 4, k, P * (f % 4):P * (f % 4) + P], xT[:, k, :],
                                                     start=(k == 0), stop=(k == KD - 1))
                                if f == 3 and bank == 4:
                                    last.then_inc(half_gu, 1)
                        last.then_inc(gu_mm, 1)
                    if more:
                        tokens(e + 1, 2 * e, 3 * e + 1)
                    pe.wait_ge(hid_ok, 3 * e + 3)
                    for q, (a, b) in enumerate(TRIOS):
                        if q == 2:
                            if more:
                                pe.wait_ge(xa_ok, 4 * e + 8)
                                pe.wait_ge(xd_ok, 6 * e + 12)
                            else:
                                pe.wait_ge(ys_ok, 2 * e)
                            pe.wait_ge(ye_ok, 6 * e + 2)
                            rows_back(*TRIOS[0])
                        for f in range(a, b):
                            if f % 4 == 0:
                                pe.wait_ge(wd_in[f // 4], 16 * e + 16)
                            for k in range(KD):
                                last = pe.matmul(PS[:, q, CAP * (f - a):CAP * (f - a + 1)],
                                                 wd[:, f // 4, k, P * (f % 4):P * (f % 4) + P], hid[:, k, :],
                                                 start=(k == 0), stop=(k == KD - 1))
                            if f == 3:
                                last.then_inc(half_d, 1)
                        last.then_inc(d_mm, 1)
                    pe.wait_ge(ye_ok, 6 * e + 4)
                    rows_back(*TRIOS[1])
                    pe.wait_ge(ye_ok, 6 * e + 6)
                    rows_back(*TRIOS[2]).then_inc(back, 1)
                turns(pe, body)

            @block.scalar
            def _(act):
                def tokens(e):
                    act.wait_ge(x_mm, 3 * e + 2)
                    for k in range(4, KD):
                        act.activation(xT[:, k, 0:CAP_S], PS[:, 7, P * (k - 4):P * (k - 3)], ACT.Identity,
                                       scale=g.gain[:, layer, 1, k, 1:2], bias=g.shift[:, layer, 1, k, 1:2]).then_inc(xa_ok, 1)
                tokens(0)

                def body(e, more):
                    for q, (a, b) in enumerate(TRIOS):
                        act.wait_ge(gu_mm, 3 * e + q + 1)
                        act.activation(sg[:, a:b], trio(q, a, b), ACT.Silu).then_inc(sg_ok, 1)
                    if more:
                        tokens(e + 1)
                    act.wait_ge(back, e + 1)
                    act.wait_ge(ys_out, 16 * e)
                    for half in range(2):
                        act.activation(y_s[:, 512 * half:512 * half + 512], PS[:, 6 + half, :], ACT.Copy,
                                       scale=g.gate_s[:, bass.ds(e, 1)]).then_inc(ys_ok, 1)
                turns(act, body)

            @block.vector
            def _(dve):
                def tokens(e):
                    dve.wait_ge(x_mm, 3 * e + 1)
                    for k in range(4):
                        dve.tensor_scalar(xT[:, k, 0:CAP_S], PS[:, 6, P * k:P * k + P], g.gain[:, layer, 1, k, 1:2],
                                          g.shift[:, layer, 1, k, 1:2], ALU.mult, ALU.add).then_inc(xd_ok, 1)
                    dve.wait_ge(x_mm, 3 * e + 3)
                    dve.tensor_tensor(xT[:, :, CAP_S:CAP], PS[:, 3, 0:P].rearrange("p (k c) -> p k c", k=KD),
                                      g.gain[:, layer, 1, :, 0:1].to_broadcast([P, KD, CAP_P]), ALU.mult).then_inc(xd_ok, 1)
                    dve.wait_ge(xd_ok, 6 * e + 5)
                    dve.tensor_tensor(xT[:, :, CAP_S:CAP], xT[:, :, CAP_S:CAP],
                                      g.shift[:, layer, 1, :, 0:1].to_broadcast([P, KD, CAP_P]), ALU.add).then_inc(xd_ok, 1)
                tokens(0)

                def body(e, more):
                    for q, (a, b) in enumerate(TRIOS):
                        dve.wait_ge(sg_ok, 3 * e + q + 1)
                        dve.tensor_tensor(hid[:, a:b], sg[:, a:b], trio(3 + q, a, b), ALU.mult).then_inc(hid_ok, 1)
                    if more:
                        tokens(e + 1)
                    for q, (a, b) in enumerate(TRIOS):
                        dve.wait_ge(d_mm, 3 * e + q + 1)
                        for c0, c1, j in ((0, CAP_S, 1), (CAP_S, CAP, 0)):
                            dve.tensor_tensor(ye[:, a:b, c0:c1], trio(q, a, b)[:, :, c0:c1],
                                              g.modc[:, layer, 40 + a:40 + b, j:j + 1].to_broadcast([P, b - a, c1 - c0]),
                                              ALU.mult).then_inc(ye_ok, 1)
                    dve.wait_ge(back, e + 1)
                    dve.wait_ge(yp_out, 16 * e)
                    dve.tensor_scalar(y_p[:].rearrange("p (h n) -> p h n", h=2), PS[0:CAP_P, 4:6, :],
                                      g.gate_p[:, bass.ds(e, 1)], None, ALU.mult).then_inc(yp_ok, 1)
                turns(dve, body)

def ssm_gate_and_steps(nc, g, io, hT, q):
    with Stage(nc, "ssmz") as st:
        WZ = 256
        w = st.sb("w", [P, 2, KD, WZ])
        w_hi = st.sb("w_hi", [P, 2, KD, WZ], F32R)
        w_lo = st.sb("w_lo", [P, 2, KD, WZ], F32R)
        zs = st.sb("zs", [P, 3, WZ])
        wdt = st.sb("wdt", [P, KD, 2 * SH])
        wdt_hi = st.sb("wdt_hi", [P, KD, 2 * SH], F32R)
        wdt_lo = st.sb("wdt_lo", [P, KD, 2 * SH], F32R)
        bias = st.sb("bias", [P, 2 * SH])
        alog = st.sb("alog", [P, 2 * SH])
        a = st.sb("a", [P, 2 * SH])
        N2 = 2 * NB * SH
        v, e, s2, q2, pw = (st.sb(n, [P, N2]) for n in ("v", "e", "s2", "q2", "pw"))
        diff = st.sb("diff", [P, 2, NB, SH])
        w_in = [st.sem("w_in0"), st.sem("w_in1")]
        hi_ok, lo_ok, dt_hi, dt_lo = st.sem("hi_ok"), st.sem("lo_ok"), st.sem("dt_hi"), st.sem("dt_lo")
        small, z_mm, z_ok = st.sem("small"), st.sem("z_mm"), st.sem("z_ok")
        z_out = [st.sem(f"z_out{i}") for i in range(3)]
        dt_mm, v_ok, e_ok, a_ok = st.sem("dt_mm"), st.sem("v_ok"), st.sem("e_ok"), st.sem("a_ok")
        chain, power, cum, exps = st.sem("chain"), st.sem("power"), st.sem("cum"), st.sem("exps")
        PS = g.PS
        w_dram = io["ssm_w_in"][0].rearrange("(k p) n -> p k n", p=P)
        NC_ = DI // WZ
        h_hi, h_lo = hT

        def chunks(eng, body):
            with eng.Fori(0, NC_ // 2 - 1) as i:
                for u in range(2):
                    body(i, u, True)
            body(NC_ // 2 - 1, 0, True)
            body(NC_ // 2 - 1, 1, False)

        def tokens(k, b):
            return h_hi[:, k, P * b:P * b + P], h_lo[:, k, P * b:P * b + P]

        with nc.Block(no_gpsimd_drain=True) as block:
            @block.sync
            def _(sp):
                sp.dma_start(wdt[:], w_dram[:, :, DI + CONV:IN_DIM]).then_inc(small, 16)
                sp.dma_start(bias[:], io["ssm_dt_bias"][0].rearrange("d h -> (d h)").partition_broadcast(P)).then_inc(small, 16)
                sp.dma_start(alog[:], io["ssm_a_log"][0].rearrange("d h -> (d h)").partition_broadcast(P)).then_inc(small, 16)
                sp.dma_start(q.skip[:], io["ssm_d_skip"][0].partition_broadcast(P)).then_inc(small, 16)
                for u in range(2):
                    sp.dma_start(w[:, u], w_dram[:, :, WZ * u:WZ * u + WZ]).then_inc(w_in[u], 16)
                with sp.Fori(1, NC_ // 2) as i:
                    for u in range(2):
                        sp.wait_ge(lo_ok, 2 * i + u - 1)
                        sp.dma_start(w[:, u], w_dram[:, :, bass.ds(i * 2 * WZ + WZ * u, WZ)]).then_inc(w_in[u], 16)

            @block.gpsimd
            def _(pool):
                with pool.Fori(0, NC_ // 2) as i:
                    for u in range(2):
                        for b in range(NB):
                            pool.wait_ge(z_ok, 2 * NB * i + NB * u + b + 1)
                            pool.dma_start(g.z[P * b:P * b + P, bass.ds(i * 2 * WZ + WZ * u, WZ)], zs[:, b % 3]
                                           ).then_inc(z_out[b % 3], 16)
                for s in z_out:
                    pool.wait_ge(s, 16 * NC_ * NB // 3)

            @block.tensor
            def _(pe):
                pe.wait_ge(dt_lo, 1)
                for b in range(NB):
                    for k in range(KD):
                        last = exact_products(pe, PS[:, 4 + b // 8, 64 * (b % 8):64 * (b % 8) + 64], tokens(k, b),
                                              (wdt_hi[:, k], wdt_lo[:, k]), k == 0, k == KD - 1)
                last.then_inc(dt_mm, 1)
                pe.wait_ge(v_ok, 4)
                with pe.Fori(0, NC_ // 2) as i:
                    for u in range(2):
                        pe.wait_ge(lo_ok, 2 * i + u + 1)
                        for b in range(NB):
                            if b < 4:
                                pe.wait_ge(z_ok, 2 * NB * i)
                            else:
                                pe.wait_ge(z_ok, 2 * NB * i + NB * u + b - 3)
                            for k in range(KD):
                                last = exact_products(pe, PS[:, 4 * u + b % 4, 0:WZ], tokens(k, b),
                                                      (w_hi[:, u, k], w_lo[:, u, k]), k == 0, k == KD - 1)
                            last.then_inc(z_mm, 1)
                pe.wait_ge(chain, 12)
                pe.wait_ge(z_ok, NC_ * NB)
                f = q.da[:].rearrange("p d b h -> p d (b h)")
                for d in range(2):
                    pe.matmul(PS[:, 6, 0:NB * SH], (g.upper, g.lower)[d][:], f[:, d], start=True, stop=True).then_inc(cum, 1)
                    pe.matmul(PS[:, 7, 0:NB * SH], g.ones[:], f[:, d], start=True, stop=True).then_inc(cum, 1)
                    pe.wait_ge(exps, 2 * d + 2)
                    pe.wait_ge(chain, 13 + d)

            @block.scalar
            def _(act):
                def rounded(turn, slot, used):
                    act.wait_ge(w_in[slot], 16 * turn + 16)
                    act.wait_ge(z_mm, used)
                    act.copy(w_hi[:, slot], w[:, slot]).then_inc(hi_ok, 1)

                act.wait_ge(small, 64)
                act.copy(wdt_hi[:], wdt[:]).then_inc(dt_hi, 1)
                act.activation(a[:], alog[:], ACT.Exp).then_inc(a_ok, 1)
                rounded(0, 0, 0)
                act.wait_ge(v_ok, 4)
                act.activation(e[:], v[:], ACT.Abs).then_inc(e_ok, 1)
                act.wait_ge(e_ok, 1)
                act.activation(e[:], e[:], ACT.Exp, scale=-1.0).then_inc(e_ok, 1)

                def body(i, u, more):
                    if more:
                        rounded(i + u, 1 - u, 2 * NB * i + NB * u)
                    for b in range(NB):
                        act.wait_ge(z_mm, 2 * NB * i + NB * u + b + 1)
                        act.wait_ge(z_out[b % 3], i * 96 + 48 * u + 16 * (b // 3))
                        act.activation(zs[:, b % 3], PS[:, 4 * u + b % 4, 0:WZ], ACT.Silu).then_inc(z_ok, 1)
                chunks(act, body)
                for d in range(2):
                    act.wait_ge(cum, 2 * d + 2)
                    ps = PS[:, 6:8, 0:NB * SH]
                    act.activation(q.grow[:, d].rearrange("p b h -> p (b h)"), ps[:, 0], ACT.Exp).then_inc(exps, 1)
                    act.activation(q.dec[:, d].rearrange("p b h -> p (b h)"), ps[:, 1], ACT.Exp).then_inc(exps, 1)
                act.wait_ge(chain, 14)
                act.activation(diff[:], diff[:], ACT.Exp).then_inc(exps, 1)

            @block.vector
            def _(dve):
                def rest(c, slot):
                    dve.wait_ge(hi_ok, c + 1)
                    dve.tensor_tensor(w_lo[:, slot], w[:, slot], w_hi[:, slot].bitcast(F32), ALU.subtract).then_inc(lo_ok, 1)

                dve.wait_ge(dt_hi, 1)
                dve.tensor_tensor(wdt_lo[:], wdt[:], wdt_hi[:].bitcast(F32), ALU.subtract).then_inc(dt_lo, 1)
                rest(0, 0)
                dve.wait_ge(dt_mm, 1)
                vv = v[:].rearrange("p (d b h) -> p d b h", d=2, b=NB)
                for d in range(2):
                    for b0, b1, bank in ((0, 8, 4), (8, 9, 5)):
                        dve.tensor_tensor(vv[:, d, b0:b1],
                                          PS[:, bank, 0:64 * (b1 - b0)].rearrange("p (b d h) -> p b d h", d=2, h=SH)[:, :, d],
                                          bias[:, SH * d:SH * d + SH].unsqueeze(1).to_broadcast([P, b1 - b0, SH]),
                                          ALU.add).then_inc(v_ok, 1)
                steps, powers = Steps(dve, chain), Steps(dve, power)
                dve.wait_ge(e_ok, 2)
                steps.alone(dve.tensor_scalar(s2[:], e[:], 2.0, None, ALU.add))
                steps.alone(dve.reciprocal(s2[:], s2[:]))
                steps.alone(dve.tensor_tensor(s2[:], s2[:], e[:], ALU.mult))
                steps.alone(dve.tensor_tensor(q2[:], s2[:], s2[:], ALU.mult))
                steps.alone(dve.tensor_scalar(pw[:], q2[:], 1.0 / 15, 1.0 / 13, ALU.mult, ALU.add))
                for c in (11, 9, 7, 5, 3):
                    powers.alone(dve.tensor_tensor(pw[:], pw[:], q2[:], ALU.mult))
                    powers.alone(dve.tensor_scalar(pw[:], pw[:], 1.0 / c, None, ALU.add))
                steps.alone(dve.tensor_tensor(pw[:], pw[:], q2[:], ALU.mult))
                steps.alone(dve.scalar_tensor_tensor(out=pw[:], in0=pw[:], scalar=1.0, in1=s2[:], op0=ALU.add, op1=ALU.mult))
                steps.alone(dve.tensor_scalar(v[:], v[:], 0.0, None, ALU.max))
                dt = q.dt[:].rearrange("p d b h -> p (d b h)")
                steps.alone(dve.scalar_tensor_tensor(out=dt, in0=pw[:], scalar=2.0, in1=v[:], op0=ALU.mult, op1=ALU.add))
                dve.wait_ge(a_ok, 1)
                steps.alone(dve.tensor_scalar(a[:], a[:], -1.0, None, ALU.mult))
                for d in range(2):
                    steps.did(dve.tensor_tensor(q.da[:, d], q.dt[:, d],
                                                a[:, SH * d:SH * d + SH].unsqueeze(1).to_broadcast([P, NB, SH]), ALU.mult))
                steps.settle()
                assert steps.n == 12
                with dve.Fori(0, NC_ // 2 - 1) as i:
                    rest(2 * i + 1, 1)
                    rest(2 * i + 2, 0)
                rest(NC_ - 1, 1)
                for d in range(2):
                    dve.wait_ge(exps, 2 * d + 2)
                    dd = diff[:, d].rearrange("p b h -> p (b h)")
                    powers.alone(dve.tensor_copy(dd, PS[:, 7, 0:NB * SH]))
                    steps.alone(dve.tensor_tensor(dd, dd, PS[:, 6, 0:NB * SH], ALU.subtract))
                dve.wait_ge(exps, 5)
                dve.tensor_tensor(q.toend[:], diff[:], q.dt[:], ALU.mult).then_inc(a_ok, 1)


def ssm_conv(nc, g, io, hT):
    with Stage(nc, "conv") as st:
        w = st.sb("w", [P, 2, KD, P])
        w_hi = st.sb("w_hi", [P, 2, KD, P], F32R)
        w_lo = st.sb("w_lo", [P, 2, KD, P], F32R)
        W = T + 4
        at_p, at_s = 1, SEQ + 3
        pre = st.sb("pre", [P, 2, W])
        acc = st.sb("acc", [P, 2, W])
        acc2 = st.sb("acc2", [P, W])
        act_ = st.sb("act", [P, 2, W])
        tok = st.sb("tok", [P, 2, NB, P])
        w_in = [st.sem("w_in0"), st.sem("w_in1")]
        hi_ok, lo_ok = st.sem("hi_ok"), st.sem("lo_ok")
        zero, mm, pre_ok, chain = st.sem("zero"), st.sem("mm"), st.sem("pre_ok"), st.sem("chain")
        acc_ok, silu_ok, tp, ta_ok, td_ok = st.sem("acc_ok"), st.sem("silu_ok"), st.sem("tp"), st.sem("ta_ok"), st.sem("td_ok")
        saved_t = [st.sem("saved_t0"), st.sem("saved_t1")]
        saved_c = [st.sem("saved_c0"), st.sem("saved_c1")]
        PS = g.PS
        w_dram = io["ssm_w_in"][0].rearrange("(k p) n -> p k n", p=P)

        h_hi, h_lo = hT

        def turns(eng, body):
            with eng.Fori(0, DI // 512) as i:
                body(4 * i, "x", i)
            body(DI // P, "b", DI // 512)
            body(DI // P + 4, "c", DI // 512 + 1)

        def cols(b):
            return slice(at_p, at_p + P) if b == 0 else slice(at_s + P * (b - 1), at_s + P * b)

        with nc.Block(no_gpsimd_drain=True) as block:
            @block.sync
            def _(sp):
                def load(m, s):
                    sp.dma_start(w[:, s], w_dram[:, :, bass.ds(m * P + DI, P)]).then_inc(w_in[s], 16)

                load(0, 0)
                load(1, 1)
                with sp.Fori(1, MC // 2) as i:
                    for s in range(2):
                        sp.wait_ge(lo_ok, 2 * i + s - 1)
                        load(2 * i + s, s)

            @block.gpsimd
            def _(pool):
                for s in range(2):
                    pool.memset(pre[:, s], 0.0).then_inc(zero, 1)

                def body(m0, kind, i):
                    for v in range(4):
                        if kind != "c":
                            pool.wait_ge(ta_ok, 4 * i + v + 1)
                            pool.wait_ge(td_ok, 8 * i + 2 * v + 2)
                            out = g.xs if kind == "x" else g.btok
                            c = bass.ds(m0 * P + P * v, P) if kind == "x" else slice(P * v, P * v + P)
                            pool.dma_start(out.rearrange("(b p) c -> p b c", p=P)[:, :, c], tok[:, v % 2]
                                           ).then_inc(saved_t[v % 2], 16)
                        if kind != "x":
                            pool.wait_ge(silu_ok, 4 * i + v + 1)
                            out = g.bT if kind == "b" else g.cT
                            s = saved_c[v % 2]
                            pool.dma_start(out[P * v:P * v + P, 0:SEQ], act_[:, v % 2, at_p:at_p + SEQ]).then_inc(s, 16)
                            pool.dma_start(out[P * v:P * v + P, SEQ:T], act_[:, v % 2, at_s:at_s + DEC]).then_inc(s, 16)
                turns(pool, body)
                for s in saved_t:
                    pool.wait_ge(s, 16 * 10)
                for s in saved_c:
                    pool.wait_ge(s, 16 * 8)

            @block.tensor
            def _(pe):
                def project(i, v, first=False):
                    pe.wait_ge(lo_ok, 4 * i + v + 1)
                    if not first:
                        pe.wait_ge(pre_ok, 4 * i + v - 1)
                    for t in range(NT):
                        c = slice(TILE * t, TILE * t + TILE)
                        for k in range(KD):
                            last = exact_products(pe, PS[:, 3 * (v % 2) + t, 0:TILE], (w_hi[:, v % 2, k], w_lo[:, v % 2, k]),
                                                  (h_hi[:, k, c], h_lo[:, k, c]), k == 0, k == KD - 1)
                    last.then_inc(mm, 1)

                def turn(i, v):
                    pe.wait_ge(silu_ok, 4 * i + v + 1)
                    pe.wait_ge(td_ok, 8 * i + 2 * v)
                    pe.wait_ge(ta_ok, 4 * i + v)
                    for b in range(NB):
                        if b == 8:
                            pe.wait_ge(td_ok, 8 * i + 2 * v + 1)
                        last = pe.transpose(PS[:, 6 + b // 4 % 2, P * (b % 4):P * (b % 4) + P], act_[:, v % 2, cols(b)], g.ident[:])
                        if b in (3, 7, 8):
                            last.then_inc(tp, 1)

                def body(m0, kind, i):
                    for v in range(1, 4):
                        project(i, v)
                        if kind != "c":
                            turn(i, v - 1)
                    if kind != "c":
                        project(i + 1, 0)
                        turn(i, 3)
                project(0, 0, first=True)
                turns(pe, body)

            @block.scalar
            def _(act):

                def rounded(i, v, first=False):
                    act.wait_ge(w_in[v % 2], 32 * i + 16 * (v // 2) + 16)
                    if not first:
                        act.wait_ge(mm, 4 * i + v - 1)
                    act.copy(w_hi[:, v % 2], w[:, v % 2]).then_inc(hi_ok, 1)

                def take(i, v, first=False):
                    act.wait_ge(mm, 4 * i + v + 1)
                    if not first:
                        act.wait_ge(acc_ok, 4 * i + v - 1)
                    s, b0 = v % 2, 3 * (v % 2)
                    act.copy(pre[:, s, at_p:at_p + SEQ], PS[:, b0, 0:SEQ])
                    act.copy(pre[:, s, at_s:at_s + TILE - SEQ], PS[:, b0, SEQ:TILE])
                    act.copy(pre[:, s, at_s + TILE - SEQ:at_s + DEC].rearrange("p (t n) -> p t n", t=2),
                             PS[:, b0 + 1:b0 + 3, 0:TILE]).then_inc(pre_ok, 1)

                def silu(i, v, kind, first=False):
                    act.wait_ge(acc_ok, 4 * i + v + 1)
                    if kind != "c" and not first:
                        act.wait_ge(tp, 12 * i + 3 * (v - 1))
                    if kind == "b" and v >= 2:
                        act.wait_ge(saved_c[v % 2], 32)
                    if kind == "c":
                        act.wait_ge(saved_c[v % 2], 64 + 32 * (v // 2))
                    act.activation(act_[:, v % 2, 1:W - 1], acc[:, v % 2, 1:W - 1], ACT.Silu).then_inc(silu_ok, 1)

                def turned(i, v):
                    act.wait_ge(tp, 12 * i + 3 * v + 2)
                    act.wait_ge(saved_t[v % 2], 32 * i + 16 * (v // 2))
                    act.copy(tok[:, v % 2, 4:8], PS[:, 7, :].rearrange("p (b c) -> p b c", c=P)).then_inc(ta_ok, 1)

                def body(m0, kind, i):
                    for v in range(1, 4):
                        if kind != "c" or v < 3:
                            rounded(i + (v + 1) // 4, (v + 1) % 4)
                        take(i, v)
                        if kind != "c":
                            turned(i, v - 1)
                        silu(i, v, kind)
                    if kind != "c":
                        rounded(i + 1, 1)
                        take(i + 1, 0)
                        turned(i, 3)
                        silu(i + 1, 0, "c" if kind == "b" else "x")
                rounded(0, 0, first=True)
                rounded(0, 1, first=True)
                act.wait_ge(zero, 2)
                take(0, 0, first=True)
                silu(0, 0, "x", first=True)
                turns(act, body)

            @block.vector
            def _(dve):
                def rest(i, v):
                    dve.wait_ge(hi_ok, 4 * i + v + 1)
                    dve.tensor_tensor(w_lo[:, v % 2], w[:, v % 2], w_hi[:, v % 2].bitcast(F32), ALU.subtract).then_inc(lo_ok, 1)

                def convolve(m0, i, v, first=False):
                    s = v % 2
                    m = m0 + v
                    n = slice(1, W - 1)
                    wj = [g.convw[:, j, bass.ds(m, 1)] for j in range(3)]
                    steps = Steps(dve, chain, i, 8, 2 * v)
                    dve.wait_ge(pre_ok, 4 * i + v + 1)
                    if not first:
                        dve.wait_ge(silu_ok, 4 * i + v - 1)
                    steps.alone(dve.tensor_scalar(acc[:, s, n], pre[:, s, n], wj[1], g.vcol[:, bass.ds(m + V_CB, 1)],
                                                  ALU.mult, ALU.add))
                    steps.alone(dve.scalar_tensor_tensor(out=acc2[:, n], in0=pre[:, s, 0:W - 2], scalar=wj[0],
                                                         in1=acc[:, s, n], op0=ALU.mult, op1=ALU.add))
                    dve.scalar_tensor_tensor(out=acc[:, s, n], in0=pre[:, s, 2:W], scalar=wj[2],
                                             in1=acc2[:, n], op0=ALU.mult, op1=ALU.add).then_inc(acc_ok, 1)

                def turned(i, v):
                    dve.wait_ge(tp, 12 * i + 3 * v + 1)
                    dve.wait_ge(saved_t[v % 2], 32 * i + 16 * (v // 2))
                    dve.tensor_copy(tok[:, v % 2, 0:4], PS[:, 6, :].rearrange("p (b c) -> p b c", c=P)).then_inc(td_ok, 1)
                    dve.wait_ge(tp, 12 * i + 3 * v + 3)
                    dve.tensor_copy(tok[:, v % 2, 8], PS[:, 6, 0:P]).then_inc(td_ok, 1)

                def body(m0, kind, i):
                    for v in range(1, 4):
                        if kind != "c" or v < 3:
                            rest(i + (v + 1) // 4, (v + 1) % 4)
                        if kind != "c":
                            turned(i, v - 1)
                        convolve(m0, i, v)
                    if kind != "c":
                        rest(i + 1, 1)
                        turned(i, 3)
                        convolve(m0 + 4, i + 1, 0)
                rest(0, 0)
                rest(0, 1)
                convolve(0, 0, 0, first=True)
                turns(dve, body)


def ssm_states(nc, g, io, q):
    NQ = DEC // P
    with Stage(nc, "states") as st:
        x = st.sb("x", [P, 2, 2, DI])
        b_ = st.sb("b", [P, 2, 2, GN])
        xw = st.sb("xw", [P, 2, DI])
        h = st.sb("h", [P, 2, 2, DI])
        raw = st.sb("raw", [P, 2, DI // P, NS])
        fin = st.sb("fin", [P, 2, DI // P, NS])
        x_in = [[st.sem(f"x_in{d}{u}") for u in range(2)] for d in range(2)]
        raw_in, init_mm, init_ok = st.sem("raw_in"), st.sem("init_mm"), st.sem("init_ok")
        xw_ok = [st.sem("xw_ok0"), st.sem("xw_ok1")]
        s_mm = [st.sem("s_mm0"), st.sem("s_mm1")]
        h_ok = [st.sem("h_ok0"), st.sem("h_ok1")]
        dec_ok = [st.sem("dec_ok0"), st.sem("dec_ok1")]
        h_out = [[st.sem(f"h_out{d}{u}") for u in range(2)] for d in range(2)]
        fin_mm, fin_ok, fin_out, zero = st.sem("fin_mm"), st.sem("fin_ok"), st.sem("fin_out"), st.sem("zero")
        PS = g.PS
        NBK = DI // P

        def loop(eng, body):
            with eng.Fori(0, NQ // 2) as i:
                for u in range(2):
                    body(2 * i + u, u, (2 * i + u + 1, i * -2 + NQ - u))
            body(NQ, 0, (0, 0))

        def rows(b, n):
            return bass.ds(b * P, P) if n is not NQ else slice(0, P)

        with nc.Block(no_gpsimd_drain=True) as block:
            @block.sync
            def _(sp):
                for d in range(2):
                    sp.dma_start(raw[:, d], io["state_ssm"][0, 0, d].rearrange("h p n -> (h p) n").rearrange(
                        "(m q) n -> q m n", q=P)).then_inc(raw_in, 16)

                def body(n, u, bs):
                    for d in range(2):
                        sp.wait_ge(s_mm[d], n)
                        sp.dma_start(x[:, d, u], g.xs[rows(bs[d], n), :]).then_inc(x_in[d][u], 16)
                        sp.dma_start(b_[:, d, u], g.btok[rows(bs[d], n), :]).then_inc(x_in[d][u], 16)
                loop(sp, body)

            @block.gpsimd
            def _(pool):
                def body(n, u, bs):
                    for d in range(2):
                        pool.wait_ge(x_in[d][u], 16 * n + 32 - 16 * u)
                        pool.wait_ge(s_mm[d], n + 1)
                        te = q.toend[:, d, bass.ds(bs[d], 1)] if n is not NQ else q.toend[:, d, 0:1]
                        pool.tensor_tensor(xw[:, d].rearrange("p (h c) -> p h c", c=HD),
                                           x[:, d, u].rearrange("p (h c) -> p h c", c=HD),
                                           te.squeeze(1).unsqueeze(2).to_broadcast([P, SH, HD]), ALU.mult).then_inc(xw_ok[d], 1)
                loop(pool, body)

            @block.tensor
            def _(pe):
                pe.wait_ge(raw_in, 32)
                for d in range(2):
                    pe.sem_inc(s_mm[d], 1)
                for d in range(2):
                    for m in range(NBK):
                        last = pe.transpose(PS[:, 4 * d + m // 4, P * (m % 4):P * (m % 4) + P], raw[:, d, m], g.ident[:])
                    last.then_inc(init_mm, 1)

                def body(n, u, bs):
                    for d in range(2):
                        pe.wait_ge(xw_ok[d], n + 1)
                        pe.wait_ge(h_ok[d], n + 1)
                        for k in range(SG):
                            last = pe.matmul(PS[:, 4 * d + k, :], b_[:, d, u, NS * k:NS * k + NS], xw[:, d, 512 * k:512 * k + 512],
                                             start=True, stop=True)
                        last.then_inc(s_mm[d], 1)
                loop(pe, body)
                for d in range(2):
                    pe.wait_ge(h_ok[d], NQ + 3)
                    for m in range(NBK):
                        last = pe.transpose(PS[:, 4 * d + m // 4, P * (m % 4):P * (m % 4) + P], h[:, d, 1, P * m:P * m + P], g.ident[:])
                    last.then_inc(fin_mm, 1)

            @block.vector
            def _(dve):
                for d in range(2):
                    dve.wait_ge(init_mm, d + 1)
                    dve.tensor_copy(h[:, d, 0].rearrange("p (b c) -> p b c", b=4), PS[:, 4 * d:4 * d + 4, :]).then_inc(h_ok[d], 1)

                def body(n, u, bs):
                    for d in range(2):
                        if n is NQ:
                            dve.wait_ge(h_out[d][1], 16 * (NQ // 2))
                            dve.memset(h[:, d, 0], 0.0).then_inc(h_ok[d], 1)
                            dve.wait_ge(h_ok[d], NQ + 2)
                            dec = q.dec[:, d, 0]
                            ready = n + 3
                        else:
                            dec = q.dec[:, d, bass.ds(bs[d], 1)].squeeze(1)
                            dve.wait_ge(h_ok[d], n + 1)
                            ready = n + 2
                            if u == 0:
                                dve.wait_ge(h_out[d][1], 8 * n)
                            else:
                                dve.wait_ge(h_out[d][0], 8 * n + 8)
                        new = h[:, d, 1 - u].rearrange("p (h c) -> p h c", c=HD)
                        dve.tensor_tensor(new, h[:, d, u].rearrange("p (h c) -> p h c", c=HD),
                                          dec.unsqueeze(2).to_broadcast([P, SH, HD]), ALU.mult).then_inc(dec_ok[d], 1)
                        dve.wait_ge(dec_ok[d], n + 1)
                        dve.wait_ge(s_mm[d], n + 2)
                        hb = h[:, d, 1 - u].rearrange("p (b c) -> p b c", b=4)
                        dve.tensor_tensor(hb, hb, PS[:, 4 * d:4 * d + 4, :], ALU.add).then_inc(h_ok[d], 1)
                loop(dve, body)
                for d in range(2):
                    dve.wait_ge(fin_mm, d + 1)
                    dve.tensor_copy(fin[:, d].rearrange("p (b m) n -> p b (m n)", b=4), PS[:, 4 * d:4 * d + 4, :]).then_inc(fin_ok, 1)

            @block.scalar
            def _(act):
                def body(n, u, bs):
                    for d in range(2):
                        if n is NQ:
                            act.wait_ge(h_ok[d], n + 2)
                            act.dma_start(g.hin[d, 0], h[:, d, u]).then_inc(h_out[d][u], 16)
                        else:
                            act.wait_ge(h_ok[d], n + 1)
                            act.dma_start(g.hin[d, bass.ds(bs[d], 1)].squeeze(0), h[:, d, u]).then_inc(h_out[d][u], 16)
                loop(act, body)
                for d in range(2):
                    act.wait_ge(fin_ok, d + 1)
                    act.dma_start(io["new_ssm"][0, 0, d].rearrange("h p n -> (h p) n").rearrange("(m q) n -> q m n", q=P),
                                  fin[:, d]).then_inc(fin_out, 16)
                for d in range(2):
                    act.wait_ge(h_out[d][0], 16 * (NQ // 2 + 1))
                    act.wait_ge(h_out[d][1], 16 * (NQ // 2))
                act.wait_ge(fin_out, 32)


def ssm_outputs(nc, g, io, q):
    with Stage(nc, "ssd") as st:
        x = st.sb("x", [P, 2, DI])
        z = st.sb("z", [P, 2, DI])
        hin = st.sb("hin", [P, 2, 2, DI])
        bT = st.sb("bT", [P, 2, SG, P])
        cT = st.sb("cT", [P, 2, SG, P])
        tri = st.sb("tri", [P, 2, P])
        cb = st.sb("cb", [P, 2, 2, SG, P])
        seg = st.sb("seg", [P, 2, 2, HPG, P])
        ex = st.sb("ex", [P, 2, HPG, P])
        cd = st.sb("cd", [P, 2, HPG, P])
        wt = st.sb("wt", [P, 2, HPG, P])
        t1 = st.sb("t1", [P, 2, 512])
        t2 = st.sb("t2", [P, 2, 512])
        t3 = st.sb("t3", [P, 512])
        y = st.sb("y", [P, 2, DI])
        ld = [st.sem("ld0"), st.sem("ld1")]
        tri_ok, cb_mm, cb_ok = st.sem("tri_ok"), st.sem("cb_mm"), st.sem("cb_ok")
        seg_ok, seg_mm, ex_ok, wt_ok = st.sem("seg_ok"), st.sem("seg_mm"), st.sem("ex_ok"), st.sem("wt_ok")
        cd_ok, cw_ok = st.sem("cd_ok"), st.sem("cw_ok")
        yd_mm, off_mm, t_ok, u_ok = st.sem("yd_mm"), st.sem("off_mm"), st.sem("t_ok"), st.sem("u_ok")
        p_ok, y_ok, gt_ok = st.sem("p_ok"), st.sem("y_ok"), st.sem("gt_ok")
        y_out = [st.sem("y_out0"), st.sem("y_out1")]
        PS = g.PS

        def heads(ap):
            return ap.rearrange("p (h c) -> p h c", c=HD)

        def at(t, d, n, h0=0, h1=SH):
            return t[:, d, bass.ds(n, 1), h0:h1].squeeze(1)

        def chunks(eng, body):
            with eng.Fori(0, NB // 2) as i:
                for u in range(2):
                    body(2 * i + u, u, True)
            body(NB - 1, 0, False)

        def loaded(eng, n, u):
            wait_alone(eng, ld[u], 48 * n + 96 - 48 * u)

        with nc.Block(no_gpsimd_drain=True) as block:
            @block.sync
            def _(sp):
                def loads(n, u, first=False):
                    rows = bass.ds(n * P, P)
                    if not first:
                        sp.wait_ge(gt_ok, 4 * n)
                    sp.dma_start(bT[:, u], g.bT.rearrange("(k p) t -> p k t", p=P)[:, :, rows]).then_inc(ld[u], 16)
                    sp.dma_start(cT[:, u], g.cT.rearrange("(k p) t -> p k t", p=P)[:, :, rows]).then_inc(ld[u], 16)
                    sp.dma_start(x[:, u], g.xs[rows, :]).then_inc(ld[u], 16)
                    for d in range(2):
                        sp.dma_start(hin[:, u, d], g.hin[d, bass.ds(n, 1)].squeeze(0)).then_inc(ld[u], 16)
                    sp.dma_start(z[:, u], g.z[rows, :]).then_inc(ld[u], 16)

                loads(0, 0, first=True)

                def body(n, u, more):
                    if more:
                        loads(n + 1, 1 - u)
                    sp.wait_ge(gt_ok, 4 * n + 8)
                    sp.dma_start(g.y[bass.ds(n * P, P), :], y[:, u]).then_inc(y_out[u], 16)
                chunks(sp, body)
                sp.wait_ge(y_out[0], 16 * 5)
                sp.wait_ge(y_out[1], 16 * 4)

            @block.tensor
            def _(pe):
                def products(n, u):
                    loaded(pe, n, u)
                    for k in range(SG):
                        last = pe.matmul(PS[:, 5, P * k:P * k + P], bT[:, u, k], cT[:, u, k], start=True, stop=True)
                    last.then_inc(cb_mm, 1)

                def segments(n, k, first=False):
                    if not first:
                        pe.wait_ge(ex_ok, 4 * n + k - 1)
                    for d in range(2):
                        pe.wait_ge(seg_ok, 8 * n + 2 * k + d + 1)
                        for half in range(2):
                            last = pe.matmul(PS[:, 1 + 2 * (k % 2) + half, :], tri[:, d],
                                             seg[:, k % 2, d, 4 * half:4 * half + 4].rearrange("p h i -> p (h i)"),
                                             start=(d == 0), stop=(d == 1))
                        last.then_inc(seg_mm, 1)

                pe.wait_ge(tri_ok, 2)
                products(0, 0)
                segments(0, 0, first=True)

                def body(n, u, more):
                    for k in range(SG):
                        if k + 1 < SG:
                            segments(n, k + 1)
                        pe.wait_ge(t_ok, 12 * n + max(0, 3 * k - 1))
                        for d in range(2):
                            last = pe.matmul(PS[:, 6 + d, :], cT[:, u, k], hin[:, u, d, 512 * k:512 * k + 512], start=True, stop=True)
                        last.then_inc(off_mm, 1)
                        if more and k == SG - 1:
                            pe.wait_ge(t_ok, 12 * n + 9)
                            products(n + 1, 1 - u)
                            segments(n + 1, 0)
                        pe.wait_ge(wt_ok, 4 * n + k + 1)
                        for h in range(HPG):
                            c0 = 512 * k + HD * h
                            last = pe.matmul(PS[:, 5 - 5 * (k % 2), HD * h:HD * h + HD], wt[:, k % 2, h],
                                             x[:, u, c0:c0 + HD], start=True, stop=True)
                        last.then_inc(yd_mm, 1)
                chunks(pe, body)

            @block.gpsimd
            def _(pool):
                pool.affine_select(out=tri[:, 0], in_=g.ones[:], compare_op=ALU.is_gt, fill=0.0, base=0,
                                   pattern=[[-1, P]], channel_multiplier=1).then_inc(tri_ok, 1)
                pool.affine_select(out=tri[:, 1], in_=g.ones[:], compare_op=ALU.is_gt, fill=0.0, base=0,
                                   pattern=[[1, P]], channel_multiplier=-1).then_inc(tri_ok, 1)

                def build(n, k, first=False):
                    for d in range(2):
                        c = 8 * n + 2 * k + d
                        if not first:
                            pool.wait_ge(seg_mm, c - 3)
                        pool.tensor_tensor(seg[:, k % 2, d], (g.upper, g.lower)[d][:].unsqueeze(1).to_broadcast([P, HPG, P]),
                                           at(q.da, d, n, HPG * k, HPG * k + HPG).unsqueeze(2).to_broadcast([P, HPG, P]),
                                           ALU.mult).then_inc(seg_ok, 1)

                def finish(n, u, k):
                    c = 4 * n + k
                    if k == 0:
                        loaded(pool, n, u)
                        pool.wait_ge(y_out[u], 8 * n if u == 0 else 8 * n - 8)
                    cs = slice(512 * k, 512 * k + 512)
                    pool.wait_ge(y_ok, c)
                    pool.tensor_tensor(heads(t3[:]), heads(x[:, u, cs]),
                                       q.skip[:, HPG * k:HPG * k + HPG].unsqueeze(2).to_broadcast([P, HPG, HD]),
                                       ALU.mult).then_inc(p_ok, 1)
                    pool.wait_ge(p_ok, 2 * c + 1)
                    pool.wait_ge(t_ok, 3 * c + 2)
                    pool.tensor_tensor(t3[:], t3[:], t2[:, k % 2], ALU.add).then_inc(p_ok, 1)
                    pool.wait_ge(p_ok, 2 * c + 2)
                    pool.wait_ge(t_ok, 3 * c + 3)
                    pool.tensor_tensor(y[:, u, cs], t3[:], t1[:, k % 2], ALU.add).then_inc(y_ok, 1)

                build(0, 0, first=True)
                build(0, 1, first=True)

                def body(n, u, more):
                    for k in range(SG):
                        if k + 2 < SG:
                            build(n, k + 2)
                        elif more:
                            build(n + 1, k - 2)
                        finish(n, u, k)
                chunks(pool, body)

            @block.scalar
            def _(act):
                def exps(n, u, k, first=False):
                    c = 4 * n + k
                    act.wait_ge(cb_ok, 2 * n + 2)
                    if not first:
                        act.wait_ge(wt_ok, c - 1)
                    for h in range(HPG):
                        hh = HPG * k + h
                        last = act.activation(cd[:, k % 2, h], cb[:, u, 1, k], ACT.Copy, scale=at(q.dt, 1, n, hh, hh + 1))
                    last.then_inc(cd_ok, 1)
                    act.wait_ge(seg_mm, 2 * c + 2)
                    act.activation(ex[:, k % 2].rearrange("p (b h) i -> p b (h i)", b=2),
                                   PS[:, 1 + 2 * (k % 2):3 + 2 * (k % 2), :], ACT.Exp).then_inc(ex_ok, 1)

                exps(0, 0, 0, first=True)

                def body(n, u, more):
                    for k in range(1, SG):
                        exps(n, u, k)
                    if more:
                        exps(n + 1, 1 - u, 0)
                chunks(act, body)

            @block.vector
            def _(dve):
                def masked(n, u):
                    dve.wait_ge(cb_mm, n + 1)
                    for d in range(2):
                        dve.tensor_tensor(cb[:, u, d], PS[:, 5, :].rearrange("p (k i) -> p k i", k=SG),
                                          (g.upper, g.lower)[d][:].unsqueeze(1).to_broadcast([P, SG, P]), ALU.mult).then_inc(cb_ok, 1)

                def weights(n, u, k, free):
                    c = 4 * n + k
                    dve.wait_ge(yd_mm, free)
                    dve.wait_ge(cd_ok, c + 1)
                    for h in range(HPG):
                        hh = HPG * k + h
                        last = dve.scalar_tensor_tensor(out=wt[:, k % 2, h], in0=cb[:, u, 0, k],
                                                        scalar=at(q.dt, 0, n, hh, hh + 1), in1=cd[:, k % 2, h],
                                                        op0=ALU.mult, op1=ALU.add)
                    last.then_inc(cw_ok, 1)
                    dve.wait_ge(cw_ok, c + 1)
                    dve.wait_ge(ex_ok, c + 1)
                    dve.tensor_tensor(wt[:, k % 2], wt[:, k % 2], ex[:, k % 2], ALU.mult).then_inc(wt_ok, 1)

                def parts(n, k):
                    c = 4 * n + k
                    dve.wait_ge(off_mm, c + 1)
                    if k < 2:
                        dve.wait_ge(y_ok, 4 * n)
                    else:
                        dve.wait_ge(y_ok, c - 1)
                    for d, t in ((0, t1), (1, t2)):
                        dve.tensor_tensor(heads(t[:, k % 2]), heads(PS[:, 6 + d, :]),
                                          at(q.grow, d, n, HPG * k, HPG * k + HPG).unsqueeze(2).to_broadcast([P, HPG, HD]),
                                          ALU.mult).then_inc(t_ok, 1)
                    dve.wait_ge(yd_mm, c + 1)
                    dve.wait_ge(t_ok, 3 * c + 2)
                    dve.tensor_tensor(t1[:, k % 2], t1[:, k % 2], PS[:, 5 - 5 * (k % 2), :], ALU.add).then_inc(t_ok, 1)

                def gate(n, u, k):
                    cs = slice(512 * k, 512 * k + 512)
                    dve.wait_ge(y_ok, 4 * n + k + 1)
                    dve.tensor_tensor(y[:, u, cs], y[:, u, cs], z[:, u, cs], ALU.mult).then_inc(gt_ok, 1)

                dve.sem_inc(gt_ok, SG)
                masked(0, 0)
                weights(0, 0, 0, 0)

                def body(n, u, more):
                    for k in range(SG):
                        if k + 1 < SG:
                            weights(n, u, k + 1, 4 * n + max(0, k))
                        elif more:
                            masked(n + 1, 1 - u)
                            weights(n + 1, 1 - u, 0, 4 * n + 3)
                        parts(n, k)
                        if k:
                            gate(n, u, k - 1)
                    gate(n, u, SG - 1)
                chunks(dve, body)


def ssm_out(nc, g, io, q):
    KI, KS = DI // P, 4

    def take(st, mm):
        y = st.sb("y", [P, 2, DI])
        yT = st.sb("yT", [P, 2, KI, P])
        y_hi, y_lo = (st.sb("yT" + half, [P, 2, KS, P], F32R) for half in ("_hi", "_lo"))
        hi_ok = st.sem("y_hi_ok")
        junk = st.sb("junk", [P, DI])
        ssq = st.sb("ssq", [P, NB])
        root = st.sb("root", [P, NB])
        rstd = st.sb("rstd", [P, NB])
        sq_ok, ms_ok, root_ok, rstd_ok = st.sem("sq_ok"), st.sem("ms_ok"), st.sem("root_ok"), st.sem("rstd_ok")
        y_in = [st.sem("y_in0"), st.sem("y_in1")]
        tp, ya_ok, yd_ok, yT_ok = st.sem("tp"), st.sem("ya_ok"), st.sem("yd_ok"), st.sem("yT_ok")
        PS = g.PS

        def col(t, b, grp):
            return t[:, bass.ds(b, 1)] if grp else t[:, 0:1]

        def sync(sp, n, u, b, grp):
            rows = bass.ds(b * P, P) if grp else slice(0, P)
            sp.wait_ge(tp, 2 * n)
            sp.wait_ge(sq_ok, n)
            sp.dma_start(y[:, u], g.y[rows, :]).then_inc(y_in[u], 16)

        def before_scalar(act):
            act.sem_inc(sq_ok, 1)

        def scalar(act, n, u, b, grp):
            act.wait_ge(y_in[u], 8 * n + 16 - 8 * u)
            act.wait_ge(sq_ok, n + 1)
            act.activation(junk[:], y[:, u], ACT.Square, accum_out=col(ssq, b, grp)).then_inc(sq_ok, 1)
            act.wait_ge(tp, 2 * n + 4)
            act.wait_ge(mm, n)
            for k in range(KI // 2, KI):
                last = act.activation(yT[:, u, k], PS[:, 4 + k // 4, P * (k % 4):P * (k % 4) + P], ACT.Copy,
                                      scale=g.vcol[:, V_SG + k:V_SG + k + 1])
            last.then_inc(ya_ok, 1)
            act.wait_ge(yd_ok, n + 1)
            act.wait_ge(ya_ok, n + 1)
            act.copy(y_hi[:, u], yT[:, u, 0:KS]).then_inc(hi_ok, 1)
            act.wait_ge(ms_ok, n + 1)
            act.activation(col(root, b, grp), col(ssq, b, grp), ACT.Sqrt).then_inc(root_ok, 1)

        def tensor(pe, n, u):
            if isinstance(n, int) and n == 0:
                pe.sem_inc(tp, 2)
            wait_alone(pe, y_in[u], 8 * n + 16 - 8 * u)
            pe.wait_ge(yT_ok, n)
            for k in range(KI):
                last = pe.transpose(PS[:, 4 + k // 4, P * (k % 4):P * (k % 4) + P], y[:, u, P * k:P * k + P], g.ident[:])
                if k % 8 == 7:
                    last.then_inc(tp, 1)

        def vector(dve, n, u):
            dve.wait_ge(tp, 2 * n + 3)
            dve.wait_ge(mm, n)
            for k in range(KI // 2):
                last = dve.tensor_scalar(yT[:, u, k], PS[:, 4 + k // 4, P * (k % 4):P * (k % 4) + P],
                                         g.vcol[:, V_SG + k:V_SG + k + 1], None, ALU.mult)
            last.then_inc(yd_ok, 1)
            dve.wait_ge(hi_ok, n + 1)
            dve.tensor_tensor(y_lo[:, u], yT[:, u, 0:KS], y_hi[:, u].bitcast(F32), ALU.subtract).then_inc(yT_ok, 1)

        def factor(dve, n, u, b, grp):
            dve.wait_ge(sq_ok, n + 2)
            dve.tensor_scalar(col(ssq, b, grp), col(ssq, b, grp), 1.0 / DI, EPS, ALU.mult, ALU.add).then_inc(ms_ok, 1)
            dve.wait_ge(root_ok, n + 1)
            dve.reciprocal(col(rstd, b, grp), col(root, b, grp)).then_inc(rstd_ok, 1)
            dve.wait_ge(rstd_ok, n + 1)
            return col(rstd, b, grp)

        return (y_hi, y_lo, yT[:, :, KS:KI]), yT_ok, {"sync": sync, "scalar": scalar, "tensor": tensor, "vector": vector, "factor": factor,
                           "before_scalar": before_scalar}
    project_out(nc, g, io, "wout", 1, KI, KS, io["ssm_w_out"][0], take)


def final_norm(nc, g, io):
    with Stage(nc, "final") as st:
        x = st.sb("x", [P, NB, D])
        junk = st.sb("junk", [P, D])
        gain = st.sb("gain", [P, D])
        ssq = st.sb("ssq", [P, NB])
        root = st.sb("root", [P, NB])
        rstd = st.sb("rstd", [P, NB])
        x_in = [st.sem(f"x_in{i}") for i in range(3)]
        gain_in, sq, ms, rt, rs = st.sem("gain_in"), st.sem("sq"), st.sem("ms"), st.sem("rt"), st.sem("rs")
        y_ok, y_out = st.sem("y_ok"), st.sem("y_out")
        with nc.Block(no_gpsimd_drain=True) as block:
            @block.sync
            def _(sp):
                for i in range(3):
                    sp.dma_start(x[:, 3 * i:3 * i + 3], g.res.rearrange("(b p) d -> p b d", p=P)[:, 3 * i:3 * i + 3]
                                 ).then_inc(x_in[i], 16)
                    if i == 0:
                        sp.dma_start(gain[:], io["final_norm_g"].partition_broadcast(P)).then_inc(gain_in, 16)
                sp.wait_ge(y_ok, 1)
                sp.dma_start(io["y_prompt"][0], x[:, 0]).then_inc(y_out, 16)
                for b in range(1, NB):
                    sp.wait_ge(y_ok, b + 1)
                    sp.dma_start(io["y_sample"][0, P * (b - 1):P * b], x[:, b]).then_inc(y_out, 16)
                sp.wait_ge(y_out, 16 * NB)

            @block.scalar
            def _(act):
                for i in range(3):
                    act.wait_ge(x_in[i], 16)
                    for b in range(3 * i, 3 * i + 3):
                        if b:
                            act.wait_ge(sq, b)
                        act.activation(junk[:], x[:, b], ACT.Square, accum_out=ssq[:, b:b + 1]).then_inc(sq, 1)
                    act.wait_ge(ms, i + 1)
                    act.activation(root[:, 3 * i:3 * i + 3], ssq[:, 3 * i:3 * i + 3], ACT.Sqrt).then_inc(rt, 1)

            @block.vector
            def _(dve):
                for i in range(3):
                    c = slice(3 * i, 3 * i + 3)
                    dve.wait_ge(sq, 3 * i + 3)
                    dve.tensor_scalar(ssq[:, c], ssq[:, c], 1.0 / D, EPS, ALU.mult, ALU.add).then_inc(ms, 1)
                    dve.wait_ge(rt, i + 1)
                    dve.reciprocal(rstd[:, c], root[:, c]).then_inc(rs, 1)
                    dve.wait_ge(rs, i + 1)
                    if i == 0:
                        dve.wait_ge(gain_in, 16)
                    for b in range(3 * i, 3 * i + 3):
                        dve.scalar_tensor_tensor(out=x[:, b], in0=x[:, b], scalar=rstd[:, b:b + 1], in1=gain[:],
                                                 op0=ALU.mult, op1=ALU.mult).then_inc(y_ok, 1)


class Shared:
    pass


def build(nc, io):
    g = Shared()
    ctx = ExitStack()
    with ctx:
        def sb(name, shape, dt=F32):
            return ctx.enter_context(nc.sbuf_tensor(name, shape, dt))
        g.PS = ctx.enter_context(nc.psum_tensor("banks", [P, 8, 512], F32))
        g.ident = sb("ident", [P, P])
        g.ones = sb("ones", [P, P])
        g.fold = sb("fold", [P, P])
        g.upper = sb("upper", [P, P])
        g.lower = sb("lower", [P, P])
        g.vcol = sb("vcol", [P, V_ALL])
        g.convw = sb("convw", [P, 3, MC])
        g.modc = sb("modc", [P, DEPTH, 48, 2])
        g.gain = sb("gain", [P, DEPTH, 2, KD, NB])
        g.shift = sb("shift", [P, DEPTH, 2, KD, NB])
        g.gate_row = sb("gate_row", [P, 2, D])
        g.gate_bias = sb("gate_bias", [P, DEPTH, D])
        g.cond = sb("cond", [P, KD, 2])
        g.bcol = sb("bcol", [P, 96])
        g.aff = sb("aff", [NE, T])
        g.row_s = sb("row_s", [P, NE], U32)
        g.row_p = sb("row_p", [CAP_P, NE], U32)
        g.gate_s = sb("gate_s", [P, NE])
        g.gate_p = sb("gate_p", [CAP_P, NE])
        g.res = nc.dram_tensor("res", [T, D], F32, kind="Internal").ap()
        g.normed = nc.dram_tensor("normed", [T, D], F32, kind="Internal").ap()
        g.z, g.xs, g.y, g.btok, g.bT, g.cT, g.hin = (
            nc.dram_tensor("d_" + name, shape, F32, kind="Internal").ap()
            for name, shape in (("z", [T, DI]), ("xs", [T, DI]), ("y", [T, DI]), ("btok", [T, GN]),
                                ("bT", [GN, T]), ("cT", [GN, T]), ("hin", [2, NB, P, DI])))

        start(nc, g, io)
        m = Shared()
        assert KD == HEADS
        with nc.sbuf_tensor("hT_oT", [P, HEADS, T], F32) as hT:
            m.oT = hT
            with ExitStack() as c:
                def mb(name, shape, dt=F32):
                    return c.enter_context(nc.sbuf_tensor(name, shape, dt))
                m.q_pair = [mb("q" + half, [P, KQ, T], F32R) for half in ("_hi", "_lo")]
                m.ckv_pair = [mb("ckv" + half, [P, KKV, KEYS], F32R) for half in ("_hi", "_lo")]
                m.k2_pair = [mb("k2" + half, [P, KEYS], F32R) for half in ("_hi", "_lo")]
                m.ckv = mb("ckv", [P, KKV, KEYS])
                m.rope = mb("rope", [P, T])
                norm(nc, g, io, 0, 0, hT)
                mla_project(nc, g, io, hT, m)
                mla_heads(nc, g, io, m)
            mla_out(nc, g, io, m)
        norm(nc, g, io, 0, 1)
        mixture(nc, g, io, 0)
        q = Shared()
        with ExitStack() as c:
            def qb(name, shape):
                return c.enter_context(nc.sbuf_tensor(name, shape, F32))
            q.dt, q.da, q.grow, q.toend, q.dec = (qb("q" + n, [P, 2, NB, SH]) for n in ("dt", "da", "grow", "toend", "dec"))
            q.skip = qb("qskip", [P, SH])
            with nc.sbuf_tensor("h_hi", [P, KD, T], F32R) as h_hi, nc.sbuf_tensor("h_lo", [P, KD, T], F32R) as h_lo:
                hT = (h_hi, h_lo)
                norm(nc, g, io, 1, 0, hT)
                ssm_gate_and_steps(nc, g, io, hT, q)
                ssm_conv(nc, g, io, hT)
            ssm_states(nc, g, io, q)
            ssm_outputs(nc, g, io, q)
            ssm_out(nc, g, io, q)
        norm(nc, g, io, 1, 1)
        mixture(nc, g, io, 1)
        final_norm(nc, g, io)


_INS = ["x_prompt", "x_sample", "cache_ckv", "cache_krope", "state_ssm", "c", "c_ctx", "w_mod", "b_mod", "norm1_g",
        "norm2_g", "final_norm_g", "mla_w_dq", "mla_q_norm_g", "mla_w_uq", "mla_w_dkv", "mla_kv_norm_g", "mla_w_ukv",
        "mla_w_o", "ssm_w_in", "ssm_conv_w", "ssm_conv_b", "ssm_dt_bias", "ssm_a_log", "ssm_d_skip", "ssm_norm_g",
        "ssm_w_out", "moe_w_router", "moe_w_gate", "moe_w_up", "moe_w_down"]
_OUTS = [("y_prompt", (1, SEQ, D)), ("y_sample", (1, DEC, D)), ("new_ckv", (1, 1, SEQ, KVR)),
         ("new_krope", (1, 1, SEQ, ROPE)), ("new_ssm", (1, 1, 2, SH, HD, NS))]


def rope_table():
    rows = DEC // GRID_W
    row = np.repeat(np.arange(rows), GRID_W).astype(np.float32)
    col = np.tile(np.arange(GRID_W), rows).astype(np.float32)
    pairs = ROPE // 4
    inv = np.float32(THETA) ** (-np.arange(pairs, dtype=np.float32) / np.float32(pairs))
    ang = np.concatenate([row[:, None] * inv, col[:, None] * inv], axis=-1).astype(np.float32)
    tab = np.zeros((P, T), np.float32)
    tab[0:ROPE, 0:SEQ] = 1.0
    cos, sin = np.cos(ang).T, np.sin(ang).T
    tab[:, SEQ:] = np.concatenate([cos, cos, -sin, sin], axis=0)
    return tab


def kernel(**inputs):
    import numpy as _np
    import concourse.bacc as _bacc
    from concourse.bass_utils import run_bass_kernel_spmd as _run

    nc = _bacc.Bacc("TRN2", target_bir_lowering=False, num_devices=1)
    drams, arrays = {}, {}
    for name in _INS:
        a = _np.ascontiguousarray(inputs[name])
        arrays["in_" + name] = a
        drams[name] = nc.dram_tensor("in_" + name, a.shape, F32, kind="ExternalInput").ap()
    tab = rope_table()
    arrays["in_rope"] = tab
    drams["rope"] = nc.dram_tensor("in_rope", tab.shape, F32, kind="ExternalInput").ap()
    for name, shape in _OUTS:
        drams[name] = nc.dram_tensor("out_" + name, shape, F32, kind="ExternalOutput").ap()
    build(nc, drams)
    r = _run(nc, [arrays], core_ids=[0])
    return tuple(r.results[0]["out_" + name] for name, _ in _OUTS)
```
